# Optimizing a Trainium2 kernel written in Bass

```python
import functools
import jax, jax.numpy as jnp
from jax import lax
import numpy as np

D_MODEL = 2048
BATCH = 1
SEQ = 256
DEPTH = 1
DEC_BATCH = 8
DEC_SEQ = 1
PAST_LEN = 1024
PAGE_SIZE = 128

N_META = 16
N_HEADS = 8
N_KV_HEADS = 2
HEAD_DIM = 128
ATTN_WIDTH = N_HEADS * HEAD_DIM
KV_WIDTH = N_KV_HEADS * HEAD_DIM
N_IDX_HEADS = 16
IDX_DIM = 64
TOPK_MAX = 256
POOL_WINDOWS = (2, 4, 8, 16)
POOL_WIDTH = D_MODEL - ATTN_WIDTH
POOL_GROUP = POOL_WIDTH // len(POOL_WINDOWS)
POOL_BUF = max(POOL_WINDOWS) - 1
MIX_WIDTH = ATTN_WIDTH + POOL_WIDTH
D_FF = 5632
CONV_WIDTH = 3
Q_BLOCK = 128
RMS_EPS = 1e-6

Q_END = ATTN_WIDTH
K_END = Q_END + KV_WIDTH
V_END = K_END + KV_WIDTH
IQ_END = V_END + N_IDX_HEADS * IDX_DIM
IK_END = IQ_END + IDX_DIM
IW_END = IK_END + N_IDX_HEADS
IN_COLS = IW_END + POOL_WIDTH
IN_OFFSETS = (Q_END, K_END, V_END, IQ_END, IK_END, IW_END)

kernel_name = "hymba_dsa_pool_convffn_step"

def _rmsnorm(x, g):
    xf = x.astype(jnp.float32)
    y = xf * lax.rsqrt(jnp.mean(xf * xf, axis=-1, keepdims=True) + RMS_EPS)
    return (y * g.astype(jnp.float32)).astype(x.dtype)

def _index_scores(iq, iw, ik):
    s = jnp.einsum('bqhd,bsd->bqsh', iq, ik).astype(jnp.float32) * (IDX_DIM ** -0.5)
    w = iw.astype(jnp.float32) * (N_IDX_HEADS ** -0.5)
    return jnp.einsum('bqsh,bqh->bqs', jax.nn.relu(s), w)

def _select_keys(scores, qpos, kpos, topk):
    admissible = kpos[None, None, :] <= qpos[None, :, None]
    scores = jnp.where(admissible, scores, -jnp.inf)
    _, idx = lax.top_k(scores, topk)
    valid = idx <= qpos[None, :, None]
    return idx, valid

def _attend_selected(q, k_sel, v_sel, valid):
    B, Q = q.shape[:2]
    qg = q.reshape(B, Q, N_KV_HEADS, N_HEADS // N_KV_HEADS, HEAD_DIM)
    s = jnp.einsum('bqgrd,bqkgd->bqgrk', qg, k_sel).astype(jnp.float32) * (HEAD_DIM ** -0.5)
    s = jnp.where(valid[:, :, None, None, :], s, -jnp.inf)
    p = jax.nn.softmax(s, axis=-1)
    o = jnp.einsum('bqgrk,bqkgd->bqgrd', p.astype(v_sel.dtype), v_sel)
    return o.reshape(B, Q, N_HEADS, HEAD_DIM)

def _to_blocks(a, n_blk):
    pad = n_blk * Q_BLOCK - a.shape[1]
    a = jnp.pad(a, [(0, 0), (0, pad)] + [(0, 0)] * (a.ndim - 2))
    return jnp.moveaxis(a.reshape((a.shape[0], n_blk, Q_BLOCK) + a.shape[2:]), 1, 0)

def _sparse_attn_prompt(q, k, v, iq, ik, iw, topk):
    B, T = q.shape[:2]
    n_blk = -(-T // Q_BLOCK)
    kpos = jnp.arange(T)
    gather = jax.vmap(lambda rows, ii: rows[ii])

    def block(args):
        qb, iqb, iwb, blk = args
        qpos = blk * Q_BLOCK + jnp.arange(Q_BLOCK)
        idx, valid = _select_keys(_index_scores(iqb, iwb, ik), qpos, kpos, topk)
        return _attend_selected(qb, gather(k, idx), gather(v, idx), valid)

    out = lax.map(block, (_to_blocks(q, n_blk), _to_blocks(iq, n_blk),
                          _to_blocks(iw, n_blk), jnp.arange(n_blk)))
    out = jnp.moveaxis(out, 0, 1).reshape(B, n_blk * Q_BLOCK, N_HEADS, HEAD_DIM)
    return out[:, :T]

def _sparse_attn_sample(q, k_new, v_new, iq, ik_new, iw, cache_k_l, cache_v_l, cache_kidx_l, page_table, topk):
    DB, DS = q.shape[:2]
    past = page_table.shape[1] * PAGE_SIZE
    ik_past = cache_kidx_l[page_table].reshape(DB, past, IDX_DIM)
    ik_all = jnp.concatenate([ik_past, ik_new.astype(ik_past.dtype)], axis=1)
    qpos = past + jnp.arange(DS)
    kpos = jnp.arange(past + DS)
    idx, valid = _select_keys(_index_scores(iq, iw, ik_all), qpos, kpos, topk)
    pidx = jnp.minimum(idx, past - 1)
    phys = jax.vmap(lambda pt, ii: pt[ii])(page_table, pidx // PAGE_SIZE)
    slot = pidx % PAGE_SIZE
    nidx = jnp.clip(idx - past, 0, DS - 1)
    gather = jax.vmap(lambda rows, ii: rows[ii])
    is_new = (idx >= past)[..., None, None]
    k_sel = jnp.where(is_new, gather(k_new, nidx), cache_k_l[phys, slot].astype(k_new.dtype))
    v_sel = jnp.where(is_new, gather(v_new, nidx), cache_v_l[phys, slot].astype(v_new.dtype))
    return _attend_selected(q, k_sel, v_sel, valid)

def _pool_mixer(u, buf, pos0, pool_w, pool_scale):
    T = u.shape[1]
    hp = jnp.concatenate([buf.astype(u.dtype), u], axis=1)
    upf = hp.astype(jnp.float32)
    csum = jnp.concatenate([jnp.zeros_like(upf[:, :1]), jnp.cumsum(upf, axis=1)], axis=1)
    pos = pos0 + jnp.arange(T)
    outs = []
    for g, w in enumerate(POOL_WINDOWS):
        cg = csum[..., g * POOL_GROUP:(g + 1) * POOL_GROUP]
        wsum = cg[:, POOL_BUF + 1:] - cg[:, POOL_BUF + 1 - w:POOL_BUF + 1 - w + T]
        cnt = jnp.minimum(pos + 1, w).astype(jnp.float32)[None, :, None]
        ug = upf[:, POOL_BUF:, g * POOL_GROUP:(g + 1) * POOL_GROUP]
        d = (wsum / cnt - ug).astype(u.dtype)
        outs.append(jnp.einsum('btc,cd->btd', d, pool_w[g]))
    y = jnp.concatenate(outs, axis=-1) * pool_scale
    return y, hp[:, -POOL_BUF:]

def _conv_ffn(x, buf, w_up, conv_w, conv_b, w_down):
    T = x.shape[1]
    h = jnp.einsum('btd,df->btf', x, w_up)
    hp = jnp.concatenate([buf.astype(h.dtype), h], axis=1)
    c = conv_b + conv_w[0] * hp[:, 0:T]
    for i in range(1, CONV_WIDTH):
        c = c + conv_w[i] * hp[:, i:i + T]
    gate, val = jnp.split(c, 2, axis=-1)
    y = jnp.einsum('btf,fd->btd', jax.nn.silu(gate) * val, w_down)
    return y, hp[:, -(CONV_WIDTH - 1):]

def _layer(x, attn_fn, pool_buf, conv_buf, pos0, w_in, w_o, pool_w, pool_scale,
           g_mix_pre, g_mix_post, g_ffn_pre, g_ffn_post, w_up, conv_w, conv_b, w_down):
    B, T, _ = x.shape
    h = _rmsnorm(x, g_mix_pre)
    proj = jnp.einsum('btd,dc->btc', h, w_in)
    q, k, v, iq, ik, iw, u = jnp.split(proj, IN_OFFSETS, axis=-1)
    q = q.reshape(B, T, N_HEADS, HEAD_DIM)
    k = k.reshape(B, T, N_KV_HEADS, HEAD_DIM)
    v = v.reshape(B, T, N_KV_HEADS, HEAD_DIM)
    iq = iq.reshape(B, T, N_IDX_HEADS, IDX_DIM)
    a = attn_fn(q, k, v, iq, ik, iw).reshape(B, T, ATTN_WIDTH)
    p, new_pool = _pool_mixer(u, pool_buf, pos0, pool_w, pool_scale)
    mix = jnp.concatenate([a, p.astype(a.dtype)], axis=-1)
    x = x + _rmsnorm(jnp.einsum('btm,md->btd', mix, w_o), g_mix_post)
    f, new_conv = _conv_ffn(_rmsnorm(x, g_ffn_pre), conv_buf, w_up, conv_w, conv_b, w_down)
    x = x + _rmsnorm(f, g_ffn_post)
    return x, k, v, ik, new_pool, new_conv

def setup_inputs(seed: int = 0) -> dict:
    key = jax.random.key(seed)
    ks = jax.random.split(key, 24)
    f32 = jnp.float32
    n_pages = PAST_LEN // PAGE_SIZE
    n_used = DEC_BATCH * n_pages
    n_pool = n_used + max(1, n_used // 4)
    nrm = lambda k, shape, s: jax.random.normal(k, shape, f32) * s
    page_table = jax.random.permutation(ks[0], n_pool)[:n_used].reshape(DEC_BATCH, n_pages).astype(jnp.int32)
    return {
        "x_prompt": nrm(ks[1], (BATCH, SEQ, D_MODEL), 1.0),
        "x_sample": nrm(ks[2], (DEC_BATCH, DEC_SEQ, D_MODEL), 1.0),
        "cache_k": nrm(ks[3], (DEPTH, n_pool, PAGE_SIZE, N_KV_HEADS, HEAD_DIM), 1.0),
        "cache_v": nrm(ks[4], (DEPTH, n_pool, PAGE_SIZE, N_KV_HEADS, HEAD_DIM), 1.0),
        "cache_kidx": nrm(ks[5], (DEPTH, n_pool, PAGE_SIZE, IDX_DIM), 1.0),
        "state_pool": nrm(ks[6], (DEPTH, DEC_BATCH, POOL_BUF, POOL_WIDTH), 1.0),
        "state_conv": nrm(ks[7], (DEPTH, DEC_BATCH, CONV_WIDTH - 1, 2 * D_FF), 1.0),
        "page_table": page_table,
        "meta_tokens": nrm(ks[8], (N_META, D_MODEL), 1.0),
        "w_in": nrm(ks[9], (DEPTH, D_MODEL, IN_COLS), D_MODEL ** -0.5),
        "w_o": nrm(ks[10], (DEPTH, MIX_WIDTH, D_MODEL), MIX_WIDTH ** -0.5),
        "pool_w": nrm(ks[11], (DEPTH, len(POOL_WINDOWS), POOL_GROUP, POOL_GROUP), POOL_GROUP ** -0.5),
        "pool_scale": 1.0 + nrm(ks[12], (DEPTH, POOL_WIDTH), 0.1),
        "g_mix_pre": 1.0 + nrm(ks[13], (DEPTH, D_MODEL), 0.02),
        "g_mix_post": 1.0 + nrm(ks[14], (DEPTH, D_MODEL), 0.02),
        "g_ffn_pre": 1.0 + nrm(ks[15], (DEPTH, D_MODEL), 0.02),
        "g_ffn_post": 1.0 + nrm(ks[16], (DEPTH, D_MODEL), 0.02),
        "w_up": nrm(ks[17], (DEPTH, D_MODEL, 2 * D_FF), D_MODEL ** -0.5),
        "conv_w": nrm(ks[18], (DEPTH, CONV_WIDTH, 2 * D_FF), CONV_WIDTH ** -0.5),
        "conv_b": nrm(ks[19], (DEPTH, 2 * D_FF), 0.01),
        "w_down": nrm(ks[20], (DEPTH, D_FF, D_MODEL), D_FF ** -0.5),
    }

def reference(x_prompt, x_sample, cache_k, cache_v, cache_kidx, state_pool, state_conv, page_table,
              meta_tokens, w_in, w_o, pool_w, pool_scale, g_mix_pre, g_mix_post, g_ffn_pre, g_ffn_post,
              w_up, conv_w, conv_b, w_down):
    B = x_prompt.shape[0]
    DS = x_sample.shape[1]
    meta = jnp.broadcast_to(meta_tokens[None].astype(x_prompt.dtype), (B, N_META, D_MODEL))
    xp = jnp.concatenate([meta, x_prompt], axis=1)
    xs = x_sample
    T_p = xp.shape[1]
    past = page_table.shape[1] * PAGE_SIZE
    topk_p = min(TOPK_MAX, T_p // 4)
    topk_s = min(TOPK_MAX, (past + DS) // 4)
    pool_buf0 = jnp.zeros((B, POOL_BUF, POOL_WIDTH), x_prompt.dtype)
    conv_buf0 = jnp.zeros((B, CONV_WIDTH - 1, 2 * D_FF), x_prompt.dtype)
    kp, vp, ikp, poolp, convp = [], [], [], [], []
    ks_, vs_, iks_, pools_, convs_ = [], [], [], [], []
    for l in range(DEPTH):
        wl = (w_in[l], w_o[l], pool_w[l], pool_scale[l], g_mix_pre[l], g_mix_post[l],
              g_ffn_pre[l], g_ffn_post[l], w_up[l], conv_w[l], conv_b[l], w_down[l])
        attn_p = functools.partial(_sparse_attn_prompt, topk=topk_p)
        xp, k1, v1, ik1, pl1, cv1 = _layer(xp, attn_p, pool_buf0, conv_buf0, 0, *wl)
        attn_s = functools.partial(_sparse_attn_sample, cache_k_l=cache_k[l], cache_v_l=cache_v[l],
                                   cache_kidx_l=cache_kidx[l], page_table=page_table, topk=topk_s)
        xs, k2, v2, ik2, pl2, cv2 = _layer(xs, attn_s, state_pool[l], state_conv[l], past, *wl)
        kp.append(k1); vp.append(v1); ikp.append(ik1); poolp.append(pl1); convp.append(cv1)
        ks_.append(k2); vs_.append(v2); iks_.append(ik2); pools_.append(pl2); convs_.append(cv2)
    y_prompt = xp[:, N_META:]
    y_sample = xs
    return (y_prompt, y_sample,
            jnp.stack(kp), jnp.stack(vp), jnp.stack(ikp), jnp.stack(poolp), jnp.stack(convp),
            jnp.stack(ks_), jnp.stack(vs_), jnp.stack(iks_), jnp.stack(pools_), jnp.stack(convs_))


_drawn_inputs = setup_inputs


def setup_inputs(seed=0):
    import zlib

    import numpy as np

    out = dict(_drawn_inputs(seed))
    spreads = {}
    factors = {'g_mix_post': 3.373, 'g_ffn_pre': 2.814, 'g_ffn_post': 4.982, 'conv_b': 6.811}
    for name, (base, spread) in spreads.items():
        noise = np.random.default_rng([zlib.crc32(name.encode()), seed]).standard_normal(out[name].shape)
        drawn = base * np.exp(spread * noise) if base else spread * noise
        out[name] = __import__('jax').numpy.asarray(drawn.astype(out[name].dtype))
    for name, factor in factors.items():
        out[name] = (out[name] * factor).astype(out[name].dtype)
    return out
```

```python
from contextlib import ExitStack

import concourse.bass as bass
from concourse import mybir
import numpy as np

F32 = mybir.dt.float32
F32R = mybir.dt.float32r
I32 = mybir.dt.int32
U32 = mybir.dt.uint32
ALU = mybir.AluOpType
ACT = mybir.ActivationFunctionType
AX = mybir.AxisListType

P = 128
D_MODEL, SEQ, DB, PAST, PAGE = 2048, 256, 8, 1024, 128
N_META, HEADS, KV, HD = 16, 8, 2, 128
IDX_HEADS, IDX_DIM = 16, 64
POOL_WIDTH, POOL_BUF, D_FF = 1024, 15, 5632
TOPK_MAX, EPS = 256, 1e-6
WINDOWS = (2, 4, 8, 16)

TP = N_META + SEQ
T = TP + DB
KM = D_MODEL // P
PAGES = PAST // PAGE
CTX = PAST + 1
TOPK_P = min(TOPK_MAX, TP // 4)
TOPK_S = min(TOPK_MAX, CTX // 4)
FT = D_FF // P
IKW = IDX_DIM + IDX_HEADS
PAIRS = DB // 2

QT = [(0, 128, 128), (128, 128, 256), (256, 16, 272)]
SENT = -(-TOPK_P // 8) * 8 - TOPK_P
S_AT = [0, 128 + SENT, 384 + 2 * SENT]
S_W = 656 + 3 * SENT
A_AT = [0, 128, 384]
NEG = -3e38
BIG = 3e38
MASKED = -1e30

RING = 4
CW = 8 * P

C_IK = 0
C_IQ = C_IK + 2
C_PROJ = C_IQ + 16
C_WOP = C_PROJ + 40
C_WOA = C_WOP + 16
C_UP = C_WOA + 16
C_DOWN = C_UP + 4 * FT
DOWN_CUT = [0, 8, 16, 23, 30, 37, 44]
T_IK, T_IQ = 0, 1
T_PROJ = T_IQ + 8
T_WOP = T_PROJ + 20
T_WOA = T_WOP + 16
T_UP = T_WOA + 16
T_DOWN = T_UP + 2 * FT
U0, K0, V0, Q0 = 0, 8, 10, 12

G1, G2, G3, G4, PSC = 0, 16, 32, 48, 64
CWT, CBT = 72, 72 + 3 * 2 * FT
PAR_W = CBT + 2 * FT
IDN, ONE, HREP, BLK, EXP8, M64, INV, DIX = 0, 128, 256, 384, 392, 456, 464, 528
CON_W = 529


def shape_constants():
    c = np.zeros((P, CON_W), np.float32)
    c[:, IDN:IDN + P] = np.eye(P)
    c[:, ONE:ONE + P] = 1.0
    for b in range(DB):
        for h in range(IDX_HEADS):
            c[h, HREP + IDX_HEADS * b + h] = 1.0
            c[IDX_HEADS * b + h, BLK + b] = 1.0
        c[b, EXP8 + HEADS * b:EXP8 + HEADS * (b + 1)] = 1.0
        c[HEADS * b:HEADS * (b + 1), M64 + b] = 1.0
    for g, w in enumerate(WINDOWS):
        c[:, INV + 16 * g:INV + 16 * (g + 1)] = 1.0 / np.minimum(np.arange(16) + 1, w)
    c[:, DIX] = np.arange(P) % IDX_DIM
    s = np.full((P, S_W), NEG, np.float32)
    for (q0, nq, nk), at in zip(QT, S_AT):
        for q in range(P):
            s[q, at:at + min(q0 + q + 1, nk)] = 0.0
        s[:, at + nk:at + nk + SENT] = BIG
    return c, s


class Steps:

    def __init__(self, eng, sem):
        self.eng, self.sem, self.n, self.turn = eng, sem, 0, 0

    def then(self, ins):
        ins.then_inc(self.sem, 1)
        self.n += 1

    def wait(self):
        self.eng.wait_ge(self.sem, self.turn + self.n)

    def link(self, ins):
        self.then(ins)
        self.wait()


def build_program(nc, a):
    ctx = ExitStack()

    def sem(name):
        return ctx.enter_context(nc.semaphore(name))

    def sb(name, shape, dt=F32, at=None):
        return (at or ctx).enter_context(nc.sbuf_tensor(name, shape, dt))

    raw = sb("raw", [P, RING, CW])
    hi = sb("hi", [P, RING, CW], F32R)
    lo = sb("lo", [P, RING, CW], F32R)
    par = sb("par", [P, PAR_W])
    con = sb("con", [P, CON_W])
    rms = sb("rms", [P, T])
    var = sb("var", [P, T])
    sumsq = sb("sumsq", [P, T])
    sq = sb("sq", [P, 2, T])

    at_h = ExitStack()
    h_hi = sb("h_hi", [P, KM, T], F32R, at_h)
    h_lo = sb("h_lo", [P, KM, T], F32R, at_h)

    at_1 = ExitStack()
    cache_ring = sb("cache_ring", [P, 4096], at=at_1)
    mixed = sb("mixed", [P, KM * T], at=at_1)
    short = sb("short", [P, 3984], at=at_1)
    part = sb("part", [P, KM, T], at=at_1)
    qT = sb("qT", [P, HEADS, T], at=at_1)
    qbd = sb("qbd", [P, 2 * DB * 64], at=at_1)
    kT = sb("kT", [P, KV, T], at=at_1)
    vT = sb("vT", [P, KV, T], at=at_1)
    vrow = sb("vrow", [P, 3, KV * HD], at=at_1)
    vnew = sb("vnew", [DB, KV * HD], at=at_1)
    ikT = sb("ikT", [IDX_DIM, T], at=at_1)
    iknew = sb("iknew", [P, PAIRS], at=at_1)
    iwT = sb("iwT", [IDX_HEADS, T], at=at_1)
    iwq = sb("iwq", [P, 3 * IDX_HEADS], at=at_1)
    iwblk = sb("iwblk", [P, DB], at=at_1)
    top8 = sb("top8", [P, 3, 8], at=at_1)
    top8s = sb("top8s", [DB, 8], at=at_1)
    mx = sb("mx", [P, 3], at=at_1)
    nmx = sb("nmx", [P, 3], at=at_1)
    den = sb("den", [P, 3], at=at_1)
    rden = sb("rden", [P, 3], at=at_1)
    mxs = sb("mxs", [64, 5], at=at_1)
    dens = sb("dens", [64, 5], at=at_1)
    pnm = sb("pnm", [64, DB], at=at_1)
    pnew = sb("pnew", [DB, 64], at=at_1)
    ptab = sb("ptab", [P, PAIRS * PAGES], I32, at_1)
    ptrow = sb("ptrow", [1, DB * PAGES], I32, at_1)
    kix = sb("kix", [P, PAIRS * PAGES], U32, at_1)
    S = sb("S", [P, S_W], at=at_1)
    W = sb("W", [P, S_W], at=at_1)
    Ss = sb("Ss", [DB, CTX], at=at_1)
    Ws = sb("Ws", [DB, CTX], at=at_1)

    kidx = cache_ring[:, :].rearrange("p (b s) -> p b s", b=PAIRS)
    vring = cache_ring[:, :].rearrange("p (r g e) -> p r g e", r=2, g=PAGES)
    U = mixed[:, 0:8 * (POOL_BUF + T)].rearrange("p (j t) -> p j t", j=8)
    UW = POOL_BUF + TP
    at = 8 * (POOL_BUF + T)
    win = [mixed[:, at + n * 2 * UW:at + (n + 1) * 2 * UW].rearrange("p (j t) -> p j t", j=2) for n in range(3)]
    kring = mixed[:, 0:4096].rearrange("p (r g e) -> p r g e", r=2, g=PAGES)
    x1 = mixed[:, :].rearrange("p (k t) -> p k t", k=KM)
    iq = short[0:IDX_DIM, 0:4 * T].rearrange("p (h t) -> p h t", h=4)
    relu = short[:, 1120:1120 + 1312].rearrange("p (r s) -> p r s", r=2)
    iqbd = short[:, 2432:2432 + PAIRS * P]
    relus = short[:, 2944:2944 + CTX]
    diff = short[:, 0:8 * T].rearrange("p (j t) -> p j t", j=8)
    prob = short[:, 0:1312].rearrange("p (r s) -> p r s", r=2)
    probT = short[:, 1312:1312 + 864].rearrange("p (r s) -> p r s", r=2)
    probs = short[0:64, 2176:2176 + CTX]
    probsT = short[:, 3204:3204 + 512].rearrange("p (g c) -> p g c", g=PAGES)
    x0 = part
    partf = part[:, :, :].rearrange("p k t -> p (k t)")
    poolw = partf[:, 0:2048].rearrange("p (g k d) -> p g k d", g=4, k=2)
    poolst = partf[:, 2048:2048 + 960].rearrange("p (j b s) -> p j b s", j=8, b=DB)
    end_1 = at_1

    end_1.close()
    at_2 = ExitStack()
    g_hi = sb("g_hi", [P, FT, T], F32R, at_2)
    g_lo = sb("g_lo", [P, FT, T], F32R, at_2)
    cst = sb("cst", [P, 2, 2 * FT, DB], at=at_2)
    up = sb("up", [P, 2, 2, 2 + T], at=at_2)
    act = sb("act", [P, 2, T], at=at_2)
    uplast = sb("uplast", [P, 2 * FT, 2 + DB], at=at_2)
    at_2.close()
    at_h.close()
    at_3 = ExitStack()
    x2 = sb("x2", [P, KM, T], at=at_3)
    o2 = sb("o2", [P, KM, T], at=at_3)
    at_3.close()

    bank = [ctx.enter_context(nc.psum_tensor(f"bank{i}", [P, 512], F32)) for i in range(8)]
    misc = bank[7]

    kscr = nc.dram_tensor("kscr", [DB * PAGES, P, KV * PAGE], F32).ap()
    vscr = nc.dram_tensor("vscr", [DB * PAGES, P, KV * HD], F32).ap()
    xscr = nc.dram_tensor("xscr", [P, KM, T], F32).ap()

    raw_loaded = [sem(f"raw_loaded{i}") for i in range(RING)]
    hi_ready = sem("hi_ready")
    lo_pool = sem("lo_pool")
    lo_dve = sem("lo_dve")
    chunk_used = sem("chunk_used")
    tile_freed = sem("tile_freed")
    x_loaded = [sem(f"x_loaded{i}") for i in range(4)]
    par_loaded = sem("par_loaded")
    con_loaded = sem("con_loaded")
    s_loaded = sem("s_loaded")
    pt_loaded = sem("pt_loaded")
    poolw_loaded = sem("poolw_loaded")
    kix_ready = sem("kix_ready")
    kidx_loaded = sem("kidx_loaded")
    scr_loaded = sem("scr_loaded")
    k_loaded = [sem(f"k_loaded{i}") for i in range(2)]
    v_loaded = [sem(f"v_loaded{i}") for i in range(2)]
    x1_loaded = sem("x1_loaded")
    x2_loaded = sem("x2_loaded")
    x_spilled = sem("x_spilled")
    cst_loaded = sem("cst_loaded")
    stored = sem("stored")
    u_stored = sem("u_stored")
    copied = sem("copied")
    zeroed = sem("zeroed")
    dve_step = sem("dve_step")
    act_step = sem("act_step")
    pool_step = sem("pool_step")
    h_hi_ready = sem("h_hi_ready")
    h_lo_ready = sem("h_lo_ready")
    sq_ready = sem("sq_ready")
    sq_used = sem("sq_used")
    sum_ready = sem("sum_ready")
    var_ready = sem("var_ready")
    root_ready = sem("root_ready")
    iw_ready = sem("iw_ready")
    iwq_done = sem("iwq_done")
    iq_ready = sem("iq_ready")
    iq_used = sem("iq_used")
    relu_ready = sem("relu_ready")
    relu_used = sem("relu_used")
    sidx_done = sem("sidx_done")
    srelu_done = sem("srelu_done")
    ssum_done = sem("ssum_done")
    v_ready = sem("v_ready")
    vt_done = sem("vt_done")
    vrow_ready = sem("vrow_ready")
    diff_ready = sem("diff_ready")
    pmix_done = sem("pmix_done")
    pmix_hi = sem("pmix_hi")
    pmix_lo = sem("pmix_lo")
    qkv_ready = sem("qkv_ready")
    score_done = sem("score_done")
    soft_in = sem("soft_in")
    exp_done = sem("exp_done")
    prob_ready = sem("prob_ready")
    probT_done = sem("probT_done")
    probT_ready = sem("probT_ready")
    pv_done = sem("pv_done")
    o_hi = sem("o_hi")
    o_lo = sem("o_lo")
    kq_used = sem("kq_used")
    vq_used = sem("vq_used")
    smask_ready = sem("smask_ready")
    sscore_done = sem("sscore_done")
    ssoft_in = sem("ssoft_in")
    sexp_done = sem("sexp_done")
    sprob_ready = sem("sprob_ready")
    sprobT_done = sem("sprobT_done")
    sprobT_act = sem("sprobT_act")
    sprobT_dve = sem("sprobT_dve")
    spv_done = sem("spv_done")
    so_hi = sem("so_hi")
    so_lo = sem("so_lo")
    o_ready = sem("o_ready")
    xt_ready = sem("xt_ready")
    up_ready = sem("up_ready")
    act_ready = sem("act_ready")
    conv_ready = sem("conv_ready")
    silu_ready = sem("silu_ready")
    gate_ready = sem("gate_ready")
    g_hi_ready = sem("g_hi_ready")
    g_lo_ready = sem("g_lo_ready")
    y_ready = sem("y_ready")

    def lo_wait(eng, r, cj):
        if cj < C_PROJ:
            eng.wait_ge(lo_dve, 4 * r + cj + 1)
        elif cj < C_UP:
            eng.wait_ge(lo_pool, 4 * r + cj - C_PROJ + 1)
        elif (cj - C_UP) % 2 == 0:
            eng.wait_ge(lo_pool, 2 * r + C_UP - C_PROJ + (cj - C_UP) // 2 + 1)
        else:
            eng.wait_ge(lo_dve, 2 * r + C_PROJ + (cj - C_UP + 1) // 2)

    def hi_chunk(act_eng, r, cj, width=CW):
        s = cj % RING
        act_eng.wait_ge(raw_loaded[s], 16 * (r + cj // RING + 1))
        if cj >= RING:
            act_eng.wait_ge(chunk_used, 4 * r + cj - RING + 1)
        nc.scalar.activation(hi[:, s, 0:width], raw[:, s, 0:width], ACT.Copy).then_inc(hi_ready, 1)

    def lo_chunk(eng, ops, done, r, cj, width=CW):
        s = cj % RING
        eng.wait_ge(hi_ready, 4 * r + cj + 1)
        if cj >= RING:
            eng.wait_ge(chunk_used, 4 * r + cj - RING + 1)
        ops.tensor_tensor(lo[:, s, 0:width], raw[:, s, 0:width], hi[:, s, 0:width].bitcast(F32),
                          ALU.subtract).then_inc(done, 1)

    def down_width(cj):
        i = (cj - C_DOWN) % 6
        return (DOWN_CUT[i + 1] - DOWN_CUT[i]) * P

    with nc.Block() as block:

        @block.sync
        def _(sp):
            def load(r, cj, src, width=CW):
                if not isinstance(r, int):
                    lo_wait(sp, r - 1, cj) if cj >= C_UP else lo_wait(sp, r, cj - RING)
                elif 4 * r + cj >= RING:
                    lo_wait(sp, 0, 4 * r + cj - RING)
                sp.dma_start(raw[:, cj % RING, 0:width], src).then_inc(raw_loaded[cj % RING], 16)

            for j in range(2):
                load(0, C_IK + j, a["w_ik"][:, j * 8 * IKW:(j + 1) * 8 * IKW], 8 * IKW)

            def pages(n):
                page = sp.value_load(ptrow[0:1, bass.ds(n, 1)], min_val=0, max_val=a["cache_k"].shape[0] - 1)
                sp.dma_start(kscr[n], a["cache_k"][page]).then_inc(scr_loaded, 16)
                sp.dma_start(vscr[n], a["cache_v"][page]).then_inc(scr_loaded, 16)

            w_in = a["w_in"]

            def load_in(r, cj, t):
                for j in range(2):
                    load(r, cj + j, w_in[t, :, j * CW:(j + 1) * CW])

            load_in(0, C_IQ, 0)
            sp.wait_ge(pt_loaded, 48)
            with sp.Fori(0, 4) as i:
                for t in (1, 2):
                    load_in(i, C_IQ + 2 * t, 2 * i + t)
                    pages(4 * i + 2 * t - 2)
                    pages(4 * i + 2 * t - 1)
            for t in (9, 10):
                load_in(0, C_IQ + 2 * t, t)
                pages(2 * t - 2)
                pages(2 * t - 1)
            with sp.Fori(0, 8) as i:
                for t in (11, 12):
                    load_in(i, C_IQ + 2 * t, 2 * i + t)
                    pages(4 * i + 2 * t - 2)
                    pages(4 * i + 2 * t - 1)
            load_in(0, C_IQ + 54, 27)
            with sp.Fori(0, 4) as i:
                for j in range(4):
                    load(i, C_WOP + j, a["w_o"][4 * i + j, :, CW:2 * CW])
                    if j < 3:
                        pages(3 * i + 52 + j)
            kv_src = [[kscr, vscr][n].rearrange("(b g) p e -> b p g e", b=DB) for n in range(2)]

            def load_k(b):
                if b >= 2:
                    sp.wait_ge(kq_used, b - 1)
                sp.dma_start(kring[:, b % 2], kv_src[0][b]).then_inc(k_loaded[b % 2], 16)

            def load_v(b):
                if b >= 2:
                    sp.wait_ge(vq_used, b - 1)
                sp.dma_start(vring[:, b % 2], kv_src[1][b]).then_inc(v_loaded[b % 2], 16)

            sp.wait_ge(scr_loaded, 2 * DB * PAGES * 16)
            sp.wait_ge(diff_ready, 4)
            sp.wait_ge(u_stored, 16)
            sp.wait_ge(sidx_done, 1)
            for b in range(2):
                load_k(b)
                load_v(b)
            for j in range(4):
                load(0, C_WOA + j, a["w_o"][j, :, 0:CW])
            for b in range(2, DB):
                load_k(b)
            for b in range(2, DB):
                load_v(b)
            sp.wait_ge(kq_used, DB)
            sp.dma_start(x1, a["x"]).then_inc(x1_loaded, 16)
            sp.wait_ge(so_lo, 1)
            sp.dma_start(cst[:, :, :, :], a["state_conv"]).then_inc(cst_loaded, 16)
            with sp.Fori(0, 3) as i:
                for j in range(4):
                    load(i, C_WOA + 4 + j, a["w_o"][4 * i + 4 + j, :, 0:CW])
            def load_up(r):
                for j in range(4):
                    load(r, C_UP + j, a["w_up"][2 * r + j // 2, :, (j % 2) * CW:(j % 2 + 1) * CW])

            load_up(0)
            with sp.Fori(1, FT) as i:
                load_up(i)

            def load_down(i, t):
                for j in range(6):
                    c0, c1 = DOWN_CUT[j], DOWN_CUT[j + 1]
                    load(3 * i, C_DOWN + 6 * t + j, a["w_down"][2 * i + t, :, c0 * P:c1 * P], (c1 - c0) * P)

            with sp.Fori(0, KM // 2) as i:
                load_down(i, 0)
                load_down(i, 1)
            for k in range(0, KM, 2):
                sp.wait_ge(y_ready, k + 2)
                sp.dma_start(a["y"][:, k:k + 2, :], o2[:, k:k + 2, :]).then_inc(stored, 16)
            sp.wait_ge(stored, 16 * (4 + KM // 2))
            sp.wait_ge(u_stored, 16)
            sp.wait_ge(copied, 32)

        @block.gpsimd
        def _(pool):
            nc.gpsimd.memset(iqbd, 0.0).then_inc(zeroed, 1)
            nc.gpsimd.memset(qbd[:, :], 0.0).then_inc(zeroed, 1)
            nc.gpsimd.memset(U[:, :, 0:POOL_BUF], 0.0).then_inc(zeroed, 1)
            pool.wait_ge(kix_ready, 1)
            kidx_rows = a["cache_kidx"]
            for b in range(PAIRS):
                for g in range(PAGES):
                    n = b * PAGES + g
                    nc.gpsimd.indirect_dma_start(
                        kidx[:, b, g * PAGE:(g + 1) * PAGE], None, kidx_rows,
                        bass.IndirectOffsetOnAxis(ap=kix[:, n:n + 1], axis=0)).then_inc(kidx_loaded, 16)
            with pool.Fori(0, (C_UP - C_PROJ) // 4) as i:
                for j in range(4):
                    lo_chunk(pool, nc.gpsimd, lo_pool, i, C_PROJ + j)
            with pool.Fori(0, FT) as i:
                for j in (0, 2):
                    lo_chunk(pool, nc.gpsimd, lo_pool, i, C_UP + j)
            with pool.Fori(0, KM // 2) as i:
                for j in range(0, 12, 2):
                    lo_chunk(pool, nc.gpsimd, lo_pool, 3 * i, C_DOWN + j, down_width(C_DOWN + j))

        @block.scalar
        def _(act_eng):
            ae = act_eng
            st = Steps(ae, act_step)
            for n in range(4):
                ae.dma_start(x0[:, 4 * n:4 * n + 4, :], a["x"][:, 4 * n:4 * n + 4, :]).then_inc(x_loaded[n], 16)
                if n == 0:
                    ae.dma_start(par[:, :], a["par"]).then_inc(par_loaded, 16)
                    ae.dma_start(con[:, :], a["con"]).then_inc(con_loaded, 16)
                    ae.dma_start(ptab[0:64, :], a["pages_even"].broadcast_to([64, PAIRS * PAGES])).then_inc(pt_loaded, 16)
                    ae.dma_start(ptab[64:128, :], a["pages_odd"].broadcast_to([64, PAIRS * PAGES])).then_inc(pt_loaded, 16)
                    ae.dma_start(ptrow[:, :], a["pages"]).then_inc(pt_loaded, 16)
            ae.dma_start(S[:, :], a["causal"]).then_inc(s_loaded, 16)
            ae.dma_start(a["old_pool"], a["state_pool_rows"]).then_inc(copied, 16)
            ae.dma_start(a["old_conv"], a["state_conv_rows"]).then_inc(copied, 16)
            ae.wait_ge(par_loaded, 16)
            for k in range(KM):
                ae.wait_ge(x_loaded[k // 4], 16)
                if k in (1, 3):
                    hi_chunk(ae, 0, C_IK + k // 2, 8 * IKW)
                nc.scalar.activation(h_hi[:, k, :], x0[:, k, :], ACT.Copy,
                                     scale=par[:, G1 + k:G1 + k + 1]).then_inc(h_hi_ready, 1)
                if k >= 2:
                    ae.wait_ge(sq_used, k - 1)
                nc.scalar.activation(sq[:, k % 2, :], x0[:, k, :], ACT.Square).then_inc(sq_ready, 1)
            hi_chunk(ae, 0, C_IQ)
            hi_chunk(ae, 0, C_IQ + 1)

            def root(n):
                ae.wait_ge(var_ready, n)
                nc.scalar.activation(var[:, :], var[:, :], ACT.Sqrt).then_inc(root_ready, 1)

            root(1)
            ae.wait_ge(sum_ready, 1)
            ae.wait_ge(h_lo_ready, KM)
            ae.dma_start(partf[:, 0:2048], a["pool_w"]).then_inc(poolw_loaded, 16)
            ae.dma_start(partf[:, 2048:2048 + 960], a["state_pool"]).then_inc(poolw_loaded, 16)

            IDX_SCALE = float(IDX_DIM) ** -0.5 * float(IDX_HEADS) ** -0.5

            def relu_head(h, p):
                ae.wait_ge(iq_used, h + 1)
                if not isinstance(h, int) or h >= 2:
                    ae.wait_ge(relu_used, h - 1)
                nc.scalar.activation(relu[:, p, 0:384], bank[2 + 2 * p][:, 0:384], ACT.Relu,
                                     scale=IDX_SCALE).then_inc(act_step, 1)
                nc.scalar.activation(relu[0:16, p, 384:656], bank[3 + 2 * p][0:16, 0:272], ACT.Relu,
                                     scale=IDX_SCALE).then_inc(relu_ready, 1)

            for t in (1, 2):
                hi_chunk(ae, 0, C_IQ + 2 * t)
                hi_chunk(ae, 0, C_IQ + 2 * t + 1)
                for p in range(2):
                    relu_head(2 * (t - 1) + p, p)
            with ae.Fori(1, 3) as i:
                for t in (1, 2):
                    hi_chunk(ae, i, C_IQ + 2 * t)
                    hi_chunk(ae, i, C_IQ + 2 * t + 1)
                    for p in range(2):
                        relu_head(4 * i + 2 * (t - 1) + p, p)
            hi_chunk(ae, 0, C_IQ + 14)
            hi_chunk(ae, 0, C_IQ + 15)
            for h in range(12, 16):
                relu_head(h, h % 2)
            hi_chunk(ae, 0, C_PROJ)
            hi_chunk(ae, 0, C_PROJ + 1)
            ae.wait_ge(sidx_done, 1)
            nc.scalar.activation(relus[:, 0:512], bank[4][:, :], ACT.Relu, scale=IDX_SCALE).then_inc(srelu_done, 1)
            nc.scalar.activation(relus[:, 512:1024], bank[5][:, :], ACT.Relu, scale=IDX_SCALE).then_inc(srelu_done, 1)
            nc.scalar.activation(relus[:, 1024:1025], bank[6][:, 0:1], ACT.Relu,
                                 scale=IDX_SCALE).then_inc(srelu_done, 1)
            with ae.Fori(0, 9) as i:
                for j in range(4):
                    hi_chunk(ae, i, C_PROJ + 2 + j)
            hi_chunk(ae, 0, C_PROJ + 38)
            hi_chunk(ae, 0, C_PROJ + 39)
            ae.wait_ge(vt_done, 1)
            nc.scalar.activation(vrow[:, 0, :], bank[6][:, 0:256], ACT.Copy).then_inc(vrow_ready, 1)
            nc.scalar.activation(vrow[:, 1, :], bank[6][:, 256:512], ACT.Copy).then_inc(vrow_ready, 1)
            nc.scalar.activation(vrow[0:16, 2, :], misc[0:16, 0:256], ACT.Copy).then_inc(vrow_ready, 1)
            nc.scalar.activation(vnew[:, :], misc[0:DB, 256:512], ACT.Copy).then_inc(vrow_ready, 1)
            ae.wait_ge(diff_ready, 4)
            ae.dma_start(a["u"], U[:, :, POOL_BUF:POOL_BUF + T]).then_inc(u_stored, 16)
            ae.dma_start(a["k"], kT[:, :, :]).then_inc(stored, 16)
            ae.dma_start(a["v"], vT[:, :, :]).then_inc(stored, 16)
            ae.dma_start(a["ik"], ikT[:, :]).then_inc(stored, 16)
            for j in range(8):
                ae.wait_ge(pmix_done, j + 1)
                nc.scalar.activation(h_hi[:, HEADS + j, :], bank[2 + j % 2][:, 0:T], ACT.Copy,
                                     scale=par[:, PSC + j:PSC + j + 1]).then_inc(pmix_hi, 1)
                if j in (3, 7):
                    hi_chunk(ae, 0, C_WOP + j // 4)
            SCALE = float(HD) ** -0.5
            for h in range(HEADS):
                p = h % 2
                ae.wait_ge(soft_in, h + 1)
                if h >= 2:
                    ae.wait_ge(probT_done, h - 1)
                for n, (q0, nq, nk) in enumerate(QT):
                    sl = prob[0:nq, p, A_AT[n]:A_AT[n] + nk]
                    nc.scalar.activation(sl, sl, ACT.Exp, scale=SCALE, bias=nmx[0:nq, n:n + 1],
                                         accum_out=den[0:nq, n:n + 1]).then_inc(exp_done, 1)
                if h < 7:
                    hi_chunk(ae, 0, C_WOP + 2 + 2 * h)
                ae.wait_ge(probT_done, h + 1)
                nc.scalar.activation(probT[:, p, 0:416], bank[4][:, 0:416], ACT.Copy).then_inc(probT_ready, 1)
                nc.scalar.activation(probT[0:16, p, 416:432], bank[4][0:16, 416:432], ACT.Copy).then_inc(probT_ready, 1)
                if h < 7:
                    hi_chunk(ae, 0, C_WOP + 3 + 2 * h)
                ae.wait_ge(pv_done, h + 1)
                nc.scalar.activation(h_hi[:, h, 0:TP], bank[5][:, 0:TP], ACT.Copy).then_inc(o_hi, 1)
            for j in range(4):
                hi_chunk(ae, 0, C_WOA + j)
            ae.wait_ge(ssoft_in, 1)
            for n, (c0, c1) in enumerate(((0, 512), (512, 1024), (1024, 1025))):
                nc.scalar.activation(probs[:, c0:c1], bank[[2, 3, 6][n]][0:64, 0:c1 - c0], ACT.Exp, scale=SCALE,
                                     bias=mxs[:, 4:5], accum_out=dens[:, n:n + 1]).then_inc(sexp_done, 1)
            ae.wait_ge(sprobT_done, 1)
            nc.scalar.activation(probsT[:, :, :], bank[4][:, :].rearrange("p (g c) -> p g c", g=PAGES),
                                 ACT.Copy).then_inc(sprobT_act, 1)
            ae.wait_ge(spv_done, 1)
            nc.scalar.activation(h_hi[:, 0:HEADS, TP:T], misc[:, 0:64].rearrange("p (b h) -> p h b", b=DB),
                                 ACT.Copy).then_inc(so_hi, 1)
            for j in range(KM):
                if j < 12:
                    hi_chunk(ae, 0, C_WOA + 4 + j)
                ae.wait_ge(o_ready, j + 1)
                if j >= 2:
                    ae.wait_ge(sq_used, KM + j - 2)
                nc.scalar.activation(sq[:, j % 2, :], part[:, j, :], ACT.Square).then_inc(sq_ready, 1)
            for j in range(2):
                hi_chunk(ae, 0, C_UP + j)
            root(2)
            for k in range(KM):
                ae.wait_ge(xt_ready, k + 1)
                nc.scalar.activation(h_hi[:, k, :], x1[:, k, :], ACT.Copy,
                                     scale=par[:, G3 + k:G3 + k + 1]).then_inc(h_hi_ready, 1)
                ae.wait_ge(sq_used, 2 * KM + k - 2)
                nc.scalar.activation(sq[:, k % 2, :], x1[:, k, :], ACT.Square).then_inc(sq_ready, 1)
            ae.dma_start(xscr, x1).then_inc(x_spilled, 16)
            root(3)
            ae.wait_ge(x_spilled, 16)

            def conv_bias(r, p, v):
                f = 2 * r + v
                ae.wait_ge(up_ready, f + 1)
                nc.scalar.activation(act[:, v, :], up[:, p, v, 2:2 + T], ACT.Identity,
                                     scale=par[:, bass.ds(CWT + 4 * FT + f, 1)],
                                     bias=par[:, bass.ds(CBT + f, 1)]).then_inc(act_ready, 1)

            def ffn_pair(r, p, last=False, first=False):
                hi_chunk(ae, r, C_UP + 2)
                hi_chunk(ae, r, C_UP + 3)
                if not first:
                    ae.wait_ge(g_lo_ready, r)
                conv_bias(r, p, 0)
                if not last:
                    hi_chunk(ae, r, C_UP + 4)
                    hi_chunk(ae, r, C_UP + 5)
                conv_bias(r, p, 1)
                ae.wait_ge(conv_ready, r + 1)
                nc.scalar.activation(act[:, 0, :], act[:, 0, :], ACT.Silu).then_inc(silu_ready, 1)
                ae.wait_ge(gate_ready, r + 1)
                nc.scalar.activation(g_hi[:, bass.ds(r, 1), :], act[:, 0:1, :], ACT.Copy).then_inc(g_hi_ready, 1)

            ffn_pair(0, 0, first=True)
            ffn_pair(1, 1)
            with ae.Fori(1, FT // 2 - 1) as i:
                ffn_pair(2 * i, 0)
                ffn_pair(2 * i + 1, 1)
            ffn_pair(FT - 2, 0)
            ffn_pair(FT - 1, 1, last=True)
            for j in range(RING):
                hi_chunk(ae, 0, C_DOWN + j, down_width(C_DOWN + j))
            ae.wait_ge(chunk_used, C_DOWN)
            ae.dma_start(x2[:, :, :], xscr).then_inc(x2_loaded, 16)
            ae.dma_start(a["uplast"], uplast[:, :, :]).then_inc(stored, 16)

            def down_tile(r, i, t, skip, tail=False):
                for j in range(6):
                    cj = C_DOWN + RING + 6 * t + j
                    if not (tail and t == 1 and j >= 2):
                        hi_chunk(ae, r, cj, down_width(cj))
                n = 2 * i + t
                ae.wait_ge(o_ready, KM + n + 1)
                ae.wait_ge(sq_used, 3 * KM + n - 3)
                nc.scalar.activation(sq[:, t:t + 1, :], o2[:, bass.ds(n, 1), :], ACT.Square).then_inc(sq_ready, 1)

            with ae.Fori(0, KM // 2 - 1) as i:
                down_tile(3 * i, i, 0, False)
                down_tile(3 * i, i, 1, False)
            down_tile(3 * (KM // 2 - 1), KM // 2 - 1, 0, False, True)
            down_tile(3 * (KM // 2 - 1), KM // 2 - 1, 1, False, True)
            root(4)

        @block.vector
        def _(dve):
            st = Steps(dve, dve_step)
            dve.wait_ge(pt_loaded, 48)
            dve.wait_ge(con_loaded, 16)
            nc.vector.tensor_scalar(kix[:, :], ptab[:, :], float(IDX_DIM), con[:, DIX:DIX + 1],
                                    ALU.mult, ALU.add).then_inc(kix_ready, 1)
            st.link(nc.vector.memset(den[:, :], 1.0))

            dve.wait_ge(par_loaded, 16)
            for k in range(KM):
                if k in (1, 3):
                    lo_chunk(dve, nc.vector, lo_dve, 0, C_IK + k // 2, 8 * IKW)
                dve.wait_ge(h_hi_ready, k + 1)
                nc.vector.scalar_tensor_tensor(h_lo[:, k, :], x0[:, k, :], par[:, G1 + k:G1 + k + 1],
                                               h_hi[:, k, :].bitcast(F32), ALU.mult,
                                               ALU.subtract).then_inc(h_lo_ready, 1)
            lo_chunk(dve, nc.vector, lo_dve, 0, C_IQ)
            lo_chunk(dve, nc.vector, lo_dve, 0, C_IQ + 1)

            def inv_rms(n):
                dve.wait_ge(sum_ready, n)
                nc.vector.tensor_scalar(var[:, :], misc[:, 0:T], 1.0 / D_MODEL, EPS,
                                        ALU.mult, ALU.add).then_inc(var_ready, 1)
                dve.wait_ge(root_ready, n)
                st.link(nc.vector.reciprocal(rms[:, :], var[:, :]))

            inv_rms(1)
            mul = ALU.mult

            dve.wait_ge(chunk_used, C_IK + 2)
            ps = bank[0]
            st.then(nc.vector.tensor_tensor(ikT[:, :], ps[0:64, 0:T], rms[0:64, :], mul))
            new_even, new_odd = slice(TP, T, 2), slice(TP + 1, T, 2)
            st.then(nc.vector.tensor_tensor(iknew[0:64, :], ps[0:64, new_even], rms[0:64, new_even], mul))
            st.then(nc.vector.tensor_tensor(iknew[64:128, :], ps[0:64, new_odd], rms[0:64, new_odd], mul))
            nc.vector.tensor_tensor(iwT[:, :], ps[64:80, 0:T], rms[64:80, :], mul).then_inc(tile_freed, 1)
            dve.wait_ge(iw_ready, 1)
            st.then(nc.vector.tensor_copy(iwq[:, 0:32], misc[:, 0:32]))
            st.then(nc.vector.tensor_copy(iwq[0:16, 32:48], misc[0:16, 32:48]))
            st.link(nc.vector.tensor_tensor(iwblk[:, :], misc[:, 64:72], con[:, BLK:BLK + DB], mul))
            dve.wait_ge(s_loaded, 16)
            dve.wait_ge(zeroed, 3)

            def index_queries(t):
                ps = bank[(T_IQ + t) % 2]
                dve.wait_ge(chunk_used, C_IQ + 2 * t + 2)
                if t >= 2:
                    dve.wait_ge(iq_used, 2 * t - 2)
                for e in range(2):
                    h = 2 * t + e
                    src = slice(64 * e, 64 * e + 64)
                    for half, new in ((0, new_even), (1, new_odd)):
                        off = h + 16 * half
                        st.then(nc.vector.tensor_tensor(
                            iqbd[64 * half:64 * half + 64, off:off + 160 * (PAIRS - 1) + 1:160],
                            ps[src, new], rms[src, new], mul))
                for e in range(2):
                    src = slice(64 * e, 64 * e + 64)
                    ins = nc.vector.tensor_tensor(iq[:, 2 * (t % 2) + e, :], ps[src, 0:T], rms[src, :], mul)
                    if e:
                        ins.then_inc(iq_ready, 1)
                    else:
                        st.then(ins)
                dve.wait_ge(iq_ready, t + 1)

            def index_sum(h):
                dve.wait_ge(relu_ready, h + 1)
                for n, (q0, nq, nk) in enumerate(QT):
                    acc = S[0:nq, S_AT[n]:S_AT[n] + nk]
                    ins = nc.vector.scalar_tensor_tensor(
                        acc, relu[0:nq, h % 2, A_AT[n]:A_AT[n] + nk], iwq[0:nq, 16 * n + h:16 * n + h + 1], acc,
                        ALU.mult, ALU.add)
                    if n < 2:
                        st.then(ins)
                    else:
                        ins.then_inc(relu_used, 1)
                dve.wait_ge(relu_used, h + 1)

            for t in range(8):
                if t >= 1:
                    lo_chunk(dve, nc.vector, lo_dve, 0, C_IQ + 2 * t)
                    lo_chunk(dve, nc.vector, lo_dve, 0, C_IQ + 2 * t + 1)
                if t >= 2:
                    index_sum(2 * t - 4)
                    index_sum(2 * t - 3)
                index_queries(t)
            for h in range(12, 16):
                index_sum(h)

            def prompt_round(n):
                for q, (q0, nq, nk) in enumerate(QT):
                    src = (S if n == 0 else W)[0:nq, S_AT[q]:S_AT[q] + nk + SENT]
                    st.then(nc.vector.max(top8[0:nq, q, :], src))
                st.wait()
                for q, (q0, nq, nk) in enumerate(QT):
                    src = (S if n == 0 else W)[0:nq, S_AT[q]:S_AT[q] + nk + SENT]
                    st.then(nc.vector.match_replace(W[0:nq, S_AT[q]:S_AT[q] + nk + SENT], top8[0:nq, q, :], src, NEG))
                st.wait()

            def sample_round(n):
                src = (Ss if n == 0 else Ws)[:, :]
                st.link(nc.vector.max(top8s[:, :], src))
                st.link(nc.vector.match_replace(Ws[:, :], top8s[:, :], src, NEG))

            def tile_ready(t):
                dve.wait_ge(chunk_used, C_PROJ + 2 * t + 2)
                return bank[(T_PROJ + t) % 2]

            ROUNDS_P = (TOPK_P + SENT) // 8
            ROUNDS_S = TOPK_S // 8
            rounds_s = iter(range(ROUNDS_S))
            rounds_p = iter(range(ROUNDS_P))
            for t in range(U0, U0 + 8):
                prompt_round(next(rounds_p))
                if t == 7:
                    for n in rounds_p:
                        prompt_round(n)
                ps = tile_ready(t)
                nc.vector.tensor_tensor(U[:, t, POOL_BUF:POOL_BUF + T], ps[:, 0:T], rms[:, :],
                                        mul).then_inc(tile_freed, 1)
                if t == 1:
                    dve.wait_ge(ssum_done, 1)
                    st.then(nc.vector.tensor_copy(Ss[:, 0:512], bank[2][0:DB, :]))
                    st.then(nc.vector.tensor_copy(Ss[:, 512:1024], bank[3][0:DB, :]))
                    st.link(nc.vector.tensor_copy(Ss[:, 1024:1025], misc[0:DB, 0:1]))
                if t >= 2:
                    sample_round(next(rounds_s))
            dve.wait_ge(tile_freed, 9)
            for q, (q0, nq, nk) in enumerate(QT):
                sl = slice(S_AT[q], S_AT[q] + nk)
                st.link(nc.vector.tensor_tensor(W[0:nq, sl], S[0:nq, sl], W[0:nq, sl], ALU.not_equal))
                st.link(nc.vector.tensor_scalar(W[0:nq, sl], W[0:nq, sl], -1.0, -MASKED, ALU.add, ALU.mult))

            def pool_group(g):
                w = WINDOWS[g]
                u = U[:, 2 * g:2 * g + 2, :]
                src, step, n = u, 1, 0
                while step < w:
                    dst = win[n % 2]
                    st.link(nc.vector.tensor_tensor(dst[:, :, 2 * step - 1:UW], src[:, :, 2 * step - 1:UW],
                                                    src[:, :, step - 1:UW - step], ALU.add))
                    src, step, n = dst, 2 * step, n + 1
                d = diff[:, 2 * g:2 * g + 2, :]
                inv = con[:, INV + 16 * g:INV + 16 * g + 16].unsqueeze(1).broadcast_to([P, 2, 16])
                st.link(nc.vector.tensor_tensor(win[2][:, :, 0:16], src[:, :, POOL_BUF:POOL_BUF + 16], inv, mul))
                st.then(nc.vector.tensor_tensor(d[:, :, 0:16], win[2][:, :, 0:16], u[:, :, POOL_BUF:POOL_BUF + 16],
                                                ALU.subtract))
                st.link(nc.vector.scalar_tensor_tensor(d[:, :, 16:TP], src[:, :, POOL_BUF + 16:UW], 1.0 / w,
                                                       u[:, :, POOL_BUF + 16:UW], ALU.mult, ALU.subtract))
                s = win[2][:, :, 16:16 + DB]
                un = u[:, :, POOL_BUF + TP:POOL_BUF + T]
                st.link(nc.vector.tensor_reduce(s, poolst[:, 2 * g:2 * g + 2, :, POOL_BUF - (w - 1):POOL_BUF],
                                                AX.X, ALU.add))
                st.link(nc.vector.tensor_tensor(s, s, un, ALU.add))
                nc.vector.scalar_tensor_tensor(d[:, :, TP:T], s, 1.0 / w, un, ALU.mult,
                                               ALU.subtract).then_inc(diff_ready, 1)
                dve.wait_ge(diff_ready, g + 1)

            dve.wait_ge(poolw_loaded, 32)
            for t in range(K0, K0 + 4):
                ps = tile_ready(t)
                dst = kT[:, t - K0, :] if t < V0 else vT[:, t - V0, :]
                ins = nc.vector.tensor_tensor(dst, ps[:, 0:T], rms[:, :], mul)
                ins.then_inc(tile_freed, 1)
                pool_group(t - K0)
            for t in range(Q0, Q0 + HEADS):
                h = t - Q0
                sample_round(next(rounds_s))
                sample_round(next(rounds_s))
                ps = tile_ready(t)
                off = (h // 4) * 64 + h
                st.then(nc.vector.tensor_tensor(qbd[:, off:off + 136 * (DB - 1) + 1:136], ps[:, TP:T],
                                                rms[:, TP:T], mul))
                nc.vector.tensor_tensor(qT[:, h, 0:TP], ps[:, 0:TP], rms[:, 0:TP], mul).then_inc(tile_freed, 1)

            for j in range(8):
                dve.wait_ge(pmix_hi, j + 1)
                nc.vector.scalar_tensor_tensor(h_lo[:, HEADS + j, :], bank[2 + j % 2][:, 0:T],
                                               par[:, PSC + j:PSC + j + 1], h_hi[:, HEADS + j, :].bitcast(F32),
                                               ALU.mult, ALU.subtract).then_inc(pmix_lo, 1)
            dve.wait_ge(pmix_lo, 8)

            SCALE = float(HD) ** -0.5

            def w_o_pool(j):
                dve.wait_ge(chunk_used, C_WOP + j + 1)
                nc.vector.tensor_copy(part[:, j, :], bank[(T_WOP + j) % 2][:, 0:T]).then_inc(tile_freed, 1)

            for h in range(HEADS):
                p = h % 2
                dve.wait_ge(score_done, h + 1)
                if h >= 2:
                    dve.wait_ge(probT_done, h - 1)
                for n, (q0, nq, nk) in enumerate(QT):
                    src = bank[2][0:nq, A_AT[n]:A_AT[n] + nk] if n < 2 else bank[3][0:nq, 0:nk]
                    st.then(nc.vector.tensor_tensor_reduce(
                        prob[0:nq, p, A_AT[n]:A_AT[n] + nk], src, W[0:nq, S_AT[n]:S_AT[n] + nk], 1.0, -BIG,
                        ALU.add, ALU.max, mx[0:nq, n:n + 1]))
                st.wait()
                st.then(nc.vector.tensor_scalar(nmx[:, 0:2], mx[:, 0:2], -SCALE, None, ALU.mult))
                nc.vector.tensor_scalar(nmx[0:16, 2:3], mx[0:16, 2:3], -SCALE, None, ALU.mult).then_inc(soft_in, 1)
                dve.wait_ge(exp_done, 3 * h + 3)
                st.link(nc.vector.reciprocal(rden[:, :], den[:, :]))
                for n, (q0, nq, nk) in enumerate(QT):
                    sl = prob[0:nq, p, A_AT[n]:A_AT[n] + nk]
                    nc.vector.tensor_scalar(sl, sl, rden[0:nq, n:n + 1], None, ALU.mult).then_inc(prob_ready, 1)
                dve.wait_ge(prob_ready, 3 * h + 3)
                w_o_pool(2 * h)
                if h < HEADS:
                    n = next(rounds_s, None)
                    if n is not None:
                        sample_round(n)
                    n = next(rounds_s, None)
                    if n is not None:
                        sample_round(n)
                w_o_pool(2 * h + 1)
                dve.wait_ge(o_hi, h + 1)
                nc.vector.tensor_tensor(h_lo[:, h, 0:TP], bank[5][:, 0:TP], h_hi[:, h, 0:TP].bitcast(F32),
                                        ALU.subtract).then_inc(o_lo, 1)
            assert next(rounds_s, None) is None
            st.link(nc.vector.tensor_tensor(Ws[:, :], Ss[:, :], Ws[:, :], ALU.not_equal))
            nc.vector.tensor_scalar(Ws[:, :], Ws[:, :], -1.0, -MASKED, ALU.add, ALU.mult).then_inc(smask_ready, 1)
            dve.wait_ge(sscore_done, 1)
            st.then(nc.vector.reduce_max(mxs[:, 0:1], bank[2][0:64, :], AX.X))
            st.then(nc.vector.reduce_max(mxs[:, 1:2], bank[3][0:64, :], AX.X))
            st.link(nc.vector.tensor_copy(mxs[:, 2:3], bank[6][0:64, 0:1]))
            st.link(nc.vector.reduce_max(mxs[:, 3:4], mxs[:, 0:3], AX.X))
            nc.vector.tensor_scalar(mxs[:, 4:5], mxs[:, 3:4], -SCALE, None, ALU.mult).then_inc(ssoft_in, 1)
            dve.wait_ge(sexp_done, 3)
            st.link(nc.vector.reduce_sum(dens[:, 3:4], dens[:, 0:3], AX.X))
            st.link(nc.vector.reciprocal(dens[:, 4:5], dens[:, 3:4]))
            st.link(nc.vector.tensor_scalar(probs, probs, dens[:, 4:5], None, ALU.mult))
            nc.vector.tensor_scalar(pnm[:, :], con[0:64, M64:M64 + DB], probs[:, 1024:1025], None,
                                    ALU.mult).then_inc(sprob_ready, 1)
            dve.wait_ge(sprobT_done, 1)
            nc.vector.tensor_copy(pnew[:, :], bank[5][0:DB, 0:64]).then_inc(sprobT_dve, 1)
            dve.wait_ge(so_hi, 1)
            nc.vector.tensor_tensor(h_lo[:, 0:HEADS, TP:T], misc[:, 0:64].rearrange("p (b h) -> p h b", b=DB),
                                    h_hi[:, 0:HEADS, TP:T].bitcast(F32), ALU.subtract).then_inc(so_lo, 1)

            st.link(nc.vector.memset(sumsq[:, :], 0.0))

            def add_squares(n, slot):
                dve.wait_ge(sq_ready, n)
                nc.vector.tensor_tensor(sumsq[:, :], sumsq[:, :], sq[:, slot, :], ALU.add).then_inc(sq_used, 1)
                dve.wait_ge(sq_used, n - 1)

            for j in range(KM):
                dve.wait_ge(chunk_used, C_WOA + j + 1)
                nc.vector.tensor_tensor(part[:, j, :], bank[(T_WOA + j) % 2][:, 0:T], part[:, j, :],
                                        ALU.add).then_inc(o_ready, 1)
                if j:
                    add_squares(KM + j, (j - 1) % 2)
            dve.wait_ge(o_ready, KM)
            add_squares(2 * KM, (KM - 1) % 2)
            inv_rms(2)
            dve.wait_ge(x1_loaded, 16)

            def residual(o, x, g, k):
                st.link(nc.vector.scalar_tensor_tensor(o[:, k, :], o[:, k, :], par[:, g + k:g + k + 1], rms[:, :],
                                                       ALU.mult, ALU.mult))

            for k in range(KM):
                residual(part, x1, G2, k)
                nc.vector.tensor_tensor(x1[:, k, :], x1[:, k, :], part[:, k, :], ALU.add).then_inc(xt_ready, 1)
                if k == 3:
                    lo_chunk(dve, nc.vector, lo_dve, 0, C_UP + 1)
                if k >= 1:
                    dve.wait_ge(h_hi_ready, KM + k)
                    nc.vector.scalar_tensor_tensor(h_lo[:, k - 1, :], x1[:, k - 1, :], par[:, G3 + k - 1:G3 + k],
                                                   h_hi[:, k - 1, :].bitcast(F32), ALU.mult,
                                                   ALU.subtract).then_inc(h_lo_ready, 1)
            dve.wait_ge(h_hi_ready, 2 * KM)
            nc.vector.scalar_tensor_tensor(h_lo[:, KM - 1, :], x1[:, KM - 1, :], par[:, G3 + KM - 1:G3 + KM],
                                           h_hi[:, KM - 1, :].bitcast(F32), ALU.mult,
                                           ALU.subtract).then_inc(h_lo_ready, 1)
            inv_rms(3)
            dve.wait_ge(cst_loaded, 16)
            dve.wait_ge(x_spilled, 16)
            for i in range(2):
                wi = par[:, CWT + i * 2 * FT:CWT + (i + 1) * 2 * FT].unsqueeze(2).broadcast_to([P, 2 * FT, DB])
                st.link(nc.vector.tensor_tensor(cst[:, i], cst[:, i], wi, mul))
            st.link(nc.vector.tensor_tensor(cst[:, 0], cst[:, 0], cst[:, 1], ALU.add))
            st.link(nc.vector.memset(up[:, :, :, 0:2], 0.0))

            def scaled_up(r, p, v):
                f = 2 * r + v
                dve.wait_ge(chunk_used, C_UP + 4 * r + 2 * v + 2)
                nc.vector.tensor_tensor(up[:, p, v, 2:2 + T], bank[(T_UP + v) % 2][:, 0:T], rms[:, :],
                                        mul).then_inc(up_ready, 1)
                dve.wait_ge(up_ready, f + 1)
                st.then(nc.vector.tensor_copy(uplast[:, bass.ds(f, 1), :],
                                              up[:, p, v:v + 1, TP:2 + T]))

            def conv_taps(r, v, p):
                f = 2 * r + v
                dve.wait_ge(act_ready, f + 1)
                for i in range(2):
                    st.link(nc.vector.scalar_tensor_tensor(
                        act[:, v, 0:TP], up[:, p, v, i:i + TP], par[:, bass.ds(CWT + 2 * FT * i + f, 1)],
                        act[:, v, 0:TP], ALU.mult, ALU.add))
                ins = nc.vector.tensor_tensor(act[:, v:v + 1, TP:T], act[:, v:v + 1, TP:T],
                                              cst[:, 0, bass.ds(f, 1), :], ALU.add)
                if v:
                    st.link(ins)
                else:
                    ins.then_inc(conv_ready, 1)

            def ffn_pair(r, p, last=False):
                lo_chunk(dve, nc.vector, lo_dve, r, C_UP + 3)
                scaled_up(r, p, 0)
                conv_taps(r, 0, p)
                if not last:
                    lo_chunk(dve, nc.vector, lo_dve, r, C_UP + 5)
                scaled_up(r, p, 1)
                conv_taps(r, 1, p)
                dve.wait_ge(silu_ready, r + 1)
                nc.vector.tensor_tensor(act[:, 0, :], act[:, 0, :], act[:, 1, :], mul).then_inc(gate_ready, 1)
                dve.wait_ge(g_hi_ready, r + 1)
                nc.vector.tensor_tensor(g_lo[:, bass.ds(r, 1), :], act[:, 0:1, :],
                                        g_hi[:, bass.ds(r, 1), :].bitcast(F32),
                                        ALU.subtract).then_inc(g_lo_ready, 1)

            STEPS_PER_PAIR = 7
            n0 = st.n
            with dve.Fori(0, FT // 2 - 1) as i:
                st.turn = 2 * STEPS_PER_PAIR * i
                ffn_pair(2 * i, 0)
                ffn_pair(2 * i + 1, 1)
            assert st.n - n0 == 2 * STEPS_PER_PAIR, st.n - n0
            st.turn = 0
            st.n = n0 + (FT - 2) * STEPS_PER_PAIR
            ffn_pair(FT - 2, 0)
            ffn_pair(FT - 1, 1, last=True)
            lo_chunk(dve, nc.vector, lo_dve, 0, C_DOWN + 1, down_width(C_DOWN + 1))
            lo_chunk(dve, nc.vector, lo_dve, 0, C_DOWN + 3, down_width(C_DOWN + 3))
            nc.vector.memset(sumsq[:, :], 0.0).then_inc(dve_step, 1)
            st.n += 1
            st.wait()
            dve.wait_ge(x2_loaded, 16)

            def down_out(i, t, r, tail=False, head=False):
                for j in (1, 3, 5):
                    cj = C_DOWN + RING + 6 * t + j
                    if not (tail and t == 1 and j >= 3):
                        lo_chunk(dve, nc.vector, lo_dve, r, cj, down_width(cj))
                n = 2 * i + t
                dve.wait_ge(chunk_used, 4 * r + C_DOWN + 6 * (t + 1))
                nc.vector.tensor_copy(o2[:, bass.ds(n, 1), :],
                                      bank[(T_DOWN + t) % 2][:, 0:T].unsqueeze(1)).then_inc(o_ready, 1)
                dve.wait_ge(sq_ready, 3 * KM + n + 1)
                nc.vector.tensor_tensor(sumsq[:, :], sumsq[:, :], sq[:, t, :], ALU.add).then_inc(sq_used, 1)
                dve.wait_ge(sq_used, 3 * KM + n - 1)

            with dve.Fori(0, KM // 2 - 1) as i:
                down_out(i, 0, 3 * i)
                down_out(i, 1, 3 * i)
            down_out(KM // 2 - 1, 0, 3 * (KM // 2 - 1), tail=True)
            down_out(KM // 2 - 1, 1, 3 * (KM // 2 - 1), tail=True)
            inv_rms(4)
            for k in range(KM):
                residual(o2, x2, G4, k)
                nc.vector.tensor_tensor(o2[:, k, :], x2[:, k, :], o2[:, k, :], ALU.add).then_inc(y_ready, 1)

        @block.tensor
        def _(pe):
            mm = nc.tensor.matmul

            def stream_tile(r, cjs, kts, x_hi, x_lo, out):
                total, done = sum(len(k) for k in kts), 0
                for cj, ks in zip(cjs, kts):
                    lo_wait(pe, r, cj)
                    s = cj % RING
                    for i, k in enumerate(ks):
                        w_hi = hi[:, s, i * P:(i + 1) * P]
                        w_lo = lo[:, s, i * P:(i + 1) * P]
                        mm(out, w_hi, x_hi[:, k, :], start=(done == 0), stop=False)
                        mm(out, w_hi, x_lo[:, k, :], start=False, stop=False)
                        done += 1
                        last = mm(out, w_lo, x_hi[:, k, :], start=False, stop=(done == total))
                    last.then_inc(chunk_used, 1)

            def tile_free(n):
                if isinstance(n, int) and n < 2:
                    return
                pe.wait_ge(tile_freed, n - 1)

            HALF = [list(range(8)), list(range(8, 16))]
            out = bank[0][0:IKW, 0:T]
            pe.wait_ge(con_loaded, 16)
            for k in range(KM):
                if k % 8 == 0:
                    lo_wait(pe, 0, C_IK + k // 8)
                pe.wait_ge(h_lo_ready, k + 1)
                s, i = k // 8, k % 8
                w_hi, w_lo = (w[:, s, i * IKW:(i + 1) * IKW] for w in (hi, lo))
                mm(out, w_hi, h_hi[:, k, :], start=(k == 0), stop=False)
                mm(out, w_hi, h_lo[:, k, :], start=False, stop=False)
                last = mm(out, w_lo, h_hi[:, k, :], start=False, stop=(k == KM - 1))
                if i == 7:
                    last.then_inc(chunk_used, 1)
                pe.wait_ge(sq_ready, k + 1)
                ins = mm(misc[:, 0:T], con[:, ONE:ONE + P], sq[:, k % 2, :], start=(k == 0), stop=(k == KM - 1))
                if k < KM - 1:
                    ins.then_inc(sq_used, 1)
                else:
                    ins.then_inc(sum_ready, 1)

            def q_idx_tile(r, t, p):
                stream_tile(r, [C_IQ + 2 * t, C_IQ + 2 * t + 1], HALF, h_hi, h_lo,
                            bank[(T_IQ + t) % 2][:, 0:T])

            def index_scores(h, p, e):
                if not isinstance(h, int) or h >= 2:
                    pe.wait_ge(relu_ready, h - 1)
                for n, (q0, nq, nk) in enumerate(QT):
                    o = bank[2 + 2 * e][0:nq, A_AT[n]:A_AT[n] + nk] if n < 2 else bank[3 + 2 * e][0:nq, 0:nk]
                    last = mm(o, iq[:, 2 * p + e, q0:q0 + nq], ikT[:, 0:nk], start=True, stop=True)
                last.then_inc(iq_used, 1)

            q_idx_tile(0, 0, 0)
            pe.wait_ge(tile_freed, 1)
            ident = con[:, IDN:IDN + P]
            nc.tensor.transpose(misc[:, 0:16], iwT[:, 0:128], con[0:16, IDN:IDN + 16])
            nc.tensor.transpose(misc[:, 16:32], iwT[:, 128:256], con[0:16, IDN:IDN + 16])
            nc.tensor.transpose(misc[0:16, 32:48], iwT[:, 256:272], con[0:16, IDN:IDN + 16])
            mm(misc[:, 64:72], con[0:16, HREP:HREP + P], iwT[:, TP:T], start=True, stop=True).then_inc(iw_ready, 1)

            def q_idx_pair(r, n):
                for t in (1, 2):
                    if isinstance(n, int) and 2 * n + t == 1:
                        pass
                    else:
                        pe.wait_ge(iq_ready, 2 * n + t - 1)
                    q_idx_tile(r, t, t % 2)
                    pe.wait_ge(iq_ready, 2 * n + t)
                    for e in range(2):
                        index_scores(4 * n + 2 * (t - 1) + e, (t - 1) % 2, e)

            q_idx_pair(0, 0)
            with pe.Fori(1, 3) as i:
                q_idx_pair(i, i)
            pe.wait_ge(iq_ready, 6)
            q_idx_tile(0, 7, 1)
            for t in (6, 7):
                pe.wait_ge(iq_ready, t + 1)
                for e in range(2):
                    index_scores(2 * t + e, t % 2, e)
            pe.wait_ge(relu_ready, 16)
            pe.wait_ge(kidx_loaded, 16 * PAIRS * PAGES)
            for b in range(PAIRS):
                w = iqbd[:, b * P:(b + 1) * P]
                f, l = b == 0, b == PAIRS - 1
                mm(bank[4][:, :], w, kidx[:, b, 0:512], start=f, stop=l)
                mm(bank[5][:, :], w, kidx[:, b, 512:1024], start=f, stop=l)
                last = mm(bank[6][:, 0:1], w, iknew[:, b:b + 1], start=f, stop=l)
            last.then_inc(sidx_done, 1)

            def proj_tile(r, t, n):
                if isinstance(n, int) and n < T_PROJ + 2:
                    pe.wait_ge(iq_ready, n - 2)
                else:
                    pe.wait_ge(tile_freed, n - T_PROJ)
                stream_tile(r, [C_PROJ + 2 * t, C_PROJ + 2 * t + 1], HALF, h_hi, h_lo,
                            bank[(T_PROJ + t) % 2][:, 0:T])

            proj_tile(0, 0, T_PROJ)
            pe.wait_ge(srelu_done, 3)
            mm(bank[2][0:DB, :], iwblk[:, :], relus[:, 0:512], start=True, stop=True)
            mm(bank[3][0:DB, :], iwblk[:, :], relus[:, 512:1024], start=True, stop=True)
            mm(misc[0:DB, 0:1], iwblk[:, :], relus[:, 1024:1025], start=True, stop=True).then_inc(ssum_done, 1)
            proj_tile(0, 1, T_PROJ + 1)
            with pe.Fori(0, 9) as i:
                proj_tile(i, 2, 2 * i + T_PROJ + 2)
                proj_tile(i, 3, 2 * i + T_PROJ + 3)
            for g in range(KV):
                nc.tensor.transpose(bank[6][:, g * 128:g * 128 + 128], vT[:, g, 0:128], ident)
                nc.tensor.transpose(bank[6][:, 256 + g * 128:384 + g * 128], vT[:, g, 128:256], ident)
                nc.tensor.transpose(misc[0:16, g * 128:g * 128 + 128], vT[:, g, 256:272], ident)
                last = nc.tensor.transpose(misc[0:DB, 256 + g * 128:384 + g * 128], vT[:, g, TP:T], ident)
            last.then_inc(vt_done, 1)
            pe.wait_ge(diff_ready, 4)
            for j in range(8):
                g = j // 2
                if j >= 2:
                    pe.wait_ge(pmix_lo, j - 1)
                for k in range(2):
                    last = mm(bank[2 + j % 2][:, 0:T], poolw[:, g, k, (j % 2) * P:(j % 2 + 1) * P],
                              diff[:, 2 * g + k, :], start=(k == 0), stop=(k == 1))
                last.then_inc(pmix_done, 1)

            def w_o_tile(c, j, half, n):
                pe.wait_ge(tile_freed, n)
                stream_tile(0, [c + j], [HALF[half]], h_hi, h_lo, bank[(T_WOP + j) % 2][:, 0:T])

            pe.wait_ge(tile_freed, 21)
            pe.wait_ge(pmix_lo, 8)
            for h in range(HEADS):
                p, g = h % 2, h // (HEADS // KV)
                if h:
                    pe.wait_ge(soft_in, h)
                for n, (q0, nq, nk) in enumerate(QT):
                    o = bank[2][0:nq, A_AT[n]:A_AT[n] + nk] if n < 2 else bank[3][0:nq, 0:nk]
                    last = mm(o, qT[:, h, q0:q0 + nq], kT[:, g, 0:nk], start=True, stop=True)
                last.then_inc(score_done, 1)
                w_o_tile(C_WOP, 2 * h, 1, 20 + 2 * h)
                pe.wait_ge(prob_ready, 3 * h + 3)
                if h:
                    pe.wait_ge(probT_ready, 2 * h)
                tr = nc.tensor.transpose
                for n, (q0, nq, nk) in enumerate(QT):
                    tr(bank[4][:, q0:q0 + nq], prob[0:nq, p, A_AT[n]:A_AT[n] + 128], con[0:nq, IDN:IDN + nq])
                for n in (1, 2):
                    q0, nq, nk = QT[n]
                    tr(bank[4][:, TP + q0 - 128:TP + q0 - 128 + nq],
                       prob[0:nq, p, A_AT[n] + 128:A_AT[n] + 256], con[0:nq, IDN:IDN + nq])
                tr(bank[4][0:16, 416:432], prob[0:16, p, A_AT[2] + 256:A_AT[2] + 272],
                   con[0:16, IDN:IDN + 16]).then_inc(probT_done, 1)
                w_o_tile(C_WOP, 2 * h + 1, 1, 21 + 2 * h)
                pe.wait_ge(probT_ready, 2 * h + 2)
                if h:
                    pe.wait_ge(o_lo, h)
                else:
                    pe.wait_ge(vrow_ready, 4)
                vg = slice(g * HD, (g + 1) * HD)
                mm(bank[5][:, 0:TP], vrow[:, 0, vg], probT[:, p, 0:TP], start=True, stop=False)
                mm(bank[5][:, 128:TP], vrow[:, 1, vg], probT[:, p, TP:TP + 144], start=False, stop=False)
                mm(bank[5][:, 256:TP], vrow[0:16, 2, vg], probT[0:16, p, 416:432], start=False,
                   stop=True).then_inc(pv_done, 1)
            pe.wait_ge(soft_in, HEADS)
            for b in range(DB):
                pe.wait_ge(k_loaded[b % 2], 16 * (b // 2 + 1))
                for g in range(KV):
                    w = qbd[:, (2 * b + g) * 64:(2 * b + g) * 64 + 64]
                    f = b == 0 and g == 0
                    for c in range(2):
                        last = mm(bank[2 + c][0:64, :], w,
                                  kring[:, b % 2, 4 * c:4 * c + 4, g * PAGE:(g + 1) * PAGE], start=f, stop=False)
                    last = mm(bank[6][0:64, 0:1], w, kT[:, g, TP + b:TP + b + 1], start=f, stop=False)
                last.then_inc(kq_used, 1)
            pe.wait_ge(smask_ready, 1)
            e8 = con[0:DB, EXP8:EXP8 + 64]
            mm(bank[2][0:64, :], e8, Ws[:, 0:512], start=False, stop=True)
            mm(bank[3][0:64, :], e8, Ws[:, 512:1024], start=False, stop=True)
            mm(bank[6][0:64, 0:1], e8, Ws[:, 1024:1025], start=False, stop=True).then_inc(sscore_done, 1)
            pe.wait_ge(sprob_ready, 1)
            for g in range(PAGES):
                nc.tensor.transpose(bank[4][:, 64 * g:64 * g + 64], probs[:, g * 128:g * 128 + 128],
                                    con[0:64, IDN:IDN + 64])
            pe.wait_ge(o_lo, HEADS)
            nc.tensor.transpose(bank[5][0:DB, 0:64], pnm[:, :], con[0:64, IDN:IDN + 64]).then_inc(sprobT_done, 1)
            pe.wait_ge(sprobT_act, 1)
            pe.wait_ge(sprobT_dve, 1)
            by_head = "p (b h) -> p b h"
            for g in range(KV):
                hs = slice(4 * g, 4 * g + 4)
                mm(misc[:, 0:64].rearrange(by_head, b=DB)[:, :, hs], vnew[:, g * HD:(g + 1) * HD],
                   pnew[:, :].rearrange(by_head, b=DB)[:, :, hs], start=(g == 0), stop=False, skip_group_check=True)
            for b in range(DB):
                pe.wait_ge(v_loaded[b % 2], 16 * (b // 2 + 1))
                for g in range(KV):
                    cols = slice(8 * b + 4 * g, 8 * b + 4 * g + 4)
                    for n in range(PAGES):
                        last = mm(misc[:, cols], vring[:, b % 2, n, g * HD:(g + 1) * HD], probsT[:, n, cols],
                                  start=False, stop=(b == DB - 1 and g == 1 and n == PAGES - 1),
                                  skip_group_check=True)
                last.then_inc(vq_used if b < DB - 1 else spv_done, 1)
            pe.wait_ge(so_lo, 1)
            for j in range(KM):
                if j < 2:
                    pe.wait_ge(tile_freed, 36 + j)
                else:
                    pe.wait_ge(o_ready, j - 1)
                stream_tile(0, [C_WOA + j], [HALF[0]], h_hi, h_lo, bank[(T_WOA + j) % 2][:, 0:T])

            def total(n, used):
                pe.wait_ge(sq_used, used)
                mm(misc[:, 0:T], con[:, ONE:ONE + P], sumsq[:, :], start=True, stop=True).then_inc(sum_ready, 1)

            total(2, 2 * KM - 1)
            pe.wait_ge(o_ready, KM)
            out = bank[T_UP % 2][:, 0:T]
            for k in range(KM):
                if k % 8 == 0:
                    lo_wait(pe, 0, C_UP + k // 8)
                pe.wait_ge(h_lo_ready, KM + k + 1)
                s, i = (C_UP + k // 8) % RING, k % 8
                w_hi, w_lo = (w[:, s, i * P:(i + 1) * P] for w in (hi, lo))
                mm(out, w_hi, h_hi[:, k, :], start=(k == 0), stop=False)
                mm(out, w_hi, h_lo[:, k, :], start=False, stop=False)
                last = mm(out, w_lo, h_hi[:, k, :], start=False, stop=(k == KM - 1))
                if i == 7:
                    last.then_inc(chunk_used, 1)
                pe.wait_ge(sq_ready, 2 * KM + k + 1)
                ins = mm(misc[:, 0:T], con[:, ONE:ONE + P], sq[:, k % 2, :], start=(k == 0), stop=(k == KM - 1))
                if k < KM - 1:
                    ins.then_inc(sq_used, 1)
                else:
                    ins.then_inc(sum_ready, 1)

            def up_tile(r, v):
                if not (isinstance(r, int) and r == 0):
                    pe.wait_ge(up_ready, 2 * r + v - 1)
                stream_tile(r, [C_UP + 2 * v, C_UP + 2 * v + 1], HALF, h_hi, h_lo,
                            bank[(T_UP + v) % 2][:, 0:T])

            up_tile(0, 1)
            with pe.Fori(1, FT) as i:
                up_tile(i, 0)
                up_tile(i, 1)
            pe.wait_ge(g_lo_ready, FT)
            KD = [list(range(DOWN_CUT[j], DOWN_CUT[j + 1])) for j in range(6)]

            def down_tile(r, i, t):
                if isinstance(i, int) and i == 0:
                    pe.wait_ge(up_ready, 2 * FT - 1 + t)
                else:
                    pe.wait_ge(o_ready, 2 * i + t + KM - 1)
                stream_tile(r, [C_DOWN + 6 * t + j for j in range(6)], KD, g_hi, g_lo,
                            bank[(T_DOWN + t) % 2][:, 0:T])

            down_tile(0, 0, 0)
            down_tile(0, 0, 1)
            with pe.Fori(1, KM // 2) as i:
                down_tile(3 * i, i, 0)
                down_tile(3 * i, i, 1)
            total(4, 4 * KM - 2)
    ctx.close()


_OUTS = {
    "y": (P, KM, T), "k": (P, KV, T), "v": (P, KV, T), "ik": (IDX_DIM, T), "u": (P, 8, T),
    "uplast": (P, 2 * FT, 2 + DB), "old_pool": (DB, POOL_BUF - 1, POOL_WIDTH), "old_conv": (DB, 1, 2 * D_FF),
}


def kernel(**inputs):
    import concourse.bacc as bacc
    from concourse.bass_utils import run_bass_kernel_spmd

    f = {n: np.asarray(v) for n, v in inputs.items()}

    def tiles(w, cols):
        k, n = w.shape
        return np.ascontiguousarray(
            w.reshape(k // P, P, n // cols, cols).transpose(2, 1, 0, 3)).reshape(n // cols, P, -1)

    def features(x):
        n = x.shape[-1]
        x = np.moveaxis(x, -1, 0)
        return np.ascontiguousarray(np.moveaxis(x.reshape((n // P, P) + x.shape[1:]), 1, 0))

    def pairs(x):
        s = x.shape[:-1]
        return np.moveaxis(x.reshape(s + (2, FT, P)), -3, -2).reshape(s + (2 * D_FF,))

    w_in = f["w_in"][0]
    q_end, k_end = HEADS * HD, HEADS * HD + KV * HD
    v_end = k_end + KV * HD
    iq_end = v_end + IDX_HEADS * IDX_DIM
    iw_end = iq_end + IKW
    w_main = np.concatenate([w_in[:, v_end:iq_end], w_in[:, iw_end:], w_in[:, q_end:v_end], w_in[:, :q_end]], 1)
    x = np.concatenate([f["meta_tokens"], f["x_prompt"][0], f["x_sample"][:, 0]], 0)
    par = [features(f[n][0]) for n in ("g_mix_pre", "g_mix_post", "g_ffn_pre", "g_ffn_post", "pool_scale")]
    par += [features(pairs(f["conv_w"][0])[i]) for i in range(3)] + [features(pairs(f["conv_b"][0]))]
    con, causal = shape_constants()
    n_pool = f["cache_k"].shape[1]
    table = np.ascontiguousarray(f["page_table"]).astype(np.int32, copy=False)
    state_conv = features(pairs(f["state_conv"][0]))
    arrays = {
        "x": features(x), "par": np.concatenate(par, 1), "con": con, "causal": causal,
        "w_ik": tiles(w_in[:, iq_end:iw_end], IKW)[0], "w_in": tiles(w_main, P), "w_o": tiles(f["w_o"][0], P),
        "w_up": tiles(pairs(f["w_up"][0]), P), "w_down": tiles(f["w_down"][0], P),
        "pool_w": np.ascontiguousarray(
            f["pool_w"][0].reshape(4, 2, P, 256).transpose(2, 0, 1, 3)).reshape(P, -1),
        "state_pool": features(f["state_pool"][0]).reshape(P, -1),
        "state_conv": np.ascontiguousarray(state_conv.transpose(0, 3, 1, 2)),
        "state_pool_rows": np.ascontiguousarray(f["state_pool"][0][:, 1:]),
        "state_conv_rows": np.ascontiguousarray(f["state_conv"][0][:, 1:]),
        "cache_k": np.ascontiguousarray(f["cache_k"][0].transpose(0, 3, 2, 1)).reshape(n_pool, P, KV * PAGE),
        "cache_v": f["cache_v"][0].reshape(n_pool, PAGE, KV * HD),
        "cache_kidx": np.ascontiguousarray(f["cache_kidx"][0].transpose(0, 2, 1)).reshape(n_pool * IDX_DIM, PAGE),
        "pages": table.reshape(1, -1),
        "pages_even": np.ascontiguousarray(table[0::2]).reshape(1, -1),
        "pages_odd": np.ascontiguousarray(table[1::2]).reshape(1, -1),
    }
    nc = bacc.Bacc("TRN2", target_bir_lowering=False, num_devices=1)
    ap, maps = {}, {}
    for n, v in arrays.items():
        maps["in_" + n] = np.ascontiguousarray(v)
        ap[n] = nc.dram_tensor("in_" + n, v.shape, mybir.dt.from_np(v.dtype), kind="ExternalInput").ap()
    for n, shape in _OUTS.items():
        ap[n] = nc.dram_tensor("out_" + n, shape, F32, kind="ExternalOutput").ap()
    build_program(nc, ap)
    got = run_bass_kernel_spmd(nc, [maps], core_ids=[0]).results[0]
    o = {n: np.asarray(got["out_" + n]) for n in _OUTS}

    def rows(x):
        return np.ascontiguousarray(x.transpose(2, 1, 0)).reshape(x.shape[2], -1)

    y, k, v, u, ik = rows(o["y"]), rows(o["k"]), rows(o["v"]), rows(o["u"]), np.ascontiguousarray(o["ik"].T)
    last = rows(o["uplast"]).reshape(2 + DB, FT, 2, P).transpose(0, 2, 1, 3).reshape(2 + DB, 2 * D_FF)
    kv = (KV, HD)
    return (
        y[N_META:TP][None], y[TP:][:, None],
        k[:TP].reshape((1, 1, TP) + kv), v[:TP].reshape((1, 1, TP) + kv), ik[:TP][None, None],
        u[TP - POOL_BUF:TP][None, None], last[:2][None, None],
        k[TP:].reshape((1, DB, 1) + kv), v[TP:].reshape((1, DB, 1) + kv), ik[TP:].reshape(1, DB, 1, -1),
        np.concatenate([o["old_pool"], u[TP:][:, None]], 1)[None],
        np.concatenate([o["old_conv"], last[2:][:, None]], 1)[None],
    )
```

```python
from contextlib import ExitStack

import concourse.bass as bass
from concourse import mybir
import numpy as np

F32 = mybir.dt.float32
F32R = mybir.dt.float32r
I32 = mybir.dt.int32
U32 = mybir.dt.uint32
ALU = mybir.AluOpType
ACT = mybir.ActivationFunctionType
AX = mybir.AxisListType

P = 128
D_MODEL, SEQ, DB, PAST, PAGE = 2048, 256, 8, 1024, 128
N_META, HEADS, KV, HD = 16, 8, 2, 128
IDX_HEADS, IDX_DIM = 16, 64
POOL_WIDTH, POOL_BUF, D_FF = 1024, 15, 5632
TOPK_MAX, EPS = 256, 1e-6
WINDOWS = (2, 4, 8, 16)

TP = N_META + SEQ
T = TP + DB
CONV = 3
L = N_META - (CONV - 1)
TU = T - L
TG = T - N_META
KM = D_MODEL // P
PAGES = PAST // PAGE
CTX = PAST + 1
TOPK_P = min(TOPK_MAX, TP // 4)
TOPK_S = min(TOPK_MAX, CTX // 4)
FT = D_FF // P
IKW = IDX_DIM + IDX_HEADS
PAIRS = DB // 2

QT = [(0, 128, 128), (128, 128, 256), (256, 16, 272)]
SENT = -(-TOPK_P // 8) * 8 - TOPK_P
S_AT = [0, 128 + SENT, 384 + 2 * SENT]
S_W = 656 + 3 * SENT
A_AT = [0, 128, 384]
NEG = -3e38
BIG = 3e38
MASKED = -1e30

RING = 4
CW = 8 * P

C_IK = 0
C_IQ = C_IK + 2
C_PROJ = C_IQ + 16
C_WOP = C_PROJ + 40
C_WOA = C_WOP + 16
C_UP = C_WOA + 16
C_DOWN = C_UP + 4 * FT
DOWN_CUT = [0, 8, 16, 23, 30, 37, 44]
T_IK, T_IQ = 0, 1
T_PROJ = T_IQ + 8
T_WOP = T_PROJ + 20
T_WOA = T_WOP + 16
T_UP = T_WOA + 16
T_DOWN = T_UP + 2 * FT
Y_POOL = (1, 4, 7, 10, 13)
U0, K0, V0, Q0 = 0, 8, 10, 12

G1, G2, G3, G4, PSC = 0, 16, 32, 48, 64
CWT, CBT = 72, 72 + 3 * 2 * FT
PAR_W = CBT + 2 * FT
IDN, ONE, HREP, BLK, EXP8, M64, INV, DIX = 0, 128, 256, 384, 392, 456, 464, 528
CON_W = 529


def shape_constants():
    c = np.zeros((P, CON_W), np.float32)
    c[:, IDN:IDN + P] = np.eye(P)
    c[:, ONE:ONE + P] = 1.0
    for b in range(DB):
        for h in range(IDX_HEADS):
            c[h, HREP + IDX_HEADS * b + h] = 1.0
            c[IDX_HEADS * b + h, BLK + b] = 1.0
        c[b, EXP8 + HEADS * b:EXP8 + HEADS * (b + 1)] = 1.0
        c[HEADS * b:HEADS * (b + 1), M64 + b] = 1.0
    for g, w in enumerate(WINDOWS):
        c[:, INV + 16 * g:INV + 16 * (g + 1)] = 1.0 / np.minimum(np.arange(16) + 1, w)
    c[:, DIX] = np.arange(P) % IDX_DIM
    s = np.full((P, S_W), NEG, np.float32)
    for (q0, nq, nk), at in zip(QT, S_AT):
        for q in range(P):
            s[q, at:at + min(q0 + q + 1, nk)] = 0.0
        s[:, at + nk:at + nk + SENT] = BIG
    return c, s


class Steps:

    def __init__(self, eng, sem):
        self.eng, self.sem, self.n, self.turn = eng, sem, 0, 0

    def then(self, ins):
        ins.then_inc(self.sem, 1)
        self.n += 1

    def wait(self):
        self.eng.wait_ge(self.sem, self.turn + self.n)

    def link(self, ins):
        self.then(ins)
        self.wait()


def build_program(nc, a):
    ctx = ExitStack()

    def sem(name):
        return ctx.enter_context(nc.semaphore(name))

    def sb(name, shape, dt=F32, at=None):
        return (at or ctx).enter_context(nc.sbuf_tensor(name, shape, dt))

    raw = sb("raw", [P, RING, CW])
    hi = sb("hi", [P, RING, CW], F32R)
    lo = sb("lo", [P, RING, CW], F32R)
    par = sb("par", [P, PAR_W])
    con = sb("con", [P, CON_W])
    rms = sb("rms", [P, T])
    var = sb("var", [P, T])
    root_sb = sb("root_sb", [P, T])
    sumsq = sb("sumsq", [P, T])
    sq = sb("sq", [P, 2, T])

    at_h = ExitStack()
    h_hi = sb("h_hi", [P, KM, T], F32R, at_h)
    h_lo = sb("h_lo", [P, KM, T], F32R, at_h)

    at_1 = ExitStack()
    cache_ring = sb("cache_ring", [P, 4096], at=at_1)
    mixed = sb("mixed", [P, KM * T], at=at_1)
    short = sb("short", [P, 3984], at=at_1)
    part = sb("part", [P, KM, T], at=at_1)
    qT = sb("qT", [P, HEADS, T], at=at_1)
    qbd = sb("qbd", [P, 2 * DB * 64], at=at_1)
    qnew = sb("qnew", [P, 2 * 64], at=at_1)
    kT = sb("kT", [P, KV, T], at=at_1)
    vT = sb("vT", [P, KV, T], at=at_1)
    vrow = sb("vrow", [P, 3, KV * HD], at=at_1)
    vnew = sb("vnew", [DB, KV * HD], at=at_1)
    ikT = sb("ikT", [IDX_DIM, T], at=at_1)
    iknew = sb("iknew", [P, PAIRS], at=at_1)
    iwT = sb("iwT", [IDX_HEADS, T], at=at_1)
    iwq = sb("iwq", [P, 3 * IDX_HEADS], at=at_1)
    iwblk = sb("iwblk", [P, DB], at=at_1)
    top8 = sb("top8", [P, 3, 8], at=at_1)
    top8s = sb("top8s", [DB, 8], at=at_1)
    mx = sb("mx", [P, 3], at=at_1)
    nmx = sb("nmx", [P, 3], at=at_1)
    den = sb("den", [P, 3], at=at_1)
    rden = sb("rden", [P, 3], at=at_1)
    mxs = sb("mxs", [64, 5], at=at_1)
    dens = sb("dens", [64, 5], at=at_1)
    pnm = sb("pnm", [64, DB], at=at_1)
    pnew = sb("pnew", [DB, 64], at=at_1)
    ptab = sb("ptab", [P, PAIRS * PAGES], I32, at_1)
    ptrow = sb("ptrow", [1, DB * PAGES], I32, at_1)
    kix = sb("kix", [P, PAIRS * PAGES], U32, at_1)
    cst_free = sb("outs", [HEADS, DB * KV * HD], at=at_1)
    S = sb("S", [P, S_W], at=at_1)
    W = sb("W", [P, S_W], at=at_1)
    Ss = sb("Ss", [DB, CTX], at=at_1)
    Ws = sb("Ws", [DB, CTX], at=at_1)

    kidx = cache_ring[:, :].rearrange("p (b s) -> p b s", b=PAIRS)
    vring = cache_ring[:, :].rearrange("p (r g e) -> p r g e", r=2, g=PAGES)
    U = mixed[:, 0:8 * (POOL_BUF + T)].rearrange("p (j t) -> p j t", j=8)
    UW = POOL_BUF + TP
    at = 8 * (POOL_BUF + T)
    win = [mixed[:, at + n * 2 * UW:at + (n + 1) * 2 * UW].rearrange("p (j t) -> p j t", j=2) for n in range(3)]
    kring = mixed[:, 0:4096].rearrange("p (r g e) -> p r g e", r=2, g=PAGES)

    def v_slot(b):
        return vring[:, b % 2] if b % 4 < 2 else kring[:, b % 2]

    x1 = mixed[:, :].rearrange("p (k t) -> p k t", k=KM)
    iq = short[0:IDX_DIM, 0:4 * T].rearrange("p (h t) -> p h t", h=4)
    relu = short[:, 1120:1120 + 1312].rearrange("p (r s) -> p r s", r=2)
    iqbd = short[:, 2432:2432 + PAIRS * P]
    relus = short[:, 2944:2944 + CTX]
    diff = short[:, 0:8 * T].rearrange("p (j t) -> p j t", j=8)
    prob = short[:, 0:1312].rearrange("p (r s) -> p r s", r=2)
    probT = short[:, 1312:1312 + 864].rearrange("p (r s) -> p r s", r=2)
    probs = short[0:64, 2176:2176 + CTX]
    outs = cst_free[0:HEADS, :].rearrange("h (b e) -> h b e", b=DB)
    probsT = short[:, 3204:3204 + 512].rearrange("p (g c) -> p g c", g=PAGES)
    x0 = part
    partf = part[:, :, :].rearrange("p k t -> p (k t)")
    poolw = partf[:, 0:2048].rearrange("p (g k d) -> p g k d", g=4, k=2)
    poolst = partf[:, 2048:2048 + 960].rearrange("p (j b s) -> p j b s", j=8, b=DB)
    end_1 = at_1

    end_1.close()
    at_2 = ExitStack()
    g_hi = sb("g_hi", [P, FT, TG], F32R, at_2)
    g_lo = sb("g_lo", [P, FT, TG], F32R, at_2)
    cst = sb("cst", [P, 2, 2 * FT, DB], at=at_2)
    up = sb("up", [P, 2, 2, TU], at=at_2)
    act = sb("act", [P, 2, TG], at=at_2)
    uplast = sb("uplast", [P, 2 * FT, 2 + DB], at=at_2)
    at_2.close()
    at_h.close()
    at_3 = ExitStack()
    x2 = sb("x2", [P, KM, TG], at=at_3)
    o2 = sb("o2", [P, KM, TG], at=at_3)
    at_3.close()

    bank = [ctx.enter_context(nc.psum_tensor(f"bank{i}", [P, 512], F32)) for i in range(8)]
    misc = bank[7]

    def out_by_head(g):
        return bank[4][:, 0:P].rearrange("p (b g h) -> p g h b", b=DB, g=KV)[:, g, 4 * g:4 * g + 4, :]

    kscr = nc.dram_tensor("kscr", [DB * PAGES, P, KV * PAGE], F32).ap()
    vscr = nc.dram_tensor("vscr", [DB * PAGES, P, KV * HD], F32).ap()
    xscr = nc.dram_tensor("xscr", [P, KM, TG], F32).ap()

    raw_loaded = [sem(f"raw_loaded{i}") for i in range(RING)]
    hi_ready = sem("hi_ready")
    lo_pool = sem("lo_pool")
    lo_dve = sem("lo_dve")
    chunk_used = sem("chunk_used")
    tile_freed = sem("tile_freed")
    x_loaded = [sem(f"x_loaded{i}") for i in range(4)]
    par_loaded = sem("par_loaded")
    con_loaded = sem("con_loaded")
    s_loaded = sem("s_loaded")
    pt_loaded = sem("pt_loaded")
    poolw_loaded = sem("poolw_loaded")
    kix_ready = sem("kix_ready")
    kidx_loaded = sem("kidx_loaded")
    scr_loaded = sem("scr_loaded")
    k_loaded = [sem(f"k_loaded{i}") for i in range(2)]
    v_loaded = [sem(f"v_loaded{i}") for i in range(4)]
    x1_loaded = sem("x1_loaded")
    x2_loaded = sem("x2_loaded")
    x_spilled = sem("x_spilled")
    cst_loaded = sem("cst_loaded")
    stored = sem("stored")
    u_stored = sem("u_stored")
    copied = sem("copied")
    zeroed = sem("zeroed")
    dve_step = sem("dve_step")
    act_step = sem("act_step")
    pool_step = sem("pool_step")
    h_hi_ready = sem("h_hi_ready")
    h_lo_ready = sem("h_lo_ready")
    sq_ready = sem("sq_ready")
    sq_used = sem("sq_used")
    sum_ready = sem("sum_ready")
    var_ready = sem("var_ready")
    root_ready = sem("root_ready")
    iw_ready = sem("iw_ready")
    iwq_done = sem("iwq_done")
    iq_ready = sem("iq_ready")
    iq_used = sem("iq_used")
    relu_ready = sem("relu_ready")
    relu_used = sem("relu_used")
    sidx_done = sem("sidx_done")
    srelu_done = sem("srelu_done")
    ssum_done = sem("ssum_done")
    v_ready = sem("v_ready")
    vt_done = sem("vt_done")
    vrow_ready = sem("vrow_ready")
    diff_ready = sem("diff_ready")
    pmix_done = sem("pmix_done")
    pmix_hi = sem("pmix_hi")
    pmix_lo = sem("pmix_lo")
    qkv_ready = sem("qkv_ready")
    score_done = sem("score_done")
    soft_in = sem("soft_in")
    exp_done = sem("exp_done")
    prob_ready = sem("prob_ready")
    probT_done = sem("probT_done")
    probT_ready = sem("probT_ready")
    pv_done = sem("pv_done")
    o_hi = sem("o_hi")
    o_lo = sem("o_lo")
    kq_used = sem("kq_used")
    vq_used = sem("vq_used")
    smask_ready = sem("smask_ready")
    sscore_done = sem("sscore_done")
    ssoft_in = sem("ssoft_in")
    sexp_done = sem("sexp_done")
    sprob_ready = sem("sprob_ready")
    sprobT_done = sem("sprobT_done")
    sprobT_act = sem("sprobT_act")
    sprobT_dve = sem("sprobT_dve")
    spv_done = sem("spv_done")
    so_hi = sem("so_hi")
    so_lo = sem("so_lo")
    o_ready = sem("o_ready")
    o_scaled = sem("o_scaled")
    xt_ready = sem("xt_ready")
    y_pool = sem("y_pool")
    outs_act = sem("outs_act")
    outs_dve = sem("outs_dve")
    outT_done = sem("outT_done")
    up_ready = sem("up_ready")
    act_ready = sem("act_ready")
    conv_ready = sem("conv_ready")
    silu_ready = sem("silu_ready")
    gate_ready = sem("gate_ready")
    g_hi_ready = sem("g_hi_ready")
    g_lo_ready = sem("g_lo_ready")
    y_ready = sem("y_ready")

    def lo_wait(eng, r, cj):
        if cj < C_PROJ:
            eng.wait_ge(lo_dve, 4 * r + cj + 1)
        elif cj < C_UP:
            eng.wait_ge(lo_pool, 4 * r + cj - C_PROJ + 1)
        elif (cj - C_UP) % 2 == 0:
            eng.wait_ge(lo_pool, 2 * r + C_UP - C_PROJ + (cj - C_UP) // 2 + 1)
        else:
            eng.wait_ge(lo_dve, 2 * r + C_PROJ + (cj - C_UP + 1) // 2)

    def hi_chunk(act_eng, r, cj, width=CW):
        s = cj % RING
        act_eng.wait_ge(raw_loaded[s], 16 * (r + cj // RING + 1))
        if cj >= RING:
            act_eng.wait_ge(chunk_used, 4 * r + cj - RING + 1)
        nc.scalar.activation(hi[:, s, 0:width], raw[:, s, 0:width], ACT.Copy).then_inc(hi_ready, 1)

    def lo_chunk(eng, ops, done, r, cj, width=CW):
        s = cj % RING
        eng.wait_ge(hi_ready, 4 * r + cj + 1)
        if cj >= RING:
            eng.wait_ge(chunk_used, 4 * r + cj - RING + 1)
        ops.tensor_tensor(lo[:, s, 0:width], raw[:, s, 0:width], hi[:, s, 0:width].bitcast(F32),
                          ALU.subtract).then_inc(done, 1)

    def down_width(cj):
        i = (cj - C_DOWN) % 6
        return (DOWN_CUT[i + 1] - DOWN_CUT[i]) * P

    with nc.Block() as block:

        @block.sync
        def _(sp):
            def load(r, cj, src, width=CW):
                if not isinstance(r, int):
                    lo_wait(sp, r - 1, cj) if cj >= C_UP else lo_wait(sp, r, cj - RING)
                elif 4 * r + cj >= RING:
                    lo_wait(sp, 0, 4 * r + cj - RING)
                sp.dma_start(raw[:, cj % RING, 0:width], src).then_inc(raw_loaded[cj % RING], 16)

            for j in range(2):
                load(0, C_IK + j, a["w_ik"][:, j * 8 * IKW:(j + 1) * 8 * IKW], 8 * IKW)

            def pages(n):
                page = sp.value_load(ptrow[0:1, bass.ds(n, 1)], min_val=0, max_val=a["cache_k"].shape[0] - 1)
                sp.dma_start(kscr[n], a["cache_k"][page]).then_inc(scr_loaded, 16)
                sp.dma_start(vscr[n], a["cache_v"][page]).then_inc(scr_loaded, 16)

            w_in = a["w_in"]

            def load_in(r, cj, t):
                for j in range(2):
                    load(r, cj + j, w_in[t, :, j * CW:(j + 1) * CW])

            load_in(0, C_IQ, 0)
            sp.wait_ge(pt_loaded, 48)
            with sp.Fori(0, 4) as i:
                for t in (1, 2):
                    load_in(i, C_IQ + 2 * t, 2 * i + t)
                    for n in range(2 * t - 2, 3 * t - 1):
                        pages(5 * i + n)
            for t in (9, 10):
                load_in(0, C_IQ + 2 * t, t)
                pages(2 * t + 2)
                pages(2 * t + 3)
            with sp.Fori(0, 8) as i:
                for t in (11, 12):
                    load_in(i, C_IQ + 2 * t, 2 * i + t)
                    for n in range(2 * t + 2, 3 * t - 7):
                        pages(5 * i + n)
            load_in(0, C_IQ + 54, 27)
            kv_src = [[kscr, vscr][n].rearrange("(b g) p e -> b p g e", b=DB) for n in range(2)]

            def load_k(b):
                if b >= 2:
                    sp.wait_ge(kq_used, b - 1)
                sp.dma_start(kring[:, b % 2], kv_src[0][b]).then_inc(k_loaded[b % 2], 16)

            def load_v(b):
                if b in (2, 3):
                    sp.wait_ge(kq_used, DB - 3 + b)
                if b >= 4:
                    sp.wait_ge(spv_done if b % 2 else vq_used, b // 2 - 1)
                sp.dma_start(v_slot(b), kv_src[1][b]).then_inc(v_loaded[b % 4], 16)

            def load_wo(n):
                j, half = n % KM, 1 - n // KM
                load(0, C_WOP + n, a["w_o"][j, :, half * CW:(half + 1) * CW])

            for n in range(4):
                load_wo(n)
            sp.wait_ge(scr_loaded, 2 * DB * PAGES * 16)
            sp.wait_ge(sidx_done, 1)
            sp.wait_ge(diff_ready, 4)
            sp.wait_ge(u_stored, 16)
            load_k(0)
            load_k(1)
            for n in range(4, 8):
                load_wo(n)
            load_v(0)
            load_v(1)
            load_k(2)
            for h in range(HEADS):
                load_wo(8 + h)
                if h + 3 < DB:
                    load_k(h + 3)
                elif h < 7:
                    load_v(h - 3)
            for n in range(16, 19):
                load_wo(n)
            load_v(4)
            load_v(5)
            load_wo(19)
            load_v(6)
            load_v(7)
            load_wo(20)
            load_wo(21)
            sp.wait_ge(spv_done, 4)
            for n in range(4):
                sp.dma_start(x1[:, 4 * n:4 * n + 4, :], a["x"][:, 4 * n:4 * n + 4, :]).then_inc(x1_loaded, 16)
                if n % 2:
                    load_wo(22 + n // 2)
            sp.wait_ge(so_lo, 2)
            for n in range(2):
                sp.dma_start(cst[:, n], a["state_conv"][:, n]).then_inc(cst_loaded, 16)
                load_wo(24 + n)
            for n in range(26, 32):
                load_wo(n)

            def load_up(r):
                for j in range(4):
                    load(r, C_UP + j, a["w_up"][2 * r + j // 2, :, (j % 2) * CW:(j % 2 + 1) * CW])

            load_up(0)
            with sp.Fori(1, FT) as i:
                load_up(i)

            def load_down(i, t):
                for j in range(6):
                    c0, c1 = DOWN_CUT[j], DOWN_CUT[j + 1]
                    load(3 * i, C_DOWN + 6 * t + j, a["w_down"][2 * i + t, :, c0 * P:c1 * P], (c1 - c0) * P)

            with sp.Fori(0, KM // 2) as i:
                load_down(i, 0)
                load_down(i, 1)
            for k in range(0, KM, 2):
                in_pool = sum(n <= k + 1 for n in Y_POOL)
                sp.wait_ge(y_ready, k + 2 - in_pool)
                if in_pool:
                    sp.wait_ge(y_pool, in_pool)
                sp.dma_start(a["y"][:, k:k + 2, :], o2[:, k:k + 2, :]).then_inc(stored, 16)
            sp.wait_ge(stored, 16 * (4 + KM // 2))
            sp.wait_ge(u_stored, 16)
            sp.wait_ge(copied, 32)

        @block.gpsimd
        def _(pool):
            nc.gpsimd.memset(iqbd, 0.0).then_inc(zeroed, 1)
            nc.gpsimd.memset(qbd[:, :], 0.0).then_inc(zeroed, 1)
            nc.gpsimd.memset(qnew[:, :], 0.0).then_inc(zeroed, 1)
            nc.gpsimd.memset(U[:, :, 0:POOL_BUF], 0.0).then_inc(zeroed, 1)
            pool.wait_ge(kix_ready, 1)
            kidx_rows = a["cache_kidx"]
            for b in range(PAIRS):
                for g in range(PAGES):
                    n = b * PAGES + g
                    nc.gpsimd.indirect_dma_start(
                        kidx[:, b, g * PAGE:(g + 1) * PAGE], None, kidx_rows,
                        bass.IndirectOffsetOnAxis(ap=kix[:, n:n + 1], axis=0)).then_inc(kidx_loaded, 16)
            with pool.Fori(0, (C_UP - C_PROJ) // 4) as i:
                for j in range(4):
                    lo_chunk(pool, nc.gpsimd, lo_pool, i, C_PROJ + j)
            for j in (0, 2):
                lo_chunk(pool, nc.gpsimd, lo_pool, 0, C_UP + j)
            pool.wait_ge(x1_loaded, 64)
            for k in range(KM):
                pool.wait_ge(o_scaled, k + 1)
                nc.gpsimd.tensor_tensor(x1[:, k, L:], x1[:, k, L:], part[:, k, L:], ALU.add).then_inc(xt_ready, 1)
            with pool.Fori(1, FT) as i:
                for j in (0, 2):
                    lo_chunk(pool, nc.gpsimd, lo_pool, i, C_UP + j)
            with pool.Fori(0, KM // 2) as i:
                for j in range(0, 12, 2):
                    lo_chunk(pool, nc.gpsimd, lo_pool, 3 * i, C_DOWN + j, down_width(C_DOWN + j))
            for k in Y_POOL:
                pool.wait_ge(o_scaled, KM + k + 1)
                nc.gpsimd.tensor_tensor(o2[:, k, :], x2[:, k, :], o2[:, k, :], ALU.add).then_inc(y_pool, 1)

        @block.scalar
        def _(act_eng):
            ae = act_eng
            st = Steps(ae, act_step)
            for n in range(4):
                ae.dma_start(x0[:, 4 * n:4 * n + 4, :], a["x"][:, 4 * n:4 * n + 4, :]).then_inc(x_loaded[n], 16)
                if n == 0:
                    ae.dma_start(par[:, :], a["par"]).then_inc(par_loaded, 16)
                    ae.dma_start(con[:, :], a["con"]).then_inc(con_loaded, 16)
                    ae.dma_start(ptab[0:64, :], a["pages_even"].broadcast_to([64, PAIRS * PAGES])).then_inc(pt_loaded, 16)
                    ae.dma_start(ptab[64:128, :], a["pages_odd"].broadcast_to([64, PAIRS * PAGES])).then_inc(pt_loaded, 16)
                    ae.dma_start(ptrow[:, :], a["pages"]).then_inc(pt_loaded, 16)
            ae.dma_start(S[:, :], a["causal"]).then_inc(s_loaded, 16)
            ae.dma_start(a["old_pool"], a["state_pool_rows"]).then_inc(copied, 16)
            ae.dma_start(a["old_conv"], a["state_conv_rows"]).then_inc(copied, 16)
            ae.wait_ge(par_loaded, 16)
            for k in range(KM):
                ae.wait_ge(x_loaded[k // 4], 16)
                if k in (1, 3):
                    hi_chunk(ae, 0, C_IK + k // 2, 8 * IKW)
                nc.scalar.activation(h_hi[:, k, :], x0[:, k, :], ACT.Copy,
                                     scale=par[:, G1 + k:G1 + k + 1]).then_inc(h_hi_ready, 1)
                if k >= 2:
                    ae.wait_ge(sq_used, k - 1)
                nc.scalar.activation(sq[:, k % 2, :], x0[:, k, :], ACT.Square).then_inc(sq_ready, 1)
            hi_chunk(ae, 0, C_IQ)
            hi_chunk(ae, 0, C_IQ + 1)

            def root(n, first=0):
                ae.wait_ge(var_ready, n)
                nc.scalar.activation(root_sb[:, first:], var[:, first:], ACT.Sqrt).then_inc(root_ready, 1)

            root(1)
            ae.wait_ge(sum_ready, 1)
            ae.wait_ge(h_lo_ready, KM)
            ae.dma_start(partf[:, 0:2048], a["pool_w"]).then_inc(poolw_loaded, 16)
            ae.dma_start(partf[:, 2048:2048 + 960], a["state_pool"]).then_inc(poolw_loaded, 16)

            IDX_SCALE = float(IDX_DIM) ** -0.5 * float(IDX_HEADS) ** -0.5

            def relu_head(h, p):
                ae.wait_ge(iq_used, h + 1)
                if not isinstance(h, int) or h >= 2:
                    ae.wait_ge(relu_used, h - 1)
                nc.scalar.activation(relu[:, p, 0:384], bank[2 + 2 * p][:, 0:384], ACT.Relu,
                                     scale=IDX_SCALE).then_inc(act_step, 1)
                nc.scalar.activation(relu[0:16, p, 384:656], bank[3 + 2 * p][0:16, 0:272], ACT.Relu,
                                     scale=IDX_SCALE).then_inc(relu_ready, 1)

            hi_chunk(ae, 0, C_IQ + 2)
            hi_chunk(ae, 0, C_IQ + 3)
            for t in (1, 2):
                hi_chunk(ae, 0, C_IQ + 2 * t + 2)
                hi_chunk(ae, 0, C_IQ + 2 * t + 3)
                for p in range(2):
                    relu_head(2 * (t - 1) + p, p)
            with ae.Fori(1, 3) as i:
                for t in (1, 2):
                    hi_chunk(ae, i, C_IQ + 2 * t + 2)
                    hi_chunk(ae, i, C_IQ + 2 * t + 3)
                    for p in range(2):
                        relu_head(4 * i + 2 * (t - 1) + p, p)
            for h in range(12, 16):
                relu_head(h, h % 2)
                hi_chunk(ae, 0, C_PROJ + h - 12)
            ae.wait_ge(sidx_done, 1)
            nc.scalar.activation(relus[:, 0:512], bank[4][:, :], ACT.Relu, scale=IDX_SCALE).then_inc(srelu_done, 1)
            nc.scalar.activation(relus[:, 512:1024], bank[5][:, :], ACT.Relu, scale=IDX_SCALE).then_inc(srelu_done, 1)
            nc.scalar.activation(relus[:, 1024:1025], bank[6][:, 0:1], ACT.Relu,
                                 scale=IDX_SCALE).then_inc(srelu_done, 1)
            with ae.Fori(0, 7) as i:
                for j in range(4):
                    hi_chunk(ae, i, C_PROJ + 4 + j)
            ae.wait_ge(diff_ready, 4)
            ae.dma_start(a["u"], U[:, :, POOL_BUF:POOL_BUF + T]).then_inc(u_stored, 16)
            ae.dma_start(a["k"], kT[:, :, :]).then_inc(stored, 16)
            ae.dma_start(a["v"], vT[:, :, :]).then_inc(stored, 16)
            ae.dma_start(a["ik"], ikT[:, :]).then_inc(stored, 16)
            with ae.Fori(7, 9) as i:
                for j in range(4):
                    hi_chunk(ae, i, C_PROJ + 4 + j)
            ae.wait_ge(vt_done, 1)
            nc.scalar.activation(vrow[:, 0, :], bank[6][:, 0:256], ACT.Copy).then_inc(vrow_ready, 1)
            nc.scalar.activation(vrow[:, 1, :], bank[6][:, 256:512], ACT.Copy).then_inc(vrow_ready, 1)
            nc.scalar.activation(vrow[0:16, 2, :], misc[0:16, 0:256], ACT.Copy).then_inc(vrow_ready, 1)
            nc.scalar.activation(vnew[:, :], misc[0:DB, 256:512], ACT.Copy).then_inc(vrow_ready, 1)
            for j in range(4):
                hi_chunk(ae, 0, C_WOP + j)
            for j in range(8):
                ae.wait_ge(pmix_done, j + 1)
                nc.scalar.activation(h_hi[:, HEADS + j, L:], bank[2 + j % 4][:, L:T], ACT.Copy,
                                     scale=par[:, PSC + j:PSC + j + 1]).then_inc(pmix_hi, 1)
            SCALE = float(HD) ** -0.5

            def exp_head(h):
                ae.wait_ge(soft_in, h + 1)
                for n, (q0, nq, nk) in enumerate(QT):
                    sl = prob[0:nq, h % 2, A_AT[n]:A_AT[n] + nk]
                    nc.scalar.activation(sl, sl, ACT.Exp, scale=SCALE, bias=nmx[0:nq, n:n + 1],
                                         accum_out=den[0:nq, n:n + 1]).then_inc(exp_done, 1)

            def head_out(h):
                ae.wait_ge(pv_done, h + 1)
                nc.scalar.activation(h_hi[:, h, L:TP], bank[5][:, L:TP], ACT.Copy).then_inc(o_hi, 1)

            exp_head(0)
            for h in range(HEADS):
                p = h % 2
                hi_chunk(ae, 0, C_WOP + 4 + h)
                ae.wait_ge(probT_done, h + 1)
                nc.scalar.activation(probT[:, p, 0:416], bank[4][:, 0:416], ACT.Copy).then_inc(probT_ready, 1)
                nc.scalar.activation(probT[0:16, p, 416:432], bank[4][0:16, 416:432], ACT.Copy).then_inc(probT_ready, 1)
                if h + 1 < HEADS:
                    exp_head(h + 1)
                    head_out(h)
            ae.wait_ge(ssoft_in, 1)
            for n, (c0, c1) in enumerate(((0, 512), (512, 1024), (1024, 1025))):
                src = bank[6 + n][0:64, :] if n < 2 else mxs[:, 2:3]
                nc.scalar.activation(probs[:, c0:c1], src, ACT.Exp, scale=SCALE,
                                     bias=mxs[:, 4:5], accum_out=dens[:, n:n + 1]).then_inc(sexp_done, 1)
            head_out(HEADS - 1)
            hi_chunk(ae, 0, C_WOP + 12)
            hi_chunk(ae, 0, C_WOP + 13)
            ae.wait_ge(sprobT_done, 1)
            nc.scalar.activation(probsT[:, :, :], bank[4][:, :].rearrange("p (g c) -> p g c", g=PAGES),
                                 ACT.Copy).then_inc(sprobT_act, 1)
            hi_chunk(ae, 0, C_WOP + 14)
            for n in range(2):
                ae.wait_ge(spv_done, 2 * n + 1)
                nc.scalar.activation(outs[:, 4 * n:4 * n + 2, :], bank[2 + n][0:HEADS, :].rearrange(
                    "h (b e) -> h b e", b=2), ACT.Copy).then_inc(outs_act, 1)
                hi_chunk(ae, 0, C_WOP + 15 + 2 * n)
                hi_chunk(ae, 0, C_WOP + 16 + 2 * n)
            ae.wait_ge(outT_done, 1)
            for g in range(KV):
                nc.scalar.activation(h_hi[:, 4 * g:4 * g + 4, TP:T], out_by_head(g), ACT.Copy).then_inc(so_hi, 1)
            hi_chunk(ae, 0, C_WOA + 3)
            for j in range(KM):
                hi_chunk(ae, 0, C_WOA + 4 + j)
                ae.wait_ge(o_ready, j + 1)
                if j >= 2:
                    ae.wait_ge(sq_used, KM + j - 2)
                nc.scalar.activation(sq[:, j % 2, L:], part[:, j, L:], ACT.Square).then_inc(sq_ready, 1)
            root(2, L)
            for k in range(KM):
                ae.wait_ge(xt_ready, k + 1)
                nc.scalar.activation(h_hi[:, k, L:], x1[:, k, L:], ACT.Copy,
                                     scale=par[:, G3 + k:G3 + k + 1]).then_inc(h_hi_ready, 1)
                ae.wait_ge(sq_used, 2 * KM + k - 2)
                nc.scalar.activation(sq[:, k % 2, L:], x1[:, k, L:], ACT.Square).then_inc(sq_ready, 1)
            ae.dma_start(xscr, x1[:, :, N_META:]).then_inc(x_spilled, 16)
            root(3, L)
            def conv_bias(r, p, v):
                f = 2 * r + v
                ae.wait_ge(up_ready, f + 1)
                nc.scalar.activation(act[:, v, :], up[:, p, v, CONV - 1:], ACT.Identity,
                                     scale=par[:, bass.ds(CWT + 4 * FT + f, 1)],
                                     bias=par[:, bass.ds(CBT + f, 1)]).then_inc(act_ready, 1)

            def gated_hi(r):
                ae.wait_ge(gate_ready, r + 1)
                nc.scalar.activation(g_hi[:, bass.ds(r, 1), :], act[:, 0:1, :], ACT.Copy).then_inc(g_hi_ready, 1)

            def ffn_pair(r, p, last=False, first=False):
                widths = [down_width(C_DOWN + j) if last else CW for j in range(4)]
                hi_chunk(ae, r, C_UP + 4, widths[0])
                if not first:
                    gated_hi(r - 1)
                hi_chunk(ae, r, C_UP + 5, widths[1])
                if not first:
                    ae.wait_ge(g_lo_ready, r)
                conv_bias(r, p, 0)
                hi_chunk(ae, r, C_UP + 6, widths[2])
                ae.wait_ge(conv_ready, r + 1)
                nc.scalar.activation(act[:, 0, :], act[:, 0, :], ACT.Silu).then_inc(silu_ready, 1)
                hi_chunk(ae, r, C_UP + 7, widths[3])
                conv_bias(r, p, 1)

            ffn_pair(0, 0, first=True)
            ae.wait_ge(x_spilled, 16)
            with ae.Fori(0, FT // 2 - 1) as i:
                ffn_pair(2 * i + 1, 1)
                ffn_pair(2 * i + 2, 0)
            ffn_pair(FT - 1, 1, last=True)
            gated_hi(FT - 1)
            ae.wait_ge(chunk_used, C_DOWN)
            ae.dma_start(x2[:, :, :], xscr).then_inc(x2_loaded, 16)
            ae.dma_start(a["uplast"], uplast[:, :, :]).then_inc(stored, 16)

            def down_tile(r, i, t, skip, tail=False):
                for j in range(6):
                    cj = C_DOWN + RING + 6 * t + j
                    if not (tail and t == 1 and j >= 2):
                        hi_chunk(ae, r, cj, down_width(cj))
                n = 2 * i + t
                ae.wait_ge(o_ready, KM + n + 1)
                ae.wait_ge(sq_used, 3 * KM + n - 3)
                nc.scalar.activation(sq[:, t:t + 1, N_META:], o2[:, bass.ds(n, 1), :], ACT.Square).then_inc(sq_ready, 1)

            with ae.Fori(0, KM // 2 - 1) as i:
                down_tile(3 * i, i, 0, False)
                down_tile(3 * i, i, 1, False)
            down_tile(3 * (KM // 2 - 1), KM // 2 - 1, 0, False, True)
            down_tile(3 * (KM // 2 - 1), KM // 2 - 1, 1, False, True)
            root(4, N_META)

        @block.vector
        def _(dve):
            st = Steps(dve, dve_step)
            mul = ALU.mult
            dve.wait_ge(pt_loaded, 48)
            dve.wait_ge(con_loaded, 16)
            nc.vector.tensor_scalar(kix[:, :], ptab[:, :], float(IDX_DIM), con[:, DIX:DIX + 1],
                                    ALU.mult, ALU.add).then_inc(kix_ready, 1)
            st.link(nc.vector.memset(den[:, :], 1.0))

            dve.wait_ge(par_loaded, 16)
            for k in range(KM):
                if k in (1, 3):
                    lo_chunk(dve, nc.vector, lo_dve, 0, C_IK + k // 2, 8 * IKW)
                dve.wait_ge(h_hi_ready, k + 1)
                nc.vector.scalar_tensor_tensor(h_lo[:, k, :], x0[:, k, :], par[:, G1 + k:G1 + k + 1],
                                               h_hi[:, k, :].bitcast(F32), ALU.mult,
                                               ALU.subtract).then_inc(h_lo_ready, 1)
            lo_chunk(dve, nc.vector, lo_dve, 0, C_IQ)
            lo_chunk(dve, nc.vector, lo_dve, 0, C_IQ + 1)

            def inv_rms(n, first=0):
                r, v, y = rms[:, first:], var[:, first:], root_sb[:, first:]
                dve.wait_ge(sum_ready, n)
                nc.vector.tensor_scalar(v, misc[:, first:T], 1.0 / D_MODEL, EPS,
                                        ALU.mult, ALU.add).then_inc(var_ready, 1)
                dve.wait_ge(root_ready, n)
                st.link(nc.vector.reciprocal(r, y))
                st.link(nc.vector.scalar_tensor_tensor(y, r, -0.5, r, mul, mul))
                st.link(nc.vector.tensor_tensor(y, y, v, mul))
                st.link(nc.vector.scalar_tensor_tensor(r, y, 1.5, r, ALU.add, mul))

            inv_rms(1)

            dve.wait_ge(chunk_used, C_IK + 2)
            ps = bank[0]
            st.then(nc.vector.tensor_tensor(ikT[:, :], ps[0:64, 0:T], rms[0:64, :], mul))
            new_even, new_odd = slice(TP, T, 2), slice(TP + 1, T, 2)
            st.then(nc.vector.tensor_tensor(iknew[0:64, :], ps[0:64, new_even], rms[0:64, new_even], mul))
            st.then(nc.vector.tensor_tensor(iknew[64:128, :], ps[0:64, new_odd], rms[0:64, new_odd], mul))
            nc.vector.tensor_tensor(iwT[:, :], ps[64:80, 0:T], rms[64:80, :], mul).then_inc(tile_freed, 1)
            dve.wait_ge(iw_ready, 1)
            st.then(nc.vector.tensor_copy(iwq[:, 0:32], misc[:, 0:32]))
            st.then(nc.vector.tensor_copy(iwq[0:16, 32:48], misc[0:16, 32:48]))
            st.link(nc.vector.tensor_tensor(iwblk[:, :], misc[:, 64:72], con[:, BLK:BLK + DB], mul))
            dve.wait_ge(s_loaded, 16)
            dve.wait_ge(zeroed, 4)

            def index_queries(t):
                ps = bank[(T_IQ + t) % 2]
                dve.wait_ge(chunk_used, C_IQ + 2 * t + 2)
                if t >= 2:
                    dve.wait_ge(iq_used, 2 * t - 2)
                for e in range(2):
                    h = 2 * t + e
                    src = slice(64 * e, 64 * e + 64)
                    for half, new in ((0, new_even), (1, new_odd)):
                        off = h + 16 * half
                        st.then(nc.vector.tensor_tensor(
                            iqbd[64 * half:64 * half + 64, off:off + 160 * (PAIRS - 1) + 1:160],
                            ps[src, new], rms[src, new], mul))
                for e in range(2):
                    src = slice(64 * e, 64 * e + 64)
                    ins = nc.vector.tensor_tensor(iq[:, 2 * (t % 2) + e, :], ps[src, 0:T], rms[src, :], mul)
                    if e:
                        ins.then_inc(iq_ready, 1)
                    else:
                        st.then(ins)
                dve.wait_ge(iq_ready, t + 1)

            def index_sum(h):
                dve.wait_ge(relu_ready, h + 1)
                for n, (q0, nq, nk) in enumerate(QT):
                    acc = S[0:nq, S_AT[n]:S_AT[n] + nk]
                    ins = nc.vector.scalar_tensor_tensor(
                        acc, relu[0:nq, h % 2, A_AT[n]:A_AT[n] + nk], iwq[0:nq, 16 * n + h:16 * n + h + 1], acc,
                        ALU.mult, ALU.add)
                    if n < 2:
                        st.then(ins)
                    else:
                        ins.then_inc(relu_used, 1)
                dve.wait_ge(relu_used, h + 1)

            for t in range(8):
                if t + 1 < 8:
                    lo_chunk(dve, nc.vector, lo_dve, 0, C_IQ + 2 * t + 2)
                    lo_chunk(dve, nc.vector, lo_dve, 0, C_IQ + 2 * t + 3)
                if t >= 2:
                    index_sum(2 * t - 4)
                    index_sum(2 * t - 3)
                index_queries(t)
            for h in range(12, 16):
                index_sum(h)

            def prompt_round(n):
                for q, (q0, nq, nk) in enumerate(QT):
                    src = (S if n == 0 else W)[0:nq, S_AT[q]:S_AT[q] + nk + SENT]
                    st.then(nc.vector.max(top8[0:nq, q, :], src))
                st.wait()
                for q, (q0, nq, nk) in enumerate(QT):
                    src = (S if n == 0 else W)[0:nq, S_AT[q]:S_AT[q] + nk + SENT]
                    st.then(nc.vector.match_replace(W[0:nq, S_AT[q]:S_AT[q] + nk + SENT], top8[0:nq, q, :], src, NEG))
                st.wait()

            def sample_round(n):
                src = (Ss if n == 0 else Ws)[:, :]
                st.link(nc.vector.max(top8s[:, :], src))
                st.link(nc.vector.match_replace(Ws[:, :], top8s[:, :], src, NEG))

            def tile_ready(t):
                dve.wait_ge(chunk_used, C_PROJ + 2 * t + 2)
                return bank[(T_PROJ + t) % 2]

            ROUNDS_P = (TOPK_P + SENT) // 8
            ROUNDS_S = TOPK_S // 8
            rounds_s = iter(range(ROUNDS_S))
            rounds_p = iter(range(ROUNDS_P))
            for t in range(U0, U0 + 8):
                prompt_round(next(rounds_p))
                if t == 7:
                    for n in rounds_p:
                        prompt_round(n)
                ps = tile_ready(t)
                nc.vector.tensor_tensor(U[:, t, POOL_BUF:POOL_BUF + T], ps[:, 0:T], rms[:, :],
                                        mul).then_inc(tile_freed, 1)
                if t == 1:
                    dve.wait_ge(ssum_done, 1)
                    st.then(nc.vector.tensor_copy(Ss[:, 0:512], bank[2][0:DB, :]))
                    st.then(nc.vector.tensor_copy(Ss[:, 512:1024], bank[3][0:DB, :]))
                    st.link(nc.vector.tensor_copy(Ss[:, 1024:1025], misc[0:DB, 0:1]))
                if t >= 2:
                    sample_round(next(rounds_s))
            dve.wait_ge(tile_freed, 9)
            for q, (q0, nq, nk) in enumerate(QT):
                sl = slice(S_AT[q], S_AT[q] + nk)
                st.link(nc.vector.tensor_tensor(W[0:nq, sl], S[0:nq, sl], W[0:nq, sl], ALU.not_equal))
                st.link(nc.vector.tensor_scalar(W[0:nq, sl], W[0:nq, sl], -1.0, -MASKED, ALU.add, ALU.mult))

            def pool_group(g):
                w = WINDOWS[g]
                u = U[:, 2 * g:2 * g + 2, :]
                src, step, n = u, 1, 0
                while step < w:
                    dst = win[n % 2]
                    st.link(nc.vector.tensor_tensor(dst[:, :, 2 * step - 1:UW], src[:, :, 2 * step - 1:UW],
                                                    src[:, :, step - 1:UW - step], ALU.add))
                    src, step, n = dst, 2 * step, n + 1
                d = diff[:, 2 * g:2 * g + 2, :]
                inv = con[:, INV + 16 * g:INV + 16 * g + 16].unsqueeze(1).broadcast_to([P, 2, 16])
                st.link(nc.vector.tensor_tensor(win[2][:, :, 0:16], src[:, :, POOL_BUF:POOL_BUF + 16], inv, mul))
                st.then(nc.vector.tensor_tensor(d[:, :, 0:16], win[2][:, :, 0:16], u[:, :, POOL_BUF:POOL_BUF + 16],
                                                ALU.subtract))
                st.link(nc.vector.scalar_tensor_tensor(d[:, :, 16:TP], src[:, :, POOL_BUF + 16:UW], 1.0 / w,
                                                       u[:, :, POOL_BUF + 16:UW], ALU.mult, ALU.subtract))
                s = win[2][:, :, 16:16 + DB]
                un = u[:, :, POOL_BUF + TP:POOL_BUF + T]
                st.link(nc.vector.tensor_reduce(s, poolst[:, 2 * g:2 * g + 2, :, POOL_BUF - (w - 1):POOL_BUF],
                                                AX.X, ALU.add))
                st.link(nc.vector.tensor_tensor(s, s, un, ALU.add))
                nc.vector.scalar_tensor_tensor(d[:, :, TP:T], s, 1.0 / w, un, ALU.mult,
                                               ALU.subtract).then_inc(diff_ready, 1)
                dve.wait_ge(diff_ready, g + 1)

            dve.wait_ge(poolw_loaded, 32)
            for t in range(K0, K0 + 4):
                ps = tile_ready(t)
                dst = kT[:, t - K0, :] if t < V0 else vT[:, t - V0, :]
                ins = nc.vector.tensor_tensor(dst, ps[:, 0:T], rms[:, :], mul)
                ins.then_inc(tile_freed, 1)
                pool_group(t - K0)
            for t in range(Q0, Q0 + HEADS):
                h = t - Q0
                sample_round(next(rounds_s))
                sample_round(next(rounds_s))
                ps = tile_ready(t)
                off = (h // 4) * 64 + h
                st.then(nc.vector.tensor_tensor(qbd[:, off:off + 136 * (DB - 1) + 1:136], ps[:, TP:T],
                                                rms[:, TP:T], mul))
                st.then(nc.vector.tensor_tensor(qnew[:, off:off + 8 * (DB - 1) + 1:8], ps[:, TP:T],
                                                rms[:, TP:T], mul))
                nc.vector.tensor_tensor(qT[:, h, 0:TP], ps[:, 0:TP], rms[:, 0:TP], mul).then_inc(tile_freed, 1)

            for j in range(8):
                dve.wait_ge(pmix_hi, j + 1)
                nc.vector.scalar_tensor_tensor(h_lo[:, HEADS + j, L:], bank[2 + j % 4][:, L:T],
                                               par[:, PSC + j:PSC + j + 1], h_hi[:, HEADS + j, L:].bitcast(F32),
                                               ALU.mult, ALU.subtract).then_inc(pmix_lo, 1)
            dve.wait_ge(pmix_lo, 8)

            SCALE = float(HD) ** -0.5

            def w_o_pool(j):
                dve.wait_ge(chunk_used, C_WOP + j + 1)
                nc.vector.tensor_copy(part[:, j, L:], bank[(T_WOP + j) % 2][:, L:T]).then_inc(tile_freed, 1)

            def masked_scores(h):
                dve.wait_ge(score_done, h + 1)
                if h >= 2:
                    dve.wait_ge(probT_done, h - 1)
                for n, (q0, nq, nk) in enumerate(QT):
                    src = bank[2][0:nq, A_AT[n]:A_AT[n] + nk] if n < 2 else bank[3][0:nq, 0:nk]
                    st.then(nc.vector.tensor_tensor_reduce(
                        prob[0:nq, h % 2, A_AT[n]:A_AT[n] + nk], src, W[0:nq, S_AT[n]:S_AT[n] + nk], 1.0, -BIG,
                        ALU.add, ALU.max, mx[0:nq, n:n + 1]))
                st.wait()
                st.then(nc.vector.tensor_scalar(nmx[:, 0:2], mx[:, 0:2], -SCALE, None, ALU.mult))
                nc.vector.tensor_scalar(nmx[0:16, 2:3], mx[0:16, 2:3], -SCALE, None, ALU.mult).then_inc(soft_in, 1)

            def head_low(h):
                dve.wait_ge(o_hi, h + 1)
                nc.vector.tensor_tensor(h_lo[:, h, L:TP], bank[5][:, L:TP], h_hi[:, h, L:TP].bitcast(F32),
                                        ALU.subtract).then_inc(o_lo, 1)

            masked_scores(0)
            for h in range(HEADS):
                p = h % 2
                dve.wait_ge(exp_done, 3 * h + 3)
                st.link(nc.vector.reciprocal(rden[:, :], den[:, :]))
                for n, (q0, nq, nk) in enumerate(QT):
                    sl = prob[0:nq, p, A_AT[n]:A_AT[n] + nk]
                    nc.vector.tensor_scalar(sl, sl, rden[0:nq, n:n + 1], None, ALU.mult).then_inc(prob_ready, 1)
                dve.wait_ge(prob_ready, 3 * h + 3)
                w_o_pool(h)
                if h + 1 < HEADS:
                    masked_scores(h + 1)
                    for n in range(2 if h < 4 else 1):
                        left = next(rounds_s, None)
                        if left is not None:
                            sample_round(left)
                    if h == HEADS - 2:
                        st.link(nc.vector.tensor_tensor(Ws[:, :], Ss[:, :], Ws[:, :], ALU.not_equal))
                        nc.vector.tensor_scalar(Ws[:, :], Ws[:, :], -1.0, -MASKED, ALU.add,
                                                ALU.mult).then_inc(smask_ready, 1)
                    head_low(h)
            assert next(rounds_s, None) is None
            dve.wait_ge(sscore_done, 1)
            st.then(nc.vector.reduce_max(mxs[:, 0:1], bank[6][0:64, :], AX.X))
            st.then(nc.vector.reduce_max(mxs[:, 1:2], bank[7][0:64, :], AX.X))
            st.link(nc.vector.tensor_tensor(pnm[:, :], bank[2][0:64, 0:DB], con[0:64, M64:M64 + DB], mul))
            st.link(nc.vector.reduce_sum(mxs[:, 2:3], pnm[:, :], AX.X))
            st.link(nc.vector.tensor_tensor(mxs[:, 2:3], mxs[:, 2:3], bank[2][0:64, DB:DB + 1], ALU.add))
            st.link(nc.vector.reduce_max(mxs[:, 3:4], mxs[:, 0:3], AX.X))
            nc.vector.tensor_scalar(mxs[:, 4:5], mxs[:, 3:4], -SCALE, None, ALU.mult).then_inc(ssoft_in, 1)
            w_o_pool(8)
            dve.wait_ge(sexp_done, 3)
            st.link(nc.vector.reduce_sum(dens[:, 3:4], dens[:, 0:3], AX.X))
            st.link(nc.vector.reciprocal(dens[:, 4:5], dens[:, 3:4]))
            st.link(nc.vector.tensor_scalar(probs, probs, dens[:, 4:5], None, ALU.mult))
            nc.vector.tensor_scalar(pnm[:, :], con[0:64, M64:M64 + DB], probs[:, 1024:1025], None,
                                    ALU.mult).then_inc(sprob_ready, 1)
            head_low(HEADS - 1)
            w_o_pool(9)
            dve.wait_ge(sprobT_done, 1)
            nc.vector.tensor_copy(pnew[:, :], bank[5][0:DB, 0:64]).then_inc(sprobT_dve, 1)
            w_o_pool(10)
            for n in range(2):
                w_o_pool(11 + 2 * n)
                dve.wait_ge(spv_done, 2 * n + 2)
                nc.vector.tensor_copy(outs[:, 4 * n + 2:4 * n + 4, :], bank[6 + n][0:HEADS, :].rearrange(
                    "h (b e) -> h b e", b=2)).then_inc(outs_dve, 1)
                w_o_pool(12 + 2 * n)
            dve.wait_ge(so_hi, KV)
            for g in range(KV):
                nc.vector.tensor_tensor(h_lo[:, 4 * g:4 * g + 4, TP:T], out_by_head(g),
                                        h_hi[:, 4 * g:4 * g + 4, TP:T].bitcast(F32),
                                        ALU.subtract).then_inc(so_lo, 1)
            w_o_pool(15)
            st.link(nc.vector.memset(sumsq[:, :], 0.0))

            def conv_state():
                dve.wait_ge(cst_loaded, 32)
                for i in range(2):
                    wi = par[:, CWT + i * 2 * FT:CWT + (i + 1) * 2 * FT].unsqueeze(2).broadcast_to([P, 2 * FT, DB])
                    st.link(nc.vector.tensor_tensor(cst[:, i], cst[:, i], wi, mul))
                st.link(nc.vector.tensor_tensor(cst[:, 0], cst[:, 0], cst[:, 1], ALU.add))

            def add_squares(n, slot):
                dve.wait_ge(sq_ready, n)
                nc.vector.tensor_tensor(sumsq[:, L:], sumsq[:, L:], sq[:, slot, L:], ALU.add).then_inc(sq_used, 1)
                dve.wait_ge(sq_used, n - 1)

            for j in range(KM):
                dve.wait_ge(chunk_used, C_WOA + j + 1)
                nc.vector.tensor_tensor(part[:, j, L:], bank[(T_WOA + j) % 2][:, L:T], part[:, j, L:],
                                        ALU.add).then_inc(o_ready, 1)
                if j:
                    add_squares(KM + j, (j - 1) % 2)
                if j == 10:
                    conv_state()
                if j in (13, 15):
                    lo_chunk(dve, nc.vector, lo_dve, 0, C_UP + j - 12)
            dve.wait_ge(o_ready, KM)
            add_squares(2 * KM, (KM - 1) % 2)
            inv_rms(2, L)

            def residual(o, k, g, first, done):
                nc.vector.scalar_tensor_tensor(o, o, par[:, g + k:g + k + 1], rms[:, first:],
                                               ALU.mult, ALU.mult).then_inc(done, 1)

            def stage_hi_lo(k):
                dve.wait_ge(h_hi_ready, KM + k + 1)
                nc.vector.scalar_tensor_tensor(h_lo[:, k, L:], x1[:, k, L:], par[:, G3 + k:G3 + k + 1],
                                               h_hi[:, k, L:].bitcast(F32), ALU.mult,
                                               ALU.subtract).then_inc(h_lo_ready, 1)

            for k in range(KM):
                residual(part[:, k, L:], k, G2, L, o_scaled)
                if k >= 2:
                    stage_hi_lo(k - 2)
            stage_hi_lo(KM - 2)
            stage_hi_lo(KM - 1)
            inv_rms(3, L)

            def scaled_up(r, p, v):
                f = 2 * r + v
                dve.wait_ge(chunk_used, C_UP + 4 * r + 2 * v + 2)
                nc.vector.tensor_tensor(up[:, p, v, :], bank[(T_UP + v) % 2][:, L:T], rms[:, L:],
                                        mul).then_inc(up_ready, 1)
                dve.wait_ge(up_ready, f + 1)
                st.then(nc.vector.tensor_copy(uplast[:, bass.ds(f, 1), :],
                                              up[:, p, v:v + 1, SEQ:TU]))

            def conv_taps(r, v, p):
                f = 2 * r + v
                dve.wait_ge(act_ready, f + 1)
                for i in range(2):
                    st.link(nc.vector.scalar_tensor_tensor(
                        act[:, v, 0:SEQ], up[:, p, v, i:i + SEQ], par[:, bass.ds(CWT + 2 * FT * i + f, 1)],
                        act[:, v, 0:SEQ], ALU.mult, ALU.add))
                ins = nc.vector.tensor_tensor(act[:, v:v + 1, SEQ:], act[:, v:v + 1, SEQ:],
                                              cst[:, 0, bass.ds(f, 1), :], ALU.add)
                if v:
                    st.link(ins)
                else:
                    ins.then_inc(conv_ready, 1)

            def gated(r, p):
                conv_taps(r, 1, p)
                dve.wait_ge(silu_ready, r + 1)
                nc.vector.tensor_tensor(act[:, 0, :], act[:, 0, :], act[:, 1, :], mul).then_inc(gate_ready, 1)
                dve.wait_ge(g_hi_ready, r + 1)
                nc.vector.tensor_tensor(g_lo[:, bass.ds(r, 1), :], act[:, 0:1, :],
                                        g_hi[:, bass.ds(r, 1), :].bitcast(F32),
                                        ALU.subtract).then_inc(g_lo_ready, 1)

            def ffn_pair(r, p, last=False, first=False):
                widths = [down_width(C_DOWN + j) if last else CW for j in range(4)]
                if not first:
                    gated(r - 1, 1 - p)
                scaled_up(r, p, 0)
                conv_taps(r, 0, p)
                lo_chunk(dve, nc.vector, lo_dve, r, C_UP + 5, widths[1])
                scaled_up(r, p, 1)
                lo_chunk(dve, nc.vector, lo_dve, r, C_UP + 7, widths[3])

            STEPS_PER_PAIR = 7
            ffn_pair(0, 0, first=True)
            n0 = st.n
            with dve.Fori(0, FT // 2 - 1) as i:
                st.turn = 2 * STEPS_PER_PAIR * i
                ffn_pair(2 * i + 1, 1)
                ffn_pair(2 * i + 2, 0)
            assert st.n - n0 == 2 * STEPS_PER_PAIR, st.n - n0
            st.turn = 0
            st.n = n0 + (FT - 2) * STEPS_PER_PAIR
            ffn_pair(FT - 1, 1, last=True)
            gated(FT - 1, 1)
            st.link(nc.vector.memset(sumsq[:, :], 0.0))
            dve.wait_ge(x2_loaded, 16)

            def down_out(i, t, r, tail=False, head=False):
                for j in (1, 3, 5):
                    cj = C_DOWN + RING + 6 * t + j
                    if not (tail and t == 1 and j >= 3):
                        lo_chunk(dve, nc.vector, lo_dve, r, cj, down_width(cj))
                n = 2 * i + t
                dve.wait_ge(chunk_used, 4 * r + C_DOWN + 6 * (t + 1))
                nc.vector.tensor_copy(o2[:, bass.ds(n, 1), :],
                                      bank[(T_DOWN + t) % 2][:, N_META:T].unsqueeze(1)).then_inc(o_ready, 1)
                dve.wait_ge(sq_ready, 3 * KM + n + 1)
                nc.vector.tensor_tensor(sumsq[:, N_META:], sumsq[:, N_META:], sq[:, t, N_META:], ALU.add).then_inc(sq_used, 1)
                dve.wait_ge(sq_used, 3 * KM + n - 1)

            with dve.Fori(0, KM // 2 - 1) as i:
                down_out(i, 0, 3 * i)
                down_out(i, 1, 3 * i)
            down_out(KM // 2 - 1, 0, 3 * (KM // 2 - 1), tail=True)
            down_out(KM // 2 - 1, 1, 3 * (KM // 2 - 1), tail=True)
            inv_rms(4, N_META)
            for k in range(KM):
                residual(o2[:, k, :], k, G4, N_META, o_scaled)
                if k not in Y_POOL:
                    dve.wait_ge(o_scaled, KM + k + 1)
                    nc.vector.tensor_tensor(o2[:, k, :], x2[:, k, :], o2[:, k, :], ALU.add).then_inc(y_ready, 1)

        @block.tensor
        def _(pe):
            mm = nc.tensor.matmul

            def stream_tile(r, cjs, kts, x_hi, x_lo, out, first=0, ready=None):
                total, done = sum(len(k) for k in kts), 0
                for cj, ks in zip(cjs, kts):
                    lo_wait(pe, r, cj)
                    s = cj % RING
                    for i, k in enumerate(ks):
                        if ready:
                            pe.wait_ge(ready, done + 1)
                        w_hi = hi[:, s, i * P:(i + 1) * P]
                        w_lo = lo[:, s, i * P:(i + 1) * P]
                        mm(out, w_hi, x_hi[:, k, first:], start=(done == 0), stop=False)
                        mm(out, w_hi, x_lo[:, k, first:], start=False, stop=False)
                        done += 1
                        last = mm(out, w_lo, x_hi[:, k, first:], start=False, stop=(done == total))
                    last.then_inc(chunk_used, 1)

            def tile_free(n):
                if isinstance(n, int) and n < 2:
                    return
                pe.wait_ge(tile_freed, n - 1)

            HALF = [list(range(8)), list(range(8, 16))]
            out = bank[0][0:IKW, 0:T]
            pe.wait_ge(con_loaded, 16)
            for k in range(KM):
                if k % 8 == 0:
                    lo_wait(pe, 0, C_IK + k // 8)
                pe.wait_ge(h_lo_ready, k + 1)
                s, i = k // 8, k % 8
                w_hi, w_lo = (w[:, s, i * IKW:(i + 1) * IKW] for w in (hi, lo))
                mm(out, w_hi, h_hi[:, k, :], start=(k == 0), stop=False)
                mm(out, w_hi, h_lo[:, k, :], start=False, stop=False)
                last = mm(out, w_lo, h_hi[:, k, :], start=False, stop=(k == KM - 1))
                if i == 7:
                    last.then_inc(chunk_used, 1)
                pe.wait_ge(sq_ready, k + 1)
                ins = mm(misc[:, 0:T], con[:, ONE:ONE + P], sq[:, k % 2, :], start=(k == 0), stop=(k == KM - 1))
                if k < KM - 1:
                    ins.then_inc(sq_used, 1)
                else:
                    ins.then_inc(sum_ready, 1)

            def q_idx_tile(r, t, p):
                stream_tile(r, [C_IQ + 2 * t, C_IQ + 2 * t + 1], HALF, h_hi, h_lo,
                            bank[(T_IQ + t) % 2][:, 0:T])

            def index_scores(h, p, e):
                if not isinstance(h, int) or h >= 2:
                    pe.wait_ge(relu_ready, h - 1)
                for n, (q0, nq, nk) in enumerate(QT):
                    o = bank[2 + 2 * e][0:nq, A_AT[n]:A_AT[n] + nk] if n < 2 else bank[3 + 2 * e][0:nq, 0:nk]
                    last = mm(o, iq[:, 2 * p + e, q0:q0 + nq], ikT[:, 0:nk], start=True, stop=True)
                last.then_inc(iq_used, 1)

            q_idx_tile(0, 0, 0)
            pe.wait_ge(tile_freed, 1)
            ident = con[:, IDN:IDN + P]
            nc.tensor.transpose(misc[:, 0:16], iwT[:, 0:128], con[0:16, IDN:IDN + 16])
            nc.tensor.transpose(misc[:, 16:32], iwT[:, 128:256], con[0:16, IDN:IDN + 16])
            nc.tensor.transpose(misc[0:16, 32:48], iwT[:, 256:272], con[0:16, IDN:IDN + 16])
            mm(misc[:, 64:72], con[0:16, HREP:HREP + P], iwT[:, TP:T], start=True, stop=True).then_inc(iw_ready, 1)

            def q_idx_pair(r, n):
                for t in (1, 2):
                    if isinstance(n, int) and 2 * n + t == 1:
                        pass
                    else:
                        pe.wait_ge(iq_ready, 2 * n + t - 1)
                    q_idx_tile(r, t, t % 2)
                    pe.wait_ge(iq_ready, 2 * n + t)
                    for e in range(2):
                        index_scores(4 * n + 2 * (t - 1) + e, (t - 1) % 2, e)

            q_idx_pair(0, 0)
            with pe.Fori(1, 3) as i:
                q_idx_pair(i, i)
            pe.wait_ge(iq_ready, 6)
            q_idx_tile(0, 7, 1)
            for t in (6, 7):
                pe.wait_ge(iq_ready, t + 1)
                for e in range(2):
                    index_scores(2 * t + e, t % 2, e)
            pe.wait_ge(relu_ready, 16)
            pe.wait_ge(kidx_loaded, 16 * PAIRS * PAGES)
            for b in range(PAIRS):
                w = iqbd[:, b * P:(b + 1) * P]
                f, l = b == 0, b == PAIRS - 1
                mm(bank[4][:, :], w, kidx[:, b, 0:512], start=f, stop=l)
                mm(bank[5][:, :], w, kidx[:, b, 512:1024], start=f, stop=l)
                last = mm(bank[6][:, 0:1], w, iknew[:, b:b + 1], start=f, stop=l)
            last.then_inc(sidx_done, 1)

            def proj_tile(r, t, n):
                if isinstance(n, int) and n < T_PROJ + 2:
                    pe.wait_ge(iq_ready, n - 2)
                else:
                    pe.wait_ge(tile_freed, n - T_PROJ)
                stream_tile(r, [C_PROJ + 2 * t, C_PROJ + 2 * t + 1], HALF, h_hi, h_lo,
                            bank[(T_PROJ + t) % 2][:, 0:T])

            proj_tile(0, 0, T_PROJ)
            pe.wait_ge(srelu_done, 3)
            mm(bank[2][0:DB, :], iwblk[:, :], relus[:, 0:512], start=True, stop=True)
            mm(bank[3][0:DB, :], iwblk[:, :], relus[:, 512:1024], start=True, stop=True)
            mm(misc[0:DB, 0:1], iwblk[:, :], relus[:, 1024:1025], start=True, stop=True).then_inc(ssum_done, 1)
            proj_tile(0, 1, T_PROJ + 1)
            with pe.Fori(0, 8) as i:
                proj_tile(i, 2, 2 * i + T_PROJ + 2)
                proj_tile(i, 3, 2 * i + T_PROJ + 3)
            for g in range(KV):
                nc.tensor.transpose(bank[6][:, g * 128:g * 128 + 128], vT[:, g, 0:128], ident)
                nc.tensor.transpose(bank[6][:, 256 + g * 128:384 + g * 128], vT[:, g, 128:256], ident)
                nc.tensor.transpose(misc[0:16, g * 128:g * 128 + 128], vT[:, g, 256:272], ident)
                last = nc.tensor.transpose(misc[0:DB, 256 + g * 128:384 + g * 128], vT[:, g, TP:T], ident)
            last.then_inc(vt_done, 1)
            proj_tile(0, 18, T_PROJ + 18)
            proj_tile(0, 19, T_PROJ + 19)
            pe.wait_ge(diff_ready, 4)
            for j in range(8):
                g = j // 2
                if j >= 4:
                    pe.wait_ge(pmix_lo, j - 3)
                for k in range(2):
                    last = mm(bank[2 + j % 4][:, L:T], poolw[:, g, k, (j % 2) * P:(j % 2 + 1) * P],
                              diff[:, 2 * g + k, L:], start=(k == 0), stop=(k == 1))
                last.then_inc(pmix_done, 1)

            def w_o_tile(j, ready=None):
                pe.wait_ge(tile_freed, 20 + j)
                stream_tile(0, [C_WOP + j], [HALF[1]], h_hi, h_lo, bank[(T_WOP + j) % 2][:, L:T], L, ready)

            def attention_scores(h):
                if h:
                    pe.wait_ge(soft_in, h)
                g = h // (HEADS // KV)
                for n, (q0, nq, nk) in enumerate(QT):
                    o = bank[2][0:nq, A_AT[n]:A_AT[n] + nk] if n < 2 else bank[3][0:nq, 0:nk]
                    last = mm(o, qT[:, h, q0:q0 + nq], kT[:, g, 0:nk], start=True, stop=True)
                last.then_inc(score_done, 1)

            def sample_scores(b):
                pe.wait_ge(k_loaded[b % 2], 16 * (b // 2 + 1))
                for g in range(KV):
                    w = qbd[:, (2 * b + g) * 64:(2 * b + g) * 64 + 64]
                    f = b == 0 and g == 0
                    for c in range(2):
                        last = mm(bank[6 + c][0:64, :], w,
                                  kring[:, b % 2, 4 * c:4 * c + 4, g * PAGE:(g + 1) * PAGE], start=f, stop=False)
                last.then_inc(kq_used, 1)

            def sample_mask():
                for g in range(KV):
                    mm(bank[2][0:64, 0:DB], qnew[:, 64 * g:64 * g + 64], kT[:, g, TP:T], start=(g == 0), stop=(g == 1))
                pe.wait_ge(smask_ready, 1)
                e8 = con[0:DB, EXP8:EXP8 + 64]
                mm(bank[6][0:64, :], e8, Ws[:, 0:512], start=False, stop=True)
                mm(bank[7][0:64, :], e8, Ws[:, 512:1024], start=False, stop=True)
                mm(bank[2][0:64, DB:DB + 1], e8, Ws[:, 1024:1025], start=True, stop=True).then_inc(sscore_done, 1)

            def sample_values(b):
                pe.wait_ge(v_loaded[b % 4], 16 * (b // 4 + 1))
                o = bank[(2, 6, 3, 7)[b // 2]][0:HEADS, (b % 2) * 256:(b % 2) * 256 + 256]
                cols = slice(HEADS * b, HEADS * b + HEADS)
                mm(o, pnew[:, cols], vnew[:, :], start=True, stop=False)
                for n in range(PAGES):
                    last = mm(o, probsT[:, n, cols], v_slot(b)[:, n, :], start=False, stop=(n == PAGES - 1))
                last.then_inc(vq_used if b % 2 == 0 else spv_done, 1)

            pe.wait_ge(tile_freed, 21)
            pe.wait_ge(pmix_lo, 6)
            attention_scores(0)
            w_o_tile(0, pmix_lo)
            pe.wait_ge(vrow_ready, 4)
            sample_scores(0)
            for h in range(HEADS):
                p, g = h % 2, h // (HEADS // KV)
                if h:
                    w_o_tile(h)
                pe.wait_ge(prob_ready, 3 * h + 3)
                if h:
                    pe.wait_ge(probT_ready, 2 * h)
                tr = nc.tensor.transpose
                for n, (q0, nq, nk) in enumerate(QT):
                    tr(bank[4][:, q0:q0 + nq], prob[0:nq, p, A_AT[n]:A_AT[n] + 128], con[0:nq, IDN:IDN + nq])
                for n in (1, 2):
                    q0, nq, nk = QT[n]
                    tr(bank[4][:, TP + q0 - 128:TP + q0 - 128 + nq],
                       prob[0:nq, p, A_AT[n] + 128:A_AT[n] + 256], con[0:nq, IDN:IDN + nq])
                tr(bank[4][0:16, 416:432], prob[0:16, p, A_AT[2] + 256:A_AT[2] + 272],
                   con[0:16, IDN:IDN + 16]).then_inc(probT_done, 1)
                if h + 1 < HEADS:
                    attention_scores(h + 1)
                    sample_scores(h + 1)
                else:
                    sample_mask()
                    w_o_tile(8)
                pe.wait_ge(probT_ready, 2 * h + 2)
                if h:
                    pe.wait_ge(o_lo, h)
                vg = slice(g * HD, (g + 1) * HD)
                mm(bank[5][:, L:TP], vrow[:, 0, vg], probT[:, p, L:TP], start=True, stop=False)
                mm(bank[5][:, 128:TP], vrow[:, 1, vg], probT[:, p, TP:TP + 144], start=False, stop=False)
                mm(bank[5][:, 256:TP], vrow[0:16, 2, vg], probT[0:16, p, 416:432], start=False,
                   stop=True).then_inc(pv_done, 1)
            w_o_tile(9)
            pe.wait_ge(sprob_ready, 1)
            for g in range(PAGES):
                nc.tensor.transpose(bank[4][:, 64 * g:64 * g + 64], probs[:, g * 128:g * 128 + 128],
                                    con[0:64, IDN:IDN + 64])
            pe.wait_ge(o_lo, HEADS)
            nc.tensor.transpose(bank[5][0:DB, 0:64], pnm[:, :], con[0:64, IDN:IDN + 64]).then_inc(sprobT_done, 1)
            w_o_tile(10)
            pe.wait_ge(sprobT_act, 1)
            pe.wait_ge(sprobT_dve, 1)
            for n in range(4):
                sample_values(2 * n)
                sample_values(2 * n + 1)
                w_o_tile(11 + n)
            for b in range(DB):
                pe.wait_ge(outs_act if b % 4 < 2 else outs_dve, b // 4 + 1)
                for g in range(KV):
                    at = (2 * b + g) * HEADS
                    last = nc.tensor.transpose(bank[4][:, at:at + HEADS], outs[:, b, g * HD:(g + 1) * HD],
                                               con[0:HEADS, IDN:IDN + HEADS])
            last.then_inc(outT_done, 1)
            w_o_tile(15)
            pe.wait_ge(so_lo, 2)
            for j in range(KM):
                if j < 2:
                    pe.wait_ge(tile_freed, 36 + j)
                else:
                    pe.wait_ge(o_ready, j - 1)
                stream_tile(0, [C_WOA + j], [HALF[0]], h_hi, h_lo, bank[(T_WOA + j) % 2][:, L:T], L)

            def total(n, used, first):
                pe.wait_ge(sq_used, used)
                mm(misc[:, first:T], con[:, ONE:ONE + P], sumsq[:, first:], start=True, stop=True).then_inc(sum_ready, 1)

            total(2, 2 * KM - 1, L)
            pe.wait_ge(o_ready, KM)
            out = bank[T_UP % 2][:, L:T]
            for k in range(KM):
                if k % 8 == 0:
                    lo_wait(pe, 0, C_UP + k // 8)
                pe.wait_ge(h_lo_ready, KM + k + 1)
                s, i = (C_UP + k // 8) % RING, k % 8
                w_hi, w_lo = (w[:, s, i * P:(i + 1) * P] for w in (hi, lo))
                mm(out, w_hi, h_hi[:, k, L:], start=(k == 0), stop=False)
                mm(out, w_hi, h_lo[:, k, L:], start=False, stop=False)
                last = mm(out, w_lo, h_hi[:, k, L:], start=False, stop=(k == KM - 1))
                if i == 7:
                    last.then_inc(chunk_used, 1)
                pe.wait_ge(sq_ready, 2 * KM + k + 1)
                ins = mm(misc[:, L:T], con[:, ONE:ONE + P], sq[:, k % 2, L:], start=(k == 0), stop=(k == KM - 1))
                if k < KM - 1:
                    ins.then_inc(sq_used, 1)
                else:
                    ins.then_inc(sum_ready, 1)

            def up_tile(r, v):
                if not (isinstance(r, int) and r == 0):
                    pe.wait_ge(up_ready, 2 * r + v - 1)
                stream_tile(r, [C_UP + 2 * v, C_UP + 2 * v + 1], HALF, h_hi, h_lo,
                            bank[(T_UP + v) % 2][:, L:T], L)

            up_tile(0, 1)
            with pe.Fori(1, FT) as i:
                up_tile(i, 0)
                up_tile(i, 1)
            pe.wait_ge(g_lo_ready, FT)
            KD = [list(range(DOWN_CUT[j], DOWN_CUT[j + 1])) for j in range(6)]

            def down_tile(r, i, t):
                if isinstance(i, int) and i == 0:
                    pe.wait_ge(up_ready, 2 * FT - 1 + t)
                else:
                    pe.wait_ge(o_ready, 2 * i + t + KM - 1)
                stream_tile(r, [C_DOWN + 6 * t + j for j in range(6)], KD, g_hi, g_lo,
                            bank[(T_DOWN + t) % 2][:, N_META:T])

            down_tile(0, 0, 0)
            down_tile(0, 0, 1)
            with pe.Fori(1, KM // 2) as i:
                down_tile(3 * i, i, 0)
                down_tile(3 * i, i, 1)
            total(4, 4 * KM - 2, N_META)
    ctx.close()


_OUTS = {
    "y": (P, KM, TG), "k": (P, KV, T), "v": (P, KV, T), "ik": (IDX_DIM, T), "u": (P, 8, T),
    "uplast": (P, 2 * FT, 2 + DB), "old_pool": (DB, POOL_BUF - 1, POOL_WIDTH), "old_conv": (DB, 1, 2 * D_FF),
}


def kernel(**inputs):
    import concourse.bacc as bacc
    from concourse.bass_utils import run_bass_kernel_spmd

    f = {n: np.asarray(v) for n, v in inputs.items()}

    def tiles(w, cols):
        k, n = w.shape
        return np.ascontiguousarray(
            w.reshape(k // P, P, n // cols, cols).transpose(2, 1, 0, 3)).reshape(n // cols, P, -1)

    def features(x):
        n = x.shape[-1]
        x = np.moveaxis(x, -1, 0)
        return np.ascontiguousarray(np.moveaxis(x.reshape((n // P, P) + x.shape[1:]), 1, 0))

    def pairs(x):
        s = x.shape[:-1]
        return np.moveaxis(x.reshape(s + (2, FT, P)), -3, -2).reshape(s + (2 * D_FF,))

    w_in = f["w_in"][0]
    q_end, k_end = HEADS * HD, HEADS * HD + KV * HD
    v_end = k_end + KV * HD
    iq_end = v_end + IDX_HEADS * IDX_DIM
    iw_end = iq_end + IKW
    w_main = np.concatenate([w_in[:, v_end:iq_end], w_in[:, iw_end:], w_in[:, q_end:v_end], w_in[:, :q_end]], 1)
    x = np.concatenate([f["meta_tokens"], f["x_prompt"][0], f["x_sample"][:, 0]], 0)
    par = [features(f[n][0]) for n in ("g_mix_pre", "g_mix_post", "g_ffn_pre", "g_ffn_post", "pool_scale")]
    par += [features(pairs(f["conv_w"][0])[i]) for i in range(3)] + [features(pairs(f["conv_b"][0]))]
    con, causal = shape_constants()
    n_pool = f["cache_k"].shape[1]
    table = np.ascontiguousarray(f["page_table"]).astype(np.int32, copy=False)
    state_conv = features(pairs(f["state_conv"][0]))
    arrays = {
        "x": features(x), "par": np.concatenate(par, 1), "con": con, "causal": causal,
        "w_ik": tiles(w_in[:, iq_end:iw_end], IKW)[0], "w_in": tiles(w_main, P), "w_o": tiles(f["w_o"][0], P),
        "w_up": tiles(pairs(f["w_up"][0]), P), "w_down": tiles(f["w_down"][0], P),
        "pool_w": np.ascontiguousarray(
            f["pool_w"][0].reshape(4, 2, P, 256).transpose(2, 0, 1, 3)).reshape(P, -1),
        "state_pool": features(f["state_pool"][0]).reshape(P, -1),
        "state_conv": np.ascontiguousarray(state_conv.transpose(0, 3, 1, 2)),
        "state_pool_rows": np.ascontiguousarray(f["state_pool"][0][:, 1:]),
        "state_conv_rows": np.ascontiguousarray(f["state_conv"][0][:, 1:]),
        "cache_k": np.ascontiguousarray(f["cache_k"][0].transpose(0, 3, 2, 1)).reshape(n_pool, P, KV * PAGE),
        "cache_v": f["cache_v"][0].reshape(n_pool, PAGE, KV * HD),
        "cache_kidx": np.ascontiguousarray(f["cache_kidx"][0].transpose(0, 2, 1)).reshape(n_pool * IDX_DIM, PAGE),
        "pages": table.reshape(1, -1),
        "pages_even": np.ascontiguousarray(table[0::2]).reshape(1, -1),
        "pages_odd": np.ascontiguousarray(table[1::2]).reshape(1, -1),
    }
    nc = bacc.Bacc("TRN2", target_bir_lowering=False, num_devices=1)
    ap, maps = {}, {}
    for n, v in arrays.items():
        maps["in_" + n] = np.ascontiguousarray(v)
        ap[n] = nc.dram_tensor("in_" + n, v.shape, mybir.dt.from_np(v.dtype), kind="ExternalInput").ap()
    for n, shape in _OUTS.items():
        ap[n] = nc.dram_tensor("out_" + n, shape, F32, kind="ExternalOutput").ap()
    build_program(nc, ap)
    got = run_bass_kernel_spmd(nc, [maps], core_ids=[0]).results[0]
    o = {n: np.asarray(got["out_" + n]) for n in _OUTS}

    def rows(x):
        return np.ascontiguousarray(x.transpose(2, 1, 0)).reshape(x.shape[2], -1)

    y, k, v, u, ik = rows(o["y"]), rows(o["k"]), rows(o["v"]), rows(o["u"]), np.ascontiguousarray(o["ik"].T)
    last = rows(o["uplast"]).reshape(2 + DB, FT, 2, P).transpose(0, 2, 1, 3).reshape(2 + DB, 2 * D_FF)
    kv = (KV, HD)
    return (
        y[:SEQ][None], y[SEQ:][:, None],
        k[:TP].reshape((1, 1, TP) + kv), v[:TP].reshape((1, 1, TP) + kv), ik[:TP][None, None],
        u[TP - POOL_BUF:TP][None, None], last[:2][None, None],
        k[TP:].reshape((1, DB, 1) + kv), v[TP:].reshape((1, DB, 1) + kv), ik[TP:].reshape(1, DB, 1, -1),
        np.concatenate([o["old_pool"], u[TP:][:, None]], 1)[None],
        np.concatenate([o["old_conv"], last[2:][:, None]], 1)[None],
    )
```

```python
from contextlib import ExitStack

import concourse.bass as bass
from concourse import mybir
import numpy as np

F32 = mybir.dt.float32
F32R = mybir.dt.float32r
I32 = mybir.dt.int32
U32 = mybir.dt.uint32
ALU = mybir.AluOpType
ACT = mybir.ActivationFunctionType
AX = mybir.AxisListType

P = 128
D_MODEL, SEQ, DB, PAST, PAGE = 2048, 256, 8, 1024, 128
N_META, HEADS, KV, HD = 16, 8, 2, 128
IDX_HEADS, IDX_DIM = 16, 64
POOL_WIDTH, POOL_BUF, D_FF = 1024, 15, 5632
TOPK_MAX, EPS = 256, 1e-6
WINDOWS = (2, 4, 8, 16)

TP = N_META + SEQ
T = TP + DB
CONV = 3
L = N_META - (CONV - 1)
TU = T - L
TG = T - N_META
KM = D_MODEL // P
PAGES = PAST // PAGE
CTX = PAST + 1
TOPK_P = min(TOPK_MAX, TP // 4)
TOPK_S = min(TOPK_MAX, CTX // 4)
FT = D_FF // P
IKW = IDX_DIM + IDX_HEADS
PAIRS = DB // 2

QT = [(L, 128, 128), (128, 128, 256), (256, 16, 272)]
READ = [128 - L, 128, 16]
SENT = -(-TOPK_P // 8) * 8 - TOPK_P
S_AT = [0, 128 + SENT, 384 + 2 * SENT]
S_W = 656 + 3 * SENT
A_AT = [0, 128, 384]
NEG = -3e38
BIG = 3e38
MASKED = -1e30

RING = 4
CW = 8 * P

C_IK = 0
C_IQ = C_IK + 2
C_PROJ = C_IQ + 16
C_WOP = C_PROJ + 40
C_WOA = C_WOP + 16
C_UP = C_WOA + 16
C_DOWN = C_UP + 4 * FT
DOWN_CUT = [0, 8, 16, 23, 30, 37, 44]
T_IK, T_IQ = 0, 1
T_PROJ = T_IQ + 8
T_WOP = T_PROJ + 20
T_WOA = T_WOP + 16
T_UP = T_WOA + 16
T_DOWN = T_UP + 2 * FT
Y_PARTS = [(0, 2), (2, 5), (5, 8), (8, 11)]
Y_POOL = [(11, 13), (13, 16)]
X_PARTS = [0, 2, 4, 8, 12, 16]
KEEP = 24
EARLY = 8
U0, K0, V0, Q0 = 0, 8, 10, 12

G1, G2, G3, G4, PSC = 0, 16, 32, 48, 64
CWT, CBT = 72, 72 + 3 * 2 * FT
PAR_W = CBT + 2 * FT
IDN, ONE, HREP, BLK, EXP8, M64, INV, DIX, EPC, M16 = 0, 128, 256, 384, 392, 456, 464, 528, 529, 530
CON_W = 546


def shape_constants():
    c = np.zeros((P, CON_W), np.float32)
    c[:, IDN:IDN + P] = np.eye(P)
    c[:, ONE:ONE + P] = 1.0
    for b in range(DB):
        for h in range(IDX_HEADS):
            c[h, HREP + IDX_HEADS * b + h] = 1.0
            c[IDX_HEADS * b + h, BLK + b] = 1.0
        c[b, EXP8 + HEADS * b:EXP8 + HEADS * (b + 1)] = 1.0
        c[HEADS * b:HEADS * (b + 1), M64 + b] = 1.0
    for g, w in enumerate(WINDOWS):
        c[:, INV + 16 * g:INV + 16 * (g + 1)] = 1.0 / np.minimum(np.arange(16) + 1, w)
    c[:, DIX] = np.arange(P) % IDX_DIM
    c[:, EPC] = EPS
    c[np.arange(P), M16 + np.arange(P) % 16] = 1.0
    s = np.full((P, S_W), NEG, np.float32)
    for (q0, nq, nk), at in zip(QT, S_AT):
        for q in range(P):
            s[q, at:at + min(q0 + q + 1, nk)] = 0.0
        s[:, at + nk:at + nk + SENT] = BIG
    return c, s


class Steps:

    def __init__(self, eng, sem):
        self.eng, self.sem, self.n, self.turn = eng, sem, 0, 0

    def then(self, ins):
        ins.then_inc(self.sem, 1)
        self.n += 1

    def wait(self):
        self.eng.wait_ge(self.sem, self.turn + self.n)

    def link(self, ins):
        self.then(ins)
        self.wait()


def build_program(nc, a):
    ctx = ExitStack()

    def sem(name):
        return ctx.enter_context(nc.semaphore(name))

    def sb(name, shape, dt=F32, at=None):
        return (at or ctx).enter_context(nc.sbuf_tensor(name, shape, dt))

    raw = sb("raw", [P, RING, CW])
    hi = sb("hi", [P, RING, CW], F32R)
    lo = sb("lo", [P, RING, CW], F32R)
    par = sb("par", [P, PAR_W])
    con = sb("con", [P, CON_W])
    rms = sb("rms", [P, T])
    var = sb("var", [P, T])
    newton = sb("newton", [P, T])
    sumsq = sb("sumsq", [P, T])
    sq = sb("sq", [P, 2, T])
    idle = sb("idle", [P, P])
    squares = [sq[:, 0, :], sq[:, 1, :], var[:, :], newton[:, :]]

    at_h = ExitStack()
    h_hi = sb("h_hi", [P, KM, T], F32R, at_h)
    h_lo = sb("h_lo", [P, KM, T], F32R, at_h)

    at_1 = ExitStack()
    at_k = ExitStack()
    k_hi = sb("k_hi", [P, PAGES, KV * PAGE], F32R, at_k)
    k_lo = sb("k_lo", [P, PAGES, KV * PAGE], F32R, at_k)
    at_k.close()
    cache_ring = sb("cache_ring", [P, 4096], at=at_1)
    mixed = sb("mixed", [P, KM * T], at=at_1)
    short = sb("short", [P, 3984], at=at_1)
    part = sb("part", [P, KM, T], at=at_1)
    qT = sb("qT", [P, HEADS, T], at=at_1)
    qbd = sb("qbd", [P, 2 * DB * 64], at=at_1)
    qnew = sb("qnew", [P, 2 * 64], at=at_1)
    kT = sb("kT", [P, KV, T], at=at_1)
    vT = sb("vT", [P, KV, T], at=at_1)
    vrow = sb("vrow", [P, 3, KV * HD], at=at_1)
    vnew = sb("vnew", [DB, KV * HD], at=at_1)
    ikT = sb("ikT", [IDX_DIM, T], at=at_1)
    iknew = sb("iknew", [P, PAIRS], at=at_1)
    iwT = sb("iwT", [IDX_HEADS, T], at=at_1)
    iwq = sb("iwq", [P, 2 * IDX_HEADS], at=at_1)
    iwq3 = sb("iwq3", [P, 2, 16], at=at_1)
    iwblk = sb("iwblk", [P, DB], at=at_1)
    top8 = sb("top8", [P, 3, 8], at=at_1)
    top8s = sb("top8s", [DB, 8], at=at_1)
    mx = sb("mx", [P, 3], at=at_1)
    nmx = sb("nmx", [P, 3], at=at_1)
    den = sb("den", [P, 3], at=at_1)
    rden = sb("rden", [P, 3], at=at_1)
    mxs = sb("mxs", [64, 5], at=at_1)
    dens = sb("dens", [64, 5], at=at_1)
    pnm = sb("pnm", [64, DB], at=at_1)
    pnew = sb("pnew", [DB, 64], at=at_1)
    ptab = sb("ptab", [P, PAIRS * PAGES], I32, at_1)
    ptrow = sb("ptrow", [1, DB * PAGES], I32, at_1)
    kix = sb("kix", [P, PAIRS * PAGES], U32, at_1)
    at_q = ExitStack()
    q_hi = sb("q_hi", [P, 2 * DB * 64], F32R, at_q)
    q_lo = sb("q_lo", [P, 2 * DB * 64], F32R, at_q)
    at_q.close()
    outs_rows = sb("outs", [HEADS, DB * KV * HD], at=at_1)
    S = sb("S", [P, S_W], at=at_1)
    W = sb("W", [P, S_W], at=at_1)
    Ss = sb("Ss", [DB, CTX], at=at_1)
    Ws = sb("Ws", [DB, CTX], at=at_1)

    kidx = cache_ring[:, :].rearrange("p (b s) -> p b s", b=PAIRS)
    vring = cache_ring[:, :].rearrange("p (r g e) -> p r g e", r=2, g=PAGES)
    U = mixed[:, 0:8 * (POOL_BUF + T)].rearrange("p (j t) -> p j t", j=8)
    UW = POOL_BUF + TP
    at = 8 * (POOL_BUF + T)
    win = [mixed[:, at + n * 2 * UW:at + (n + 1) * 2 * UW].rearrange("p (j t) -> p j t", j=2) for n in range(3)]
    kring = mixed[:, 0:4096].rearrange("p (r g e) -> p r g e", r=2, g=PAGES)

    def v_slot(b):
        return kring[:, b % 2] if b % 4 < 2 else vring[:, b % 2]

    x1 = mixed[:, :].rearrange("p (k t) -> p k t", k=KM)
    iq = short[0:IDX_DIM, 0:4 * T].rearrange("p (h t) -> p h t", h=4)
    relu = short[:, 1120:1120 + 768].rearrange("p (r s) -> p r s", r=2)
    iq3 = short[0:IDX_DIM, 1888:1888 + 256]
    iwx = short[0:IDX_HEADS, 2144:2144 + 2 * P].rearrange("p (n r) -> p n r", n=2)
    iqbd = short[:, 2432:2432 + PAIRS * P]
    relus = short[:, 2944:2944 + CTX]
    relu3 = [short[:, 2144:2144 + TP], relus[:, 0:TP]]
    diff = short[:, 0:8 * T].rearrange("p (j t) -> p j t", j=8)
    prob = short[:, 0:1312].rearrange("p (r s) -> p r s", r=2)
    probT = short[:, 1312:1312 + 864].rearrange("p (r s) -> p r s", r=2)
    probs = short[0:64, 2176:2176 + CTX]
    outs = outs_rows[0:HEADS, :].rearrange("h (b e) -> h b e", b=DB)
    probsT = short[:, 3204:3204 + 512].rearrange("p (g c) -> p g c", g=PAGES)
    x0 = part
    partf = part[:, :, :].rearrange("p k t -> p (k t)")
    poolw = partf[:, 0:2048].rearrange("p (g k d) -> p g k d", g=4, k=2)
    poolst = partf[:, 2048:2048 + 960].rearrange("p (j b s) -> p j b s", j=8, b=DB)
    end_1 = at_1

    end_1.close()
    at_2 = ExitStack()
    g_hi = sb("g_hi", [P, FT, TG], F32R, at_2)
    g_lo = sb("g_lo", [P, FT, TG], F32R, at_2)
    cst = sb("cst", [P, 2, 2 * FT, DB], at=at_2)
    up = sb("up", [P, 2, 2, TU], at=at_2)
    act = sb("act", [P, 2, TG], at=at_2)
    uplast = sb("uplast", [P, 2 * FT, 2 + DB], at=at_2)
    at_2.close()
    at_h.close()
    at_3 = ExitStack()
    x2 = sb("x2", [P, KM, TG], at=at_3)
    o2 = sb("o2", [P, KM, TG], at=at_3)
    at_3.close()

    bank = [ctx.enter_context(nc.psum_tensor(f"bank{i}", [P, 512], F32)) for i in range(8)]
    misc = bank[7]

    def q_idx_bank(t):
        return bank[3 if t == 2 else (T_IQ + t) % 2]

    def out_by_head(g):
        return bank[4][:, 0:P].rearrange("p (b g h) -> p g h b", b=DB, g=KV)[:, g, 4 * g:4 * g + 4, :]

    kscr = nc.dram_tensor("kscr", [DB * PAGES, P, KV * PAGE], F32).ap()
    vscr = nc.dram_tensor("vscr", [DB * PAGES, P, KV * HD], F32).ap()
    xscr = nc.dram_tensor("xscr", [P, KM, TG], F32).ap()

    raw_loaded = [sem(f"raw_loaded{i}") for i in range(RING)]
    hi_ready = sem("hi_ready")
    lo_pool = sem("lo_pool")
    lo_dve = sem("lo_dve")
    chunk_used = sem("chunk_used")
    tile_freed = sem("tile_freed")
    x_loaded = [sem(f"x_loaded{i}") for i in range(len(X_PARTS) - 1)]
    par_loaded = sem("par_loaded")
    conv_par_loaded = sem("conv_par_loaded")
    con_loaded = sem("con_loaded")
    s_loaded = sem("s_loaded")
    pt_loaded = sem("pt_loaded")
    poolw_loaded = sem("poolw_loaded")
    kix_ready = sem("kix_ready")
    kidx_loaded = sem("kidx_loaded")
    scr_loaded = sem("scr_loaded")
    k_loaded = [sem(f"k_loaded{i}") for i in range(2)]
    v_loaded = [sem(f"v_loaded{i}") for i in range(4)]
    x1_loaded = sem("x1_loaded")
    x2_loaded = sem("x2_loaded")
    x_spilled = sem("x_spilled")
    cst_loaded = sem("cst_loaded")
    stored = sem("stored")
    u_stored = sem("u_stored")
    copied = sem("copied")
    zeroed = sem("zeroed")
    dve_step = sem("dve_step")
    act_step = sem("act_step")
    h_hi_ready = sem("h_hi_ready")
    h_lo_ready = sem("h_lo_ready")
    sq_ready = sem("sq_ready")
    sq_used = sem("sq_used")
    sum_ready = sem("sum_ready")
    var_ready = sem("var_ready")
    root_ready = sem("root_ready")
    iw_ready = sem("iw_ready")
    iq_ready = sem("iq_ready")
    iq_used = sem("iq_used")
    relu_ready = sem("relu_ready")
    score3_done = sem("score3_done")
    relu3_ready = sem("relu3_ready")
    sum3_done = sem("sum3_done")
    sum3_used = sem("sum3_used")
    relu_used = sem("relu_used")
    sidx_done = sem("sidx_done")
    srelu_done = sem("srelu_done")
    ssum_done = sem("ssum_done")
    vt_done = sem("vt_done")
    vrow_ready = sem("vrow_ready")
    diff_ready = sem("diff_ready")
    pmix_done = sem("pmix_done")
    pmix_hi = sem("pmix_hi")
    pmix_lo = sem("pmix_lo")
    score_done = sem("score_done")
    soft_in = sem("soft_in")
    exp_done = sem("exp_done")
    prob_ready = sem("prob_ready")
    probT_done = sem("probT_done")
    probT_ready = sem("probT_ready")
    pv_done = sem("pv_done")
    o_hi = sem("o_hi")
    o_lo = sem("o_lo")
    k_hi_ready = sem("k_hi_ready")
    k_lo_dve = sem("k_lo_dve")
    k_lo_pool = sem("k_lo_pool")
    q_hi_ready = sem("q_hi_ready")
    q_lo_ready = sem("q_lo_ready")
    kq_used = sem("kq_used")
    vq_used = sem("vq_used")
    smask_ready = sem("smask_ready")
    sscore_done = sem("sscore_done")
    ssoft_in = sem("ssoft_in")
    sexp_done = sem("sexp_done")
    sprob_ready = sem("sprob_ready")
    sprobT_done = sem("sprobT_done")
    sprobT_act = sem("sprobT_act")
    sprobT_dve = sem("sprobT_dve")
    spv_done = sem("spv_done")
    so_hi = sem("so_hi")
    so_lo = sem("so_lo")
    o_ready = sem("o_ready")
    o_scaled = sem("o_scaled")
    xt_ready = sem("xt_ready")
    y_pool = sem("y_pool")
    o_scaled_pool = sem("o_scaled_pool")
    o_scaled_dve = sem("o_scaled_dve")
    rms_ready = sem("rms_ready")
    ln_ready = sem("ln_ready")
    idle_ready = sem("idle_ready")
    outs_act = sem("outs_act")
    outs_dve = sem("outs_dve")
    outT_done = sem("outT_done")
    up_ready = sem("up_ready")
    act_ready = sem("act_ready")
    conv_ready = sem("conv_ready")
    silu_ready = sem("silu_ready")
    gate_ready = sem("gate_ready")
    g_hi_ready = sem("g_hi_ready")
    g_lo_ready = sem("g_lo_ready")
    y_ready = sem("y_ready")

    def lo_wait(eng, r, cj):
        if isinstance(r, int) and 4 * r + cj < EARLY:
            eng.wait_ge(lo_pool, 4 * r + cj + 1)
        elif cj < C_PROJ:
            eng.wait_ge(lo_dve, 4 * r + cj - EARLY + 1)
        elif cj < C_UP:
            eng.wait_ge(lo_pool, 4 * r + EARLY + cj - C_PROJ + 1)
        elif (cj - C_UP) % 2 == 0:
            eng.wait_ge(lo_pool, 2 * r + EARLY + C_UP - C_PROJ + (cj - C_UP) // 2 + 1)
        else:
            eng.wait_ge(lo_dve, 2 * r + C_PROJ - EARLY + (cj - C_UP + 1) // 2)

    def hi_chunk(act_eng, r, cj, width=CW):
        s = cj % RING
        act_eng.wait_ge(raw_loaded[s], 16 * (r + cj // RING + 1))
        if cj >= RING:
            act_eng.wait_ge(chunk_used, 4 * r + cj - RING + 1)
        nc.scalar.activation(hi[:, s, 0:width], raw[:, s, 0:width], ACT.Copy).then_inc(hi_ready, 1)

    def lo_chunk(eng, ops, done, r, cj, width=CW):
        s = cj % RING
        eng.wait_ge(hi_ready, 4 * r + cj + 1)
        if cj >= RING:
            eng.wait_ge(chunk_used, 4 * r + cj - RING + 1)
        ops.tensor_tensor(lo[:, s, 0:width], raw[:, s, 0:width], hi[:, s, 0:width].bitcast(F32),
                          ALU.subtract).then_inc(done, 1)

    def key_pages(c):
        return slice(PAGES // 2 * c, PAGES // 2 * (c + 1))

    def key_low(eng, ops, done, b, c):
        eng.wait_ge(k_hi_ready, 2 * b + c + 1)
        if b:
            eng.wait_ge(kq_used, 2 * b + c - 1)
        pages = key_pages(c)
        ops.tensor_tensor(k_lo[:, pages, :], kring[:, b % 2, pages, :], k_hi[:, pages, :].bitcast(F32),
                          ALU.subtract).then_inc(done, 1)

    def scale_rms(ops, k0, k1):
        by_token = rms[:, N_META:].unsqueeze(1).broadcast_to([P, k1 - k0, TG])
        return ops.tensor_tensor(o2[:, k0:k1, :], o2[:, k0:k1, :], by_token, ALU.mult)

    def down_width(cj):
        i = (cj - C_DOWN) % 6
        return (DOWN_CUT[i + 1] - DOWN_CUT[i]) * P

    with nc.Block() as block:

        def load_x(eng, n):
            part_n = slice(X_PARTS[n], X_PARTS[n + 1])
            eng.dma_start(x0[:, part_n, :], a["x"][:, part_n, :]).then_inc(x_loaded[n], 16)

        @block.sync
        def _(sp):
            def load(r, cj, src, width=CW):
                if not isinstance(r, int):
                    lo_wait(sp, r - 1, cj) if cj >= C_UP else lo_wait(sp, r, cj - RING)
                elif 4 * r + cj >= RING:
                    lo_wait(sp, 0, 4 * r + cj - RING)
                sp.dma_start(raw[:, cj % RING, 0:width], src).then_inc(raw_loaded[cj % RING], 16)

            for n in range(5):
                if n % 2 == 0:
                    load_x(sp, n)
                else:
                    j = n // 2
                    load(0, C_IK + j, a["w_ik"][:, j * 8 * IKW:(j + 1) * 8 * IKW], 8 * IKW)

            def pages(n):
                page = sp.value_load(ptrow[0:1, bass.ds(n, 1)], min_val=0, max_val=a["cache_k"].shape[0] - 1)
                sp.dma_start(kscr[n], a["cache_k"][page]).then_inc(scr_loaded, 16)
                sp.dma_start(vscr[n], a["cache_v"][page]).then_inc(scr_loaded, 16)

            w_in = a["w_in"]

            def load_in(r, cj, t):
                for j in range(2):
                    load(r, cj + j, w_in[t, :, j * CW:(j + 1) * CW])

            load_in(0, C_IQ, 0)
            sp.wait_ge(pt_loaded, 48)

            def paced_in(i, t, n0, n, r):
                load_in(r, C_IQ + 2 * t, 2 * i + t)
                for k in range(n):
                    pages(2 * n * i + n0 + k)

            paced_in(0, 1, 0, 3, 0)
            paced_in(0, 2, 3, 3, 0)
            paced_in(0, 3, 6, 3, 0)
            paced_in(0, 4, 9, 3, 0)
            with sp.Fori(2, 4) as i:
                paced_in(i, 1, 0, 3, i)
                paced_in(i, 2, 3, 3, i)
            paced_in(0, 9, 24, 4, 0)
            paced_in(0, 10, 28, 4, 0)
            with sp.Fori(0, 8) as i:
                paced_in(i, 11, 32, 2, i)
                paced_in(i, 12, 34, 2, i)
            load_in(0, C_IQ + 54, 27)
            kv_src = [[kscr, vscr][n].rearrange("(b g) p e -> b p g e", b=DB) for n in range(2)]

            def load_k(b):
                if b >= 2:
                    sp.wait_ge(k_lo_dve, b - 1)
                    sp.wait_ge(k_lo_pool, b - 1)
                sp.dma_start(kring[:, b % 2], kv_src[0][b]).then_inc(k_loaded[b % 2], 16)

            def load_v(b):
                if b < 2:
                    sp.wait_ge(k_lo_dve, DB - 1 + b)
                    sp.wait_ge(k_lo_pool, DB - 1 + b)
                if b in (2, 3):
                    sp.wait_ge(kq_used, 2 * DB)
                if b >= 4:
                    sp.wait_ge(spv_done if b % 2 else vq_used, b // 2 - 1)
                sp.dma_start(v_slot(b), kv_src[1][b]).then_inc(v_loaded[b % 4], 16)

            def load_wo(n):
                j, half = n % KM, 1 - n // KM
                load(0, C_WOP + n, a["w_o"][j, :, half * CW:(half + 1) * CW])

            for n in range(4):
                load_wo(n)
            sp.wait_ge(scr_loaded, 2 * DB * PAGES * 16)
            sp.wait_ge(sidx_done, 1)
            sp.wait_ge(diff_ready, 4)
            sp.wait_ge(u_stored, 16)
            load_k(0)
            load_k(1)
            for n in range(4, 8):
                load_wo(n)
            load_k(2)
            for h in range(HEADS):
                load_wo(8 + h)
                if h + 3 < DB:
                    load_k(h + 3)
                elif h < 7:
                    load_v(h - 5)
            load_v(2)
            load_v(3)
            for n in range(16, 19):
                load_wo(n)
            load_v(4)
            load_v(5)
            load_wo(19)
            load_v(6)
            load_v(7)
            load_wo(20)
            load_wo(21)
            sp.wait_ge(spv_done, 4)
            for n in range(4):
                sp.dma_start(x1[:, 4 * n:4 * n + 4, :], a["x"][:, 4 * n:4 * n + 4, :]).then_inc(x1_loaded, 16)
                if n % 2:
                    load_wo(22 + n // 2)
            sp.wait_ge(so_lo, 2)
            for n in range(2):
                sp.dma_start(cst[:, n], a["state_conv"][:, n]).then_inc(cst_loaded, 16)
                load_wo(24 + n)
            for n in range(26, 32):
                load_wo(n)

            def load_up(r):
                for j in range(4):
                    load(r, C_UP + j, a["w_up"][2 * r + j // 2, :, (j % 2) * CW:(j % 2 + 1) * CW])

            load_up(0)
            with sp.Fori(1, FT) as i:
                load_up(i)

            def load_down(i, t):
                for j in range(6):
                    c0, c1 = DOWN_CUT[j], DOWN_CUT[j + 1]
                    load(3 * i, C_DOWN + 6 * t + j, a["w_down"][2 * i + t, :, c0 * P:c1 * P], (c1 - c0) * P)

            with sp.Fori(0, KM // 2) as i:
                load_down(i, 0)
                load_down(i, 1)
            for done, n, (k0, k1) in ((y_ready, 1, Y_PARTS[0]), (y_ready, 2, Y_PARTS[1]), (y_pool, 1, Y_POOL[0]),
                                      (y_ready, 3, Y_PARTS[2]), (y_ready, 4, Y_PARTS[3]), (y_pool, 2, Y_POOL[1])):
                sp.wait_ge(done, n)
                sp.dma_start(a["y"][:, k0:k1, :], o2[:, k0:k1, :]).then_inc(stored, 16)
            sp.wait_ge(stored, 16 * (4 + len(Y_PARTS) + len(Y_POOL)))
            sp.wait_ge(u_stored, 16)
            sp.wait_ge(copied, 32)

        @block.gpsimd
        def _(pool):
            nc.gpsimd.memset(idle[:, :], 0.0).then_inc(idle_ready, 1)
            nc.gpsimd.memset(iqbd, 0.0).then_inc(zeroed, 1)
            nc.gpsimd.memset(qbd[:, :], 0.0).then_inc(zeroed, 1)
            nc.gpsimd.memset(qnew[:, :], 0.0).then_inc(zeroed, 1)
            nc.gpsimd.memset(U[:, :, 0:POOL_BUF], 0.0).then_inc(zeroed, 1)
            pool.dma_start(ptab[0:64, :], a["pages_even"].broadcast_to([64, PAIRS * PAGES])).then_inc(pt_loaded, 16)
            pool.dma_start(ptab[64:128, :], a["pages_odd"].broadcast_to([64, PAIRS * PAGES])).then_inc(pt_loaded, 16)
            pool.dma_start(ptrow[:, :], a["pages"]).then_inc(pt_loaded, 16)
            pool.dma_start(con[:, :], a["con"]).then_inc(con_loaded, 16)
            for c in range(EARLY):
                lo_chunk(pool, nc.gpsimd, lo_pool, 0, c, 8 * IKW if c < C_IQ else CW)
            pool.wait_ge(kix_ready, 1)
            kidx_rows = a["cache_kidx"]
            for b in range(PAIRS):
                for g in range(PAGES):
                    n = b * PAGES + g
                    nc.gpsimd.indirect_dma_start(
                        kidx[:, b, g * PAGE:(g + 1) * PAGE], None, kidx_rows,
                        bass.IndirectOffsetOnAxis(ap=kix[:, n:n + 1], axis=0)).then_inc(kidx_loaded, 16)
            with pool.Fori(0, (C_WOP - C_PROJ) // 4) as i:
                for j in range(4):
                    lo_chunk(pool, nc.gpsimd, lo_pool, i, C_PROJ + j)
            for n in range(12):
                if n == 3:
                    key_low(pool, nc.gpsimd, k_lo_pool, 0, 1)
                if 4 <= n < 11:
                    key_low(pool, nc.gpsimd, k_lo_pool, n - 3, 1)
                lo_chunk(pool, nc.gpsimd, lo_pool, 0, C_WOP + n)
            with pool.Fori(0, (C_UP - C_WOP - 12) // 4) as i:
                for j in range(4):
                    lo_chunk(pool, nc.gpsimd, lo_pool, i, C_WOP + 12 + j)
            for j in (0, 2):
                lo_chunk(pool, nc.gpsimd, lo_pool, 0, C_UP + j)
            pool.wait_ge(x1_loaded, 64)
            for k in range(KM):
                pool.wait_ge(o_scaled, k + 1)
                nc.gpsimd.tensor_tensor(x1[:, k, L:], x1[:, k, L:], part[:, k, L:], ALU.add).then_inc(xt_ready, 1)
            with pool.Fori(1, FT) as i:
                for j in (0, 2):
                    lo_chunk(pool, nc.gpsimd, lo_pool, i, C_UP + j)
            with pool.Fori(0, KM // 2) as i:
                for j in range(0, 12, 2):
                    lo_chunk(pool, nc.gpsimd, lo_pool, 3 * i, C_DOWN + j, down_width(C_DOWN + j))
            pool.wait_ge(rms_ready, 4)
            for n, (k0, k1) in enumerate(Y_POOL):
                scale_rms(nc.gpsimd, k0, k1).then_inc(o_scaled_pool, 1)
            for n, (k0, k1) in enumerate(Y_POOL):
                pool.wait_ge(o_scaled_pool, n + 1)
                nc.gpsimd.tensor_tensor(o2[:, k0:k1, :], x2[:, k0:k1, :], o2[:, k0:k1, :], ALU.add).then_inc(y_pool, 1)

        @block.scalar
        def _(act_eng):
            ae = act_eng
            st = Steps(ae, act_step)
            ae.dma_start(par[:, 0:CWT], a["par"][:, 0:CWT]).then_inc(par_loaded, 16)
            load_x(ae, 1)
            load_x(ae, 3)
            ae.wait_ge(idle_ready, 1)
            st.link(nc.scalar.activation(newton[:, 0:1], idle[:, 0:1], ACT.Copy))
            ae.wait_ge(par_loaded, 16)
            for k in range(KM):
                if k in X_PARTS:
                    ae.wait_ge(x_loaded[X_PARTS.index(k)], 16)
                if k in (0, 7):
                    hi_chunk(ae, 0, C_IK + k // 7, 8 * IKW)
                if k == 13:
                    hi_chunk(ae, 0, C_IQ)
                nc.scalar.activation(h_hi[:, k, :], x0[:, k, :], ACT.Copy,
                                     scale=par[:, G1 + k:G1 + k + 1]).then_inc(h_hi_ready, 1)
            hi_chunk(ae, 0, C_IQ + 1)
            for k in range(KM):
                if k == 8:
                    hi_chunk(ae, 0, C_IQ + 2)
                    hi_chunk(ae, 0, C_IQ + 3)
                if k >= 4:
                    ae.wait_ge(sq_used, k - 3)
                nc.scalar.activation(squares[k % 4], x0[:, k, :], ACT.Square).then_inc(sq_ready, 1)

            ae.dma_start(par[:, CWT:], a["par"][:, CWT:]).then_inc(conv_par_loaded, 16)
            ae.dma_start(S[:, :], a["causal"]).then_inc(s_loaded, 16)
            ae.dma_start(a["old_pool"], a["state_pool_rows"]).then_inc(copied, 16)
            ae.dma_start(a["old_conv"], a["state_conv_rows"]).then_inc(copied, 16)

            def root(n, first=0):
                ae.wait_ge(sum_ready, n)
                nc.scalar.activation(rms[:, first:], misc[:, first:T], ACT.Ln, scale=1.0 / D_MODEL,
                                     bias=con[:, EPC:EPC + 1]).then_inc(ln_ready, 1)
                ae.wait_ge(ln_ready, n)
                nc.scalar.activation(rms[:, first:], rms[:, first:], ACT.Exp, scale=-0.5).then_inc(root_ready, 1)

            hi_chunk(ae, 0, C_IQ + 4)
            hi_chunk(ae, 0, C_IQ + 5)
            root(1)
            ae.wait_ge(h_lo_ready, KM)
            ae.dma_start(partf[:, 0:2048], a["pool_w"]).then_inc(poolw_loaded, 16)
            ae.dma_start(partf[:, 2048:2048 + 960], a["state_pool"]).then_inc(poolw_loaded, 16)

            IDX_SCALE = float(IDX_DIM) ** -0.5 * float(IDX_HEADS) ** -0.5

            def relu_head(h, p):
                ae.wait_ge(iq_used, h + 1)
                if not isinstance(h, int) or h >= 2:
                    ae.wait_ge(relu_used, h - 1)
                nc.scalar.activation(relu[:, p, :], bank[2 + 2 * p][:, 0:384], ACT.Relu,
                                     scale=IDX_SCALE).then_inc(relu_ready, 1)

            for t in (1, 2):
                if t > 1:
                    hi_chunk(ae, 0, C_IQ + 2 * t + 2)
                    hi_chunk(ae, 0, C_IQ + 2 * t + 3)
                for p in range(2):
                    relu_head(2 * (t - 1) + p, p)
            with ae.Fori(1, 3) as i:
                for t in (1, 2):
                    hi_chunk(ae, i, C_IQ + 2 * t + 2)
                    hi_chunk(ae, i, C_IQ + 2 * t + 3)
                    for p in range(2):
                        relu_head(4 * i + 2 * (t - 1) + p, p)
            for h in range(12, 16):
                relu_head(h, h % 2)
                hi_chunk(ae, 0, C_PROJ + h - 12)
                if h == 13:
                    ae.wait_ge(score3_done, 1)
                    for n in range(2):
                        nc.scalar.activation(relu3[n], bank[3 + 2 * n][:, 0:TP], ACT.Relu,
                                             scale=IDX_SCALE).then_inc(relu3_ready, 1)
            hi_chunk(ae, 0, C_PROJ + 4)
            hi_chunk(ae, 0, C_PROJ + 5)
            ae.wait_ge(sidx_done, 1)
            nc.scalar.activation(relus[:, 0:512], bank[4][:, :], ACT.Relu, scale=IDX_SCALE).then_inc(srelu_done, 1)
            nc.scalar.activation(relus[:, 512:1024], bank[5][:, :], ACT.Relu, scale=IDX_SCALE).then_inc(srelu_done, 1)
            nc.scalar.activation(relus[:, 1024:1025], bank[6][:, 0:1], ACT.Relu,
                                 scale=IDX_SCALE).then_inc(srelu_done, 1)
            with ae.Fori(0, 7) as i:
                for j in range(4):
                    hi_chunk(ae, i, C_PROJ + 6 + j)
            ae.wait_ge(diff_ready, 4)
            ae.dma_start(a["u"], U[:, :, POOL_BUF:POOL_BUF + T]).then_inc(u_stored, 16)
            ae.dma_start(a["k"], kT[:, :, :]).then_inc(stored, 16)
            ae.dma_start(a["v"], vT[:, :, :]).then_inc(stored, 16)
            ae.dma_start(a["ik"], ikT[:, :]).then_inc(stored, 16)
            for j in range(34, 40):
                hi_chunk(ae, 0, C_PROJ + j)
            ae.wait_ge(vt_done, 1)
            nc.scalar.activation(vrow[:, 0, :], bank[6][:, 0:256], ACT.Copy).then_inc(vrow_ready, 1)
            nc.scalar.activation(vrow[:, 1, :], bank[6][:, 256:512], ACT.Copy).then_inc(vrow_ready, 1)
            nc.scalar.activation(vrow[0:16, 2, :], misc[0:16, 0:256], ACT.Copy).then_inc(vrow_ready, 1)
            nc.scalar.activation(vnew[:, :], misc[0:DB, 256:512], ACT.Copy).then_inc(vrow_ready, 1)
            for j in range(4):
                hi_chunk(ae, 0, C_WOP + j)

            def key_high(b, c):
                ae.wait_ge(k_loaded[b % 2], 16 * (b // 2 + 1))
                if b:
                    ae.wait_ge(kq_used, 2 * b + c - 1)
                pages = key_pages(c)
                nc.scalar.activation(k_hi[:, pages, :], kring[:, b % 2, pages, :], ACT.Copy).then_inc(k_hi_ready, 1)

            for j in range(8):
                ae.wait_ge(pmix_done, j + 1)
                nc.scalar.activation(h_hi[:, HEADS + j, L:], bank[2 + j % 4][:, L:T], ACT.Copy,
                                     scale=par[:, PSC + j:PSC + j + 1]).then_inc(pmix_hi, 1)
                if j == 1:
                    ae.wait_ge(tile_freed, 21)
                    nc.scalar.activation(q_hi[:, :], qbd[:, :], ACT.Copy).then_inc(q_hi_ready, 1)
                if j in (3, 5):
                    key_high(0, j // 4)
            SCALE = float(HD) ** -0.5

            def exp_head(h):
                ae.wait_ge(soft_in, h + 1)
                for n, (q0, nq, nk) in enumerate(QT):
                    sl = prob[0:nq, h % 2, A_AT[n]:A_AT[n] + nk]
                    nc.scalar.activation(sl, sl, ACT.Exp, scale=SCALE, bias=nmx[0:nq, n:n + 1],
                                         accum_out=den[0:nq, n:n + 1]).then_inc(exp_done, 1)

            def head_out(h):
                ae.wait_ge(pv_done, h + 1)
                nc.scalar.activation(h_hi[:, h, L:TP], bank[5][:, L:TP], ACT.Copy).then_inc(o_hi, 1)

            exp_head(0)
            for h in range(HEADS):
                p = h % 2
                if h + 1 < DB:
                    for c in range(2):
                        key_high(h + 1, c)
                if h:
                    hi_chunk(ae, 0, C_WOP + 4 + h)
                ae.wait_ge(probT_done, h + 1)
                nc.scalar.activation(probT[:, p, L:416], bank[4][:, L:416], ACT.Copy).then_inc(probT_ready, 1)
                nc.scalar.activation(probT[0:16, p, 416:432], bank[4][0:16, 416:432], ACT.Copy).then_inc(probT_ready, 1)
                if h + 1 < HEADS:
                    exp_head(h + 1)
                    if h == 0:
                        hi_chunk(ae, 0, C_WOP + 4)
                    head_out(h)
            ae.wait_ge(ssoft_in, 1)
            for n, (c0, c1) in enumerate(((0, 512), (512, 1024), (1024, 1025))):
                src = bank[6 + n][0:64, :] if n < 2 else mxs[:, 2:3]
                nc.scalar.activation(probs[:, c0:c1], src, ACT.Exp, scale=SCALE,
                                     bias=mxs[:, 4:5], accum_out=dens[:, n:n + 1]).then_inc(sexp_done, 1)
            head_out(HEADS - 1)
            hi_chunk(ae, 0, C_WOP + 12)
            hi_chunk(ae, 0, C_WOP + 13)
            ae.wait_ge(sprobT_done, 1)
            nc.scalar.activation(probsT[:, :, :], bank[4][:, :].rearrange("p (g c) -> p g c", g=PAGES),
                                 ACT.Copy).then_inc(sprobT_act, 1)
            hi_chunk(ae, 0, C_WOP + 14)
            for n in range(2):
                ae.wait_ge(spv_done, 2 * n + 1)
                nc.scalar.activation(outs[:, 4 * n:4 * n + 2, :], bank[2 + n][0:HEADS, :].rearrange(
                    "h (b e) -> h b e", b=2), ACT.Copy).then_inc(outs_act, 1)
                hi_chunk(ae, 0, C_WOP + 15 + 2 * n)
                hi_chunk(ae, 0, C_WOP + 16 + 2 * n)
            ae.wait_ge(outT_done, 1)
            for g in range(KV):
                nc.scalar.activation(h_hi[:, 4 * g:4 * g + 4, TP:T], out_by_head(g), ACT.Copy).then_inc(so_hi, 1)
            hi_chunk(ae, 0, C_WOA + 3)
            for j in range(KM):
                if j < KM - 1:
                    hi_chunk(ae, 0, C_WOA + 4 + j)
                ae.wait_ge(o_ready, j + 1)
                if j >= 2:
                    ae.wait_ge(sq_used, KM + j - 1)
                nc.scalar.activation(sq[:, j % 2, L:], part[:, j, L:], ACT.Square).then_inc(sq_ready, 1)
            root(2, L)
            hi_chunk(ae, 0, C_UP + 3)
            for k in range(KM):
                ae.wait_ge(xt_ready, k + 1)
                nc.scalar.activation(h_hi[:, k, L:], x1[:, k, L:], ACT.Copy,
                                     scale=par[:, G3 + k:G3 + k + 1]).then_inc(h_hi_ready, 1)
                ae.wait_ge(sq_used, 2 * KM + k - 1)
                nc.scalar.activation(sq[:, k % 2, L:], x1[:, k, L:], ACT.Square).then_inc(sq_ready, 1)
            ae.dma_start(xscr, x1[:, :, N_META:]).then_inc(x_spilled, 16)
            root(3, L)
            ae.wait_ge(conv_par_loaded, 16)

            def conv_bias(r, p, v):
                f = 2 * r + v
                ae.wait_ge(up_ready, f + 1)
                nc.scalar.activation(act[:, v, :], up[:, p, v, CONV - 1:], ACT.Identity,
                                     scale=par[:, bass.ds(CWT + 4 * FT + f, 1)],
                                     bias=par[:, bass.ds(CBT + f, 1)]).then_inc(act_ready, 1)

            def gated_hi(r):
                ae.wait_ge(gate_ready, r + 1)
                nc.scalar.activation(g_hi[:, bass.ds(r, 1), :], act[:, 0:1, :], ACT.Copy).then_inc(g_hi_ready, 1)

            def ffn_pair(r, p, last=False, first=False):
                widths = [down_width(C_DOWN + j) if last else CW for j in range(4)]
                hi_chunk(ae, r, C_UP + 4, widths[0])
                if not first:
                    gated_hi(r - 1)
                hi_chunk(ae, r, C_UP + 5, widths[1])
                if not first:
                    ae.wait_ge(g_lo_ready, r)
                conv_bias(r, p, 0)
                hi_chunk(ae, r, C_UP + 6, widths[2])
                ae.wait_ge(conv_ready, r + 1)
                nc.scalar.activation(act[:, 0, :], act[:, 0, :], ACT.Silu).then_inc(silu_ready, 1)
                hi_chunk(ae, r, C_UP + 7, widths[3])
                conv_bias(r, p, 1)

            ffn_pair(0, 0, first=True)
            ae.wait_ge(x_spilled, 16)
            with ae.Fori(0, FT // 2 - 1) as i:
                ffn_pair(2 * i + 1, 1)
                ffn_pair(2 * i + 2, 0)
            ffn_pair(FT - 1, 1, last=True)
            gated_hi(FT - 1)
            ae.wait_ge(chunk_used, C_DOWN)
            ae.dma_start(x2[:, :, :], xscr).then_inc(x2_loaded, 16)
            ae.dma_start(a["uplast"], uplast[:, :, :]).then_inc(stored, 16)

            def down_tile(r, i, t, tail=False):
                for j in range(6):
                    cj = C_DOWN + RING + 6 * t + j
                    if not (tail and t == 1 and j >= 2):
                        hi_chunk(ae, r, cj, down_width(cj))
                n = 2 * i + t
                ae.wait_ge(o_ready, KM + n + 1)
                ae.wait_ge(sq_used, 3 * KM + n - 2)
                nc.scalar.activation(sq[:, t, N_META:], bank[(T_DOWN + t) % 2][:, N_META:T], ACT.Square).then_inc(sq_ready, 1)

            with ae.Fori(0, KM // 2 - 1) as i:
                down_tile(3 * i, i, 0)
                down_tile(3 * i, i, 1)
            down_tile(3 * (KM // 2 - 1), KM // 2 - 1, 0, tail=True)
            down_tile(3 * (KM // 2 - 1), KM // 2 - 1, 1, tail=True)
            root(4, N_META)

        @block.vector
        def _(dve):
            st = Steps(dve, dve_step)
            mul = ALU.mult
            st.link(nc.vector.memset(sumsq[:, :], 0.0))
            st.link(nc.vector.memset(den[:, :], 1.0))

            dve.wait_ge(par_loaded, 16)
            for k in range(KM):
                dve.wait_ge(h_hi_ready, k + 1)
                nc.vector.scalar_tensor_tensor(h_lo[:, k, :], x0[:, k, :], par[:, G1 + k:G1 + k + 1],
                                               h_hi[:, k, :].bitcast(F32), ALU.mult,
                                               ALU.subtract).then_inc(h_lo_ready, 1)

            new_even, new_odd = slice(TP, T, 2), slice(TP + 1, T, 2)

            dve.wait_ge(pt_loaded, 48)
            dve.wait_ge(con_loaded, 16)
            nc.vector.tensor_scalar(kix[:, :], ptab[:, :], float(IDX_DIM), con[:, DIX:DIX + 1],
                                    ALU.mult, ALU.add).then_inc(kix_ready, 1)
            dve.wait_ge(zeroed, 4)

            def index_queries(t):
                ps = q_idx_bank(t)
                dve.wait_ge(chunk_used, C_IQ + 2 * t + 2)
                if t >= 2:
                    dve.wait_ge(iq_used, 2 * t - 2)
                for e in range(2):
                    h = 2 * t + e
                    src = slice(64 * e, 64 * e + 64)
                    for half, new in ((0, new_even), (1, new_odd)):
                        off = h + 16 * half
                        st.then(nc.vector.tensor_tensor(
                            iqbd[64 * half:64 * half + 64, off:off + 160 * (PAIRS - 1) + 1:160],
                            ps[src, new], rms[src, new], mul))
                    st.then(nc.vector.tensor_tensor(iq3[:, 16 * h:16 * h + 16], ps[src, TP - 16:TP],
                                                    rms[src, TP - 16:TP], mul))
                for e in range(2):
                    src = slice(64 * e, 64 * e + 64)
                    ins = nc.vector.tensor_tensor(iq[:, 2 * (t % 2) + e, L:], ps[src, L:T], rms[src, L:], mul)
                    if e:
                        ins.then_inc(iq_ready, 1)
                    else:
                        st.then(ins)
                dve.wait_ge(iq_ready, t + 1)

            def inv_rms(n, first=0):
                r, v, y = rms[:, first:], var[:, first:], newton[:, first:]
                dve.wait_ge(ln_ready, n)
                nc.vector.tensor_scalar(v, misc[:, first:T], 1.0 / D_MODEL, EPS,
                                        ALU.mult, ALU.add).then_inc(var_ready, 1)
                dve.wait_ge(var_ready, n)
                dve.wait_ge(root_ready, n)
                st.link(nc.vector.scalar_tensor_tensor(y, r, -0.5, r, mul, mul))
                st.link(nc.vector.tensor_tensor(y, y, v, mul))
                nc.vector.scalar_tensor_tensor(r, y, 1.5, r, ALU.add, mul).then_inc(rms_ready, 1)
                dve.wait_ge(rms_ready, n)

            def add_squares(n, squares, first=0):
                dve.wait_ge(sq_ready, n)
                nc.vector.tensor_tensor(sumsq[:, first:], sumsq[:, first:], squares[:, first:],
                                        ALU.add).then_inc(sq_used, 1)
                dve.wait_ge(sq_used, n)

            for k in range(KM):
                add_squares(k + 1, squares[k % 4])
            inv_rms(1)

            dve.wait_ge(chunk_used, C_IK + 2)
            ps = bank[6]
            st.then(nc.vector.tensor_tensor(ikT[:, :], ps[0:64, 0:T], rms[0:64, :], mul))
            st.then(nc.vector.tensor_tensor(iknew[0:64, :], ps[0:64, new_even], rms[0:64, new_even], mul))
            st.then(nc.vector.tensor_tensor(iknew[64:128, :], ps[0:64, new_odd], rms[0:64, new_odd], mul))
            st.link(nc.vector.tensor_tensor(iwT[:, :], ps[64:80, 0:T], rms[64:80, :], mul))
            for n in range(2):
                ins = nc.vector.tensor_tensor(
                    iwx[:, n, :].rearrange("p (h q) -> p h q", h=8),
                    con[0:16, IDN + 8 * n:IDN + 8 * n + 8].unsqueeze(2).broadcast_to([16, 8, 16]),
                    iwT[:, TP - 16:TP].unsqueeze(1).broadcast_to([16, 8, 16]), mul)
                st.then(ins) if n == 0 else ins.then_inc(tile_freed, 1)
            index_queries(0)
            dve.wait_ge(iw_ready, 1)
            st.then(nc.vector.tensor_copy(iwq[:, 0:32], misc[:, 0:32]))
            for n in range(2):
                st.then(nc.vector.tensor_tensor(iwq3[:, n, :], misc[:, 80 + 16 * n:96 + 16 * n],
                                                con[:, M16:M16 + 16], mul))
            st.link(nc.vector.tensor_tensor(iwblk[:, :], misc[:, 64:72], con[:, BLK:BLK + DB], mul))
            dve.wait_ge(s_loaded, 16)

            def index_sum(h):
                dve.wait_ge(relu_ready, h + 1)
                for n, (q0, nq, nk) in enumerate(QT[:2]):
                    acc = S[0:nq, S_AT[n]:S_AT[n] + nk]
                    ins = nc.vector.scalar_tensor_tensor(
                        acc, relu[0:nq, h % 2, A_AT[n]:A_AT[n] + nk], iwq[0:nq, 16 * n + h:16 * n + h + 1], acc,
                        ALU.mult, ALU.add)
                    if n == 0:
                        st.then(ins)
                    else:
                        ins.then_inc(relu_used, 1)
                dve.wait_ge(relu_used, h + 1)

            for t in range(8):
                if t in range(2, 7):
                    lo_chunk(dve, nc.vector, lo_dve, 0, C_IQ + 2 * t + 2)
                    lo_chunk(dve, nc.vector, lo_dve, 0, C_IQ + 2 * t + 3)
                if t >= 2:
                    index_sum(2 * t - 4)
                    index_sum(2 * t - 3)
                if t:
                    index_queries(t)
            for h in range(12, 16):
                index_sum(h)
            dve.wait_ge(sum3_done, 1)
            acc = S[0:16, S_AT[2]:S_AT[2] + TP]
            nc.vector.tensor_tensor(acc, acc, misc[0:16, 128:128 + TP], ALU.add).then_inc(sum3_used, 1)
            dve.wait_ge(sum3_used, 1)

            def prompt_round(n):
                for q, (q0, nq, nk) in enumerate(QT):
                    src = (S if n == 0 else W)[0:nq, S_AT[q]:S_AT[q] + nk + SENT]
                    st.then(nc.vector.max(top8[0:nq, q, :], src))
                st.wait()
                for q, (q0, nq, nk) in enumerate(QT):
                    src = (S if n == 0 else W)[0:nq, S_AT[q]:S_AT[q] + nk + SENT]
                    st.then(nc.vector.match_replace(W[0:nq, S_AT[q]:S_AT[q] + nk + SENT], top8[0:nq, q, :], src, NEG))
                st.wait()

            def sample_round(n):
                src = (Ss if n == 0 else Ws)[:, :]
                st.link(nc.vector.max(top8s[:, :], src))
                st.link(nc.vector.match_replace(Ws[:, :], top8s[:, :], src, NEG))

            def tile_ready(t):
                dve.wait_ge(chunk_used, C_PROJ + 2 * t + 2)
                return bank[(T_PROJ + t) % 2]

            ROUNDS_P = (TOPK_P + SENT) // 8
            ROUNDS_S = TOPK_S // 8
            rounds_s = iter(range(ROUNDS_S))
            rounds_p = iter(range(ROUNDS_P))
            for t in range(U0, U0 + 8):
                for _ in range(3 if t < 2 else 1 if t < 5 else 0):
                    prompt_round(next(rounds_p))
                ps = tile_ready(t)
                nc.vector.tensor_tensor(U[:, t, POOL_BUF:POOL_BUF + T], ps[:, 0:T], rms[:, :],
                                        mul).then_inc(tile_freed, 1)
                if t == 1:
                    dve.wait_ge(ssum_done, 1)
                    st.then(nc.vector.tensor_copy(Ss[:, 0:512], bank[2][0:DB, :]))
                    st.then(nc.vector.tensor_copy(Ss[:, 512:1024], bank[3][0:DB, :]))
                    st.link(nc.vector.tensor_copy(Ss[:, 1024:1025], misc[0:DB, 0:1]))
                if t >= 2:
                    sample_round(next(rounds_s))
                if t >= 5:
                    sample_round(next(rounds_s))
            assert next(rounds_p, None) is None
            dve.wait_ge(tile_freed, 9)
            for q, (q0, nq, nk) in enumerate(QT):
                sl = slice(S_AT[q], S_AT[q] + nk)
                st.link(nc.vector.tensor_tensor(W[0:nq, sl], S[0:nq, sl], W[0:nq, sl], ALU.not_equal))
                st.link(nc.vector.tensor_scalar(W[0:nq, sl], W[0:nq, sl], -1.0, -MASKED, ALU.add, ALU.mult))

            def pool_group(g):
                w = WINDOWS[g]
                u = U[:, 2 * g:2 * g + 2, :]
                src, step, n = u, 1, 0
                while step < w:
                    dst = win[n % 2]
                    st.link(nc.vector.tensor_tensor(dst[:, :, 2 * step - 1:UW], src[:, :, 2 * step - 1:UW],
                                                    src[:, :, step - 1:UW - step], ALU.add))
                    src, step, n = dst, 2 * step, n + 1
                d = diff[:, 2 * g:2 * g + 2, :]
                inv = con[:, INV + 16 * g:INV + 16 * g + 16].unsqueeze(1).broadcast_to([P, 2, 16])
                st.link(nc.vector.tensor_tensor(win[2][:, :, 0:16], src[:, :, POOL_BUF:POOL_BUF + 16], inv, mul))
                st.then(nc.vector.tensor_tensor(d[:, :, 0:16], win[2][:, :, 0:16], u[:, :, POOL_BUF:POOL_BUF + 16],
                                                ALU.subtract))
                st.link(nc.vector.scalar_tensor_tensor(d[:, :, 16:TP], src[:, :, POOL_BUF + 16:UW], 1.0 / w,
                                                       u[:, :, POOL_BUF + 16:UW], ALU.mult, ALU.subtract))
                s = win[2][:, :, 16:16 + DB]
                un = u[:, :, POOL_BUF + TP:POOL_BUF + T]
                st.link(nc.vector.tensor_reduce(s, poolst[:, 2 * g:2 * g + 2, :, POOL_BUF - (w - 1):POOL_BUF],
                                                AX.X, ALU.add))
                st.link(nc.vector.tensor_tensor(s, s, un, ALU.add))
                nc.vector.scalar_tensor_tensor(d[:, :, TP:T], s, 1.0 / w, un, ALU.mult,
                                               ALU.subtract).then_inc(diff_ready, 1)
                dve.wait_ge(diff_ready, g + 1)

            dve.wait_ge(poolw_loaded, 32)
            for t in range(K0, K0 + 4):
                ps = tile_ready(t)
                dst = kT[:, t - K0, :] if t < V0 else vT[:, t - V0, :]
                ins = nc.vector.tensor_tensor(dst, ps[:, 0:T], rms[:, :], mul)
                ins.then_inc(tile_freed, 1)
                pool_group(t - K0)
                if t < V0:
                    sample_round(next(rounds_s))
            for t in range(Q0, Q0 + HEADS):
                h = t - Q0
                sample_round(next(rounds_s))
                if h:
                    sample_round(next(rounds_s))
                ps = tile_ready(t)
                off = (h // 4) * 64 + h
                st.then(nc.vector.tensor_tensor(qbd[:, off:off + 136 * (DB - 1) + 1:136], ps[:, TP:T],
                                                rms[:, TP:T], mul))
                st.then(nc.vector.tensor_tensor(qnew[:, off:off + 8 * (DB - 1) + 1:8], ps[:, TP:T],
                                                rms[:, TP:T], mul))
                nc.vector.tensor_tensor(qT[:, h, L:TP], ps[:, L:TP], rms[:, L:TP], mul).then_inc(tile_freed, 1)

            for j in range(8):
                dve.wait_ge(pmix_hi, j + 1)
                nc.vector.scalar_tensor_tensor(h_lo[:, HEADS + j, L:], bank[2 + j % 4][:, L:T],
                                               par[:, PSC + j:PSC + j + 1], h_hi[:, HEADS + j, L:].bitcast(F32),
                                               ALU.mult, ALU.subtract).then_inc(pmix_lo, 1)
                if j == 3:
                    dve.wait_ge(q_hi_ready, 1)
                    nc.vector.tensor_tensor(q_lo[:, :], qbd[:, :], q_hi[:, :].bitcast(F32),
                                            ALU.subtract).then_inc(q_lo_ready, 1)
                if j == 6:
                    key_low(dve, nc.vector, k_lo_dve, 0, 0)
            dve.wait_ge(pmix_lo, 8)

            SCALE = float(HD) ** -0.5

            def w_o_pool(j):
                dve.wait_ge(chunk_used, C_WOP + j + 1)
                nc.vector.tensor_copy(part[:, j, L:], bank[(T_WOP + j) % 2][:, L:T]).then_inc(tile_freed, 1)

            def masked_scores(h):
                dve.wait_ge(score_done, h + 1)
                if h >= 2:
                    dve.wait_ge(probT_done, h - 1)
                for n, (q0, nq, nk) in enumerate(QT):
                    src = bank[2][0:nq, A_AT[n]:A_AT[n] + nk] if n < 2 else bank[3][0:nq, 0:nk]
                    st.then(nc.vector.tensor_tensor_reduce(
                        prob[0:nq, h % 2, A_AT[n]:A_AT[n] + nk], src, W[0:nq, S_AT[n]:S_AT[n] + nk], 1.0, -BIG,
                        ALU.add, ALU.max, mx[0:nq, n:n + 1]))
                st.wait()
                st.then(nc.vector.tensor_scalar(nmx[:, 0:2], mx[:, 0:2], -SCALE, None, ALU.mult))
                nc.vector.tensor_scalar(nmx[0:16, 2:3], mx[0:16, 2:3], -SCALE, None, ALU.mult).then_inc(soft_in, 1)

            def head_low(h):
                dve.wait_ge(o_hi, h + 1)
                nc.vector.tensor_tensor(h_lo[:, h, L:TP], bank[5][:, L:TP], h_hi[:, h, L:TP].bitcast(F32),
                                        ALU.subtract).then_inc(o_lo, 1)

            masked_scores(0)
            for h in range(HEADS):
                p = h % 2
                dve.wait_ge(exp_done, 3 * h + 3)
                st.link(nc.vector.reciprocal(rden[:, :], den[:, :]))
                for n, (q0, nq, nk) in enumerate(QT):
                    sl = prob[0:nq, p, A_AT[n]:A_AT[n] + nk]
                    nc.vector.tensor_scalar(sl, sl, rden[0:nq, n:n + 1], None, ALU.mult).then_inc(prob_ready, 1)
                dve.wait_ge(prob_ready, 3 * h + 3)
                if h + 1 < DB:
                    key_low(dve, nc.vector, k_lo_dve, h + 1, 0)
                w_o_pool(h)
                if h + 1 < HEADS:
                    masked_scores(h + 1)
                    left = next(rounds_s, None)
                    if left is not None:
                        sample_round(left)
                    if h == HEADS - 2:
                        st.link(nc.vector.tensor_tensor(Ws[:, :], Ss[:, :], Ws[:, :], ALU.not_equal))
                        nc.vector.tensor_scalar(Ws[:, :], Ws[:, :], -1.0, -MASKED, ALU.add,
                                                ALU.mult).then_inc(smask_ready, 1)
                    head_low(h)
            assert next(rounds_s, None) is None
            dve.wait_ge(sscore_done, 1)
            st.then(nc.vector.reduce_max(mxs[:, 0:1], bank[6][0:64, :], AX.X))
            st.then(nc.vector.reduce_max(mxs[:, 1:2], bank[7][0:64, :], AX.X))
            st.link(nc.vector.tensor_tensor(pnm[:, :], bank[2][0:64, 0:DB], con[0:64, M64:M64 + DB], mul))
            st.link(nc.vector.reduce_sum(mxs[:, 2:3], pnm[:, :], AX.X))
            st.link(nc.vector.tensor_tensor(mxs[:, 2:3], mxs[:, 2:3], bank[2][0:64, DB:DB + 1], ALU.add))
            st.link(nc.vector.reduce_max(mxs[:, 3:4], mxs[:, 0:3], AX.X))
            nc.vector.tensor_scalar(mxs[:, 4:5], mxs[:, 3:4], -SCALE, None, ALU.mult).then_inc(ssoft_in, 1)
            w_o_pool(8)
            dve.wait_ge(sexp_done, 3)
            st.link(nc.vector.reduce_sum(dens[:, 3:4], dens[:, 0:3], AX.X))
            st.link(nc.vector.reciprocal(dens[:, 4:5], dens[:, 3:4]))
            st.link(nc.vector.tensor_scalar(probs, probs, dens[:, 4:5], None, ALU.mult))
            nc.vector.tensor_scalar(pnm[:, :], con[0:64, M64:M64 + DB], probs[:, 1024:1025], None,
                                    ALU.mult).then_inc(sprob_ready, 1)
            head_low(HEADS - 1)
            w_o_pool(9)
            dve.wait_ge(sprobT_done, 1)
            nc.vector.tensor_copy(pnew[:, :], bank[5][0:DB, 0:64]).then_inc(sprobT_dve, 1)
            w_o_pool(10)
            for n in range(2):
                w_o_pool(11 + 2 * n)
                dve.wait_ge(spv_done, 2 * n + 2)
                nc.vector.tensor_copy(outs[:, 4 * n + 2:4 * n + 4, :], bank[6 + n][0:HEADS, :].rearrange(
                    "h (b e) -> h b e", b=2)).then_inc(outs_dve, 1)
                w_o_pool(12 + 2 * n)
            dve.wait_ge(so_hi, KV)
            for g in range(KV):
                nc.vector.tensor_tensor(h_lo[:, 4 * g:4 * g + 4, TP:T], out_by_head(g),
                                        h_hi[:, 4 * g:4 * g + 4, TP:T].bitcast(F32),
                                        ALU.subtract).then_inc(so_lo, 1)
            w_o_pool(15)
            st.link(nc.vector.memset(sumsq[:, :], 0.0))

            def conv_state():
                dve.wait_ge(cst_loaded, 32)
                dve.wait_ge(conv_par_loaded, 16)
                for i in range(2):
                    wi = par[:, CWT + i * 2 * FT:CWT + (i + 1) * 2 * FT].unsqueeze(2).broadcast_to([P, 2 * FT, DB])
                    st.link(nc.vector.tensor_tensor(cst[:, i], cst[:, i], wi, mul))
                st.link(nc.vector.tensor_tensor(cst[:, 0], cst[:, 0], cst[:, 1], ALU.add))

            for j in range(KM):
                dve.wait_ge(chunk_used, C_WOA + j + 1)
                nc.vector.tensor_tensor(part[:, j, L:], bank[(T_WOA + j) % 2][:, L:T], part[:, j, L:],
                                        ALU.add).then_inc(o_ready, 1)
                if j:
                    add_squares(KM + j, squares[(j - 1) % 2], L)
                if j == 10:
                    conv_state()
                if j == 13:
                    lo_chunk(dve, nc.vector, lo_dve, 0, C_UP + 1)
            dve.wait_ge(o_ready, KM)
            add_squares(2 * KM, squares[(KM - 1) % 2], L)
            inv_rms(2, L)

            def residual(k):
                o = part[:, k, L:]
                nc.vector.scalar_tensor_tensor(o, o, par[:, G2 + k:G2 + k + 1], rms[:, L:],
                                               ALU.mult, ALU.mult).then_inc(o_scaled, 1)

            def stage_hi_lo(k):
                dve.wait_ge(h_hi_ready, KM + k + 1)
                nc.vector.scalar_tensor_tensor(h_lo[:, k, L:], x1[:, k, L:], par[:, G3 + k:G3 + k + 1],
                                               h_hi[:, k, L:].bitcast(F32), ALU.mult,
                                               ALU.subtract).then_inc(h_lo_ready, 1)

            for k in range(KM):
                residual(k)
                if k >= 2:
                    stage_hi_lo(k - 2)
            stage_hi_lo(KM - 2)
            stage_hi_lo(KM - 1)
            lo_chunk(dve, nc.vector, lo_dve, 0, C_UP + 3)
            inv_rms(3, L)

            def scaled_up(r, p, v):
                f = 2 * r + v
                dve.wait_ge(chunk_used, C_UP + 4 * r + 2 * v + 2)
                nc.vector.tensor_tensor(up[:, p, v, :], bank[(T_UP + v) % 2][:, L:T], rms[:, L:],
                                        mul).then_inc(up_ready, 1)
                dve.wait_ge(up_ready, f + 1)
                st.then(nc.vector.tensor_copy(uplast[:, bass.ds(f, 1), :],
                                              up[:, p, v:v + 1, SEQ:TU]))

            def conv_taps(r, v, p):
                f = 2 * r + v
                dve.wait_ge(act_ready, f + 1)
                for i in range(2):
                    st.link(nc.vector.scalar_tensor_tensor(
                        act[:, v, 0:SEQ], up[:, p, v, i:i + SEQ], par[:, bass.ds(CWT + 2 * FT * i + f, 1)],
                        act[:, v, 0:SEQ], ALU.mult, ALU.add))
                ins = nc.vector.tensor_tensor(act[:, v:v + 1, SEQ:], act[:, v:v + 1, SEQ:],
                                              cst[:, 0, bass.ds(f, 1), :], ALU.add)
                if v:
                    st.link(ins)
                else:
                    ins.then_inc(conv_ready, 1)

            def gated(r, p):
                conv_taps(r, 1, p)
                dve.wait_ge(silu_ready, r + 1)
                nc.vector.tensor_tensor(act[:, 0, :], act[:, 0, :], act[:, 1, :], mul).then_inc(gate_ready, 1)
                dve.wait_ge(g_hi_ready, r + 1)
                nc.vector.tensor_tensor(g_lo[:, bass.ds(r, 1), :], act[:, 0:1, :],
                                        g_hi[:, bass.ds(r, 1), :].bitcast(F32),
                                        ALU.subtract).then_inc(g_lo_ready, 1)

            def ffn_pair(r, p, last=False, first=False):
                widths = [down_width(C_DOWN + j) if last else CW for j in range(4)]
                if not first:
                    gated(r - 1, 1 - p)
                scaled_up(r, p, 0)
                conv_taps(r, 0, p)
                lo_chunk(dve, nc.vector, lo_dve, r, C_UP + 5, widths[1])
                scaled_up(r, p, 1)
                lo_chunk(dve, nc.vector, lo_dve, r, C_UP + 7, widths[3])

            STEPS_PER_PAIR = 7
            ffn_pair(0, 0, first=True)
            n0 = st.n
            with dve.Fori(0, FT // 2 - 1) as i:
                st.turn = 2 * STEPS_PER_PAIR * i
                ffn_pair(2 * i + 1, 1)
                ffn_pair(2 * i + 2, 0)
            assert st.n - n0 == 2 * STEPS_PER_PAIR, st.n - n0
            st.turn = 0
            st.n = n0 + (FT - 2) * STEPS_PER_PAIR
            ffn_pair(FT - 1, 1, last=True)
            gated(FT - 1, 1)
            st.link(nc.vector.memset(sumsq[:, :], 0.0))
            dve.wait_ge(x2_loaded, 16)

            def down_out(i, t, r, tail=False):
                for j in (1, 3, 5):
                    cj = C_DOWN + RING + 6 * t + j
                    if not (tail and t == 1 and j >= 3):
                        lo_chunk(dve, nc.vector, lo_dve, r, cj, down_width(cj))
                n = 2 * i + t
                dve.wait_ge(chunk_used, 4 * r + C_DOWN + 6 * (t + 1))
                nc.vector.tensor_scalar(o2[:, bass.ds(n, 1), :], bank[(T_DOWN + t) % 2][:, N_META:T].unsqueeze(1),
                                        par[:, bass.ds(G4 + n, 1)], None, mul).then_inc(o_ready, 1)
                dve.wait_ge(sq_ready, 3 * KM + n + 1)
                nc.vector.tensor_tensor(sumsq[:, N_META:], sumsq[:, N_META:], sq[:, t, N_META:], ALU.add).then_inc(sq_used, 1)
                dve.wait_ge(sq_used, 3 * KM + n)

            with dve.Fori(0, KM // 2 - 1) as i:
                down_out(i, 0, 3 * i)
                down_out(i, 1, 3 * i)
            down_out(KM // 2 - 1, 0, 3 * (KM // 2 - 1), tail=True)
            down_out(KM // 2 - 1, 1, 3 * (KM // 2 - 1), tail=True)
            inv_rms(4, N_META)
            for n in range(len(Y_PARTS) + 1):
                if n < len(Y_PARTS):
                    scale_rms(nc.vector, *Y_PARTS[n]).then_inc(o_scaled_dve, 1)
                if n:
                    k0, k1 = Y_PARTS[n - 1]
                    dve.wait_ge(o_scaled_dve, n)
                    nc.vector.tensor_tensor(o2[:, k0:k1, :], x2[:, k0:k1, :], o2[:, k0:k1, :],
                                            ALU.add).then_inc(y_ready, 1)

        @block.tensor
        def _(pe):
            mm = nc.tensor.matmul

            def stream_tile(r, cjs, kts, x_hi, x_lo, out, first=0, ready=None,
                            part_of=(0, 1)):
                total, done = sum(len(k) for k in kts), 0
                opens, closes = part_of[0] == 0, part_of[0] == part_of[1] - 1
                for cj, ks in zip(cjs, kts):
                    lo_wait(pe, r, cj)
                    s = cj % RING
                    for i, k in enumerate(ks):
                        if ready:
                            pe.wait_ge(ready, done + 1)
                        w_hi = hi[:, s, i * P:(i + 1) * P]
                        w_lo = lo[:, s, i * P:(i + 1) * P]
                        mm(out, w_hi, x_hi[:, k, first:], start=(opens and done == 0), stop=False)
                        mm(out, w_hi, x_lo[:, k, first:], start=False, stop=False)
                        done += 1
                        last = mm(out, w_lo, x_hi[:, k, first:], start=False, stop=(closes and done == total))
                    last.then_inc(chunk_used, 1)

            def keep_clock(n):
                for _ in range(n):
                    mm(bank[5][:, 0:P], idle[:, :], idle[:, :], start=True, stop=True)

            pe.wait_ge(idle_ready, 1)
            HALF = [list(range(8)), list(range(8, 16))]
            out = bank[6][0:IKW, 0:T]
            keep_clock(16)
            for k in range(KM):
                if k % 8 == 0:
                    lo_wait(pe, 0, C_IK + k // 8)
                pe.wait_ge(h_lo_ready, k + 1)
                s, i = k // 8, k % 8
                w_hi, w_lo = (w[:, s, i * IKW:(i + 1) * IKW] for w in (hi, lo))
                mm(out, w_hi, h_hi[:, k, :], start=(k == 0), stop=False)
                mm(out, w_hi, h_lo[:, k, :], start=False, stop=False)
                last = mm(out, w_lo, h_hi[:, k, :], start=False, stop=(k == KM - 1))
                if i == 7:
                    last.then_inc(chunk_used, 1)

            def total(n, used, first):
                pe.wait_ge(sq_used, used)
                mm(misc[:, first:T], con[:, ONE:ONE + P], sumsq[:, first:], start=True, stop=True).then_inc(sum_ready, 1)

            def q_idx_tile(r, t, between=None):
                out = (q_idx_bank(t) if isinstance(r, int) else bank[(T_IQ + t) % 2])[:, L:T]
                for j in range(2):
                    stream_tile(r, [C_IQ + 2 * t + j], [HALF[j]], h_hi, h_lo, out, L, part_of=(j, 2))
                    if between and j == 0:
                        between()

            def index_scores(h, p, e):
                if not isinstance(h, int) or h >= 2:
                    pe.wait_ge(relu_ready, h - 1)
                for n, (q0, nq, nk) in enumerate(QT[:2]):
                    o = bank[2 + 2 * e][0:nq, A_AT[n]:A_AT[n] + nk]
                    last = mm(o, iq[:, 2 * p + e, q0:q0 + nq], ikT[:, 0:nk], start=True, stop=True)
                last.then_inc(iq_used, 1)

            def weights_turned():
                pe.wait_ge(tile_freed, 1)
                tr, ident = nc.tensor.transpose, con[0:16, IDN:IDN + 16]
                for n, (q0, nq, nk) in enumerate(QT[:2]):
                    tr(misc[0:nq, 16 * n:16 * n + 16], iwT[:, q0:q0 + nq], ident)
                for n in range(2):
                    mm(misc[:, 80 + 16 * n:96 + 16 * n], iwx[:, n, :], con[0:16, ONE:ONE + 16], start=True, stop=True)
                mm(misc[:, 64:72], con[0:16, HREP:HREP + P], iwT[:, TP:T], start=True, stop=True).then_inc(iw_ready, 1)

            def q_idx_pair(r, n):
                for t in (1, 2):
                    pe.wait_ge(iq_ready, 2 * n + t - 1)
                    q_idx_tile(r, t)
                    pe.wait_ge(iq_ready, 2 * n + t)
                    for e in range(2):
                        index_scores(4 * n + 2 * (t - 1) + e, (t - 1) % 2, e)

            ident = con[:, IDN:IDN + P]
            q_idx_tile(0, 0)
            pe.wait_ge(con_loaded, 16)
            q_idx_tile(0, 1, between=lambda: total(1, KM, 0))
            q_idx_tile(0, 2)
            weights_turned()
            for t in range(2):
                pe.wait_ge(iq_ready, t + 1)
                for e in range(2):
                    index_scores(2 * t + e, t, e)
            with pe.Fori(1, 3) as i:
                q_idx_pair(i, i)
            pe.wait_ge(iq_ready, 6)
            q_idx_tile(0, 7)
            pe.wait_ge(iq_ready, 7)
            for h in (12, 13):
                index_scores(h, 0, h - 12)
            pe.wait_ge(iq_ready, 8)
            for n in range(2):
                last = mm(bank[3 + 2 * n][:, 0:TP], iq3[:, P * n:P * n + P], ikT[:, 0:TP], start=True, stop=True)
            last.then_inc(score3_done, 1)
            for h in (14, 15):
                index_scores(h, 1, h - 14)
            pe.wait_ge(relu3_ready, 2)
            for n in range(2):
                last = mm(misc[0:16, 128:128 + TP], iwq3[:, n, :], relu3[n], start=(n == 0), stop=(n == 1))
            last.then_inc(sum3_done, 1)

            def proj_tile(r, t, n, first=0):
                if isinstance(n, int) and n < T_PROJ + 2:
                    pe.wait_ge(iq_ready, n - 2)
                else:
                    pe.wait_ge(tile_freed, n - T_PROJ)
                stream_tile(r, [C_PROJ + 2 * t, C_PROJ + 2 * t + 1], HALF, h_hi, h_lo,
                            bank[(T_PROJ + t) % 2][:, first:T], first)

            proj_tile(0, 0, T_PROJ)
            pe.wait_ge(relu_ready, 16)
            pe.wait_ge(kidx_loaded, 16 * PAIRS * PAGES)
            for b in range(PAIRS):
                w = iqbd[:, b * P:(b + 1) * P]
                f, l = b == 0, b == PAIRS - 1
                mm(bank[4][:, :], w, kidx[:, b, 0:512], start=f, stop=l)
                mm(bank[5][:, :], w, kidx[:, b, 512:1024], start=f, stop=l)
                last = mm(bank[6][:, 0:1], w, iknew[:, b:b + 1], start=f, stop=l)
            last.then_inc(sidx_done, 1)

            proj_tile(0, 1, T_PROJ + 1)
            pe.wait_ge(srelu_done, 3)
            pe.wait_ge(sum3_used, 1)
            mm(bank[2][0:DB, :], iwblk[:, :], relus[:, 0:512], start=True, stop=True)
            mm(bank[3][0:DB, :], iwblk[:, :], relus[:, 512:1024], start=True, stop=True)
            mm(misc[0:DB, 0:1], iwblk[:, :], relus[:, 1024:1025], start=True, stop=True).then_inc(ssum_done, 1)
            with pe.Fori(0, 5) as i:
                proj_tile(i, 2, 2 * i + T_PROJ + 2)
                proj_tile(i, 3, 2 * i + T_PROJ + 3)
            with pe.Fori(5, 8) as i:
                proj_tile(i, 2, 2 * i + T_PROJ + 2, L)
                proj_tile(i, 3, 2 * i + T_PROJ + 3, L)
            for g in range(KV):
                nc.tensor.transpose(bank[6][:, g * 128:g * 128 + 128], vT[:, g, 0:128], ident)
                nc.tensor.transpose(bank[6][:, 256 + g * 128:384 + g * 128], vT[:, g, 128:256], ident)
                nc.tensor.transpose(misc[0:16, g * 128:g * 128 + 128], vT[:, g, 256:272], ident)
                last = nc.tensor.transpose(misc[0:DB, 256 + g * 128:384 + g * 128], vT[:, g, TP:T], ident)
            last.then_inc(vt_done, 1)
            proj_tile(0, 18, T_PROJ + 18, L)
            proj_tile(0, 19, T_PROJ + 19, L)
            pe.wait_ge(diff_ready, 4)
            for j in range(8):
                g = j // 2
                if j >= 4:
                    pe.wait_ge(pmix_lo, j - 3)
                for k in range(2):
                    last = mm(bank[2 + j % 4][:, L:T], poolw[:, g, k, (j % 2) * P:(j % 2 + 1) * P],
                              diff[:, 2 * g + k, L:], start=(k == 0), stop=(k == 1))
                last.then_inc(pmix_done, 1)

            def w_o_tile(j, ready=None):
                pe.wait_ge(tile_freed, 20 + j)
                stream_tile(0, [C_WOP + j], [HALF[1]], h_hi, h_lo, bank[(T_WOP + j) % 2][:, L:T], L, ready)

            def attention_scores(h):
                if h:
                    pe.wait_ge(soft_in, h)
                g = h // (HEADS // KV)
                for n, (q0, nq, nk) in enumerate(QT):
                    o = bank[2][0:nq, A_AT[n]:A_AT[n] + nk] if n < 2 else bank[3][0:nq, 0:nk]
                    last = mm(o, qT[:, h, q0:q0 + nq], kT[:, g, 0:nk], start=True, stop=True)
                last.then_inc(score_done, 1)

            def sample_scores(b):
                for c, (low, bk) in enumerate(((k_lo_dve, bank[6]), (k_lo_pool, bank[7]))):
                    pe.wait_ge(low, b + 1)
                    for g in range(KV):
                        cols = slice((2 * b + g) * 64, (2 * b + g) * 64 + 64)
                        keys_hi, keys_lo = (k[:, key_pages(c), g * PAGE:(g + 1) * PAGE] for k in (k_hi, k_lo))
                        mm(bk[0:64, :], q_hi[:, cols], keys_hi, start=(b == 0 and g == 0), stop=False)
                        mm(bk[0:64, :], q_hi[:, cols], keys_lo, start=False, stop=False)
                        last = mm(bk[0:64, :], q_lo[:, cols], keys_hi, start=False, stop=False)
                    last.then_inc(kq_used, 1)

            def sample_mask():
                for g in range(KV):
                    mm(bank[2][0:64, 0:DB], qnew[:, 64 * g:64 * g + 64], kT[:, g, TP:T], start=(g == 0), stop=(g == 1))
                pe.wait_ge(smask_ready, 1)
                e8 = con[0:DB, EXP8:EXP8 + 64]
                mm(bank[6][0:64, :], e8, Ws[:, 0:512], start=False, stop=True)
                mm(bank[7][0:64, :], e8, Ws[:, 512:1024], start=False, stop=True)
                mm(bank[2][0:64, DB:DB + 1], e8, Ws[:, 1024:1025], start=True, stop=True).then_inc(sscore_done, 1)

            def sample_values(b):
                pe.wait_ge(v_loaded[b % 4], 16 * (b // 4 + 1))
                o = bank[(2, 6, 3, 7)[b // 2]][0:HEADS, (b % 2) * 256:(b % 2) * 256 + 256]
                cols = slice(HEADS * b, HEADS * b + HEADS)
                mm(o, pnew[:, cols], vnew[:, :], start=True, stop=False)
                for n in range(PAGES):
                    last = mm(o, probsT[:, n, cols], v_slot(b)[:, n, :], start=False, stop=(n == PAGES - 1))
                last.then_inc(vq_used if b % 2 == 0 else spv_done, 1)

            pe.wait_ge(tile_freed, 21)
            pe.wait_ge(pmix_lo, 6)
            attention_scores(0)
            w_o_tile(0, pmix_lo)
            pe.wait_ge(vrow_ready, 4)
            pe.wait_ge(q_lo_ready, 1)
            sample_scores(0)
            for h in range(HEADS):
                p, g = h % 2, h // (HEADS // KV)
                if h:
                    w_o_tile(h)
                pe.wait_ge(prob_ready, 3 * h + 3)
                if h:
                    pe.wait_ge(probT_ready, 2 * h)
                tr = nc.tensor.transpose
                for (q0, _, nk), nq, at in zip(QT, READ, A_AT):
                    tr(bank[4][:, q0:q0 + nq], prob[0:nq, p, at:at + 128], con[0:nq, IDN:IDN + nq])
                for n in (1, 2):
                    q0, nq, nk = QT[n]
                    tr(bank[4][:, TP + q0 - 128:TP + q0 - 128 + nq],
                       prob[0:nq, p, A_AT[n] + 128:A_AT[n] + 256], con[0:nq, IDN:IDN + nq])
                tr(bank[4][0:16, 416:432], prob[0:16, p, A_AT[2] + 256:A_AT[2] + 272],
                   con[0:16, IDN:IDN + 16]).then_inc(probT_done, 1)
                if h + 1 < HEADS:
                    attention_scores(h + 1)
                    sample_scores(h + 1)
                else:
                    sample_mask()
                    w_o_tile(8)
                pe.wait_ge(probT_ready, 2 * h + 2)
                if h:
                    pe.wait_ge(o_lo, h)
                vg = slice(g * HD, (g + 1) * HD)
                mm(bank[5][:, L:TP], vrow[:, 0, vg], probT[:, p, L:TP], start=True, stop=False)
                mm(bank[5][:, 128:TP], vrow[:, 1, vg], probT[:, p, TP:TP + 144], start=False, stop=False)
                mm(bank[5][:, 256:TP], vrow[0:16, 2, vg], probT[0:16, p, 416:432], start=False,
                   stop=True).then_inc(pv_done, 1)
            w_o_tile(9)
            pe.wait_ge(sprob_ready, 1)
            for g in range(PAGES):
                nc.tensor.transpose(bank[4][:, 64 * g:64 * g + 64], probs[:, g * 128:g * 128 + 128],
                                    con[0:64, IDN:IDN + 64])
            pe.wait_ge(o_lo, HEADS)
            nc.tensor.transpose(bank[5][0:DB, 0:64], pnm[:, :], con[0:64, IDN:IDN + 64]).then_inc(sprobT_done, 1)
            w_o_tile(10)
            pe.wait_ge(sprobT_act, 1)
            pe.wait_ge(sprobT_dve, 1)
            for n in range(4):
                sample_values(2 * n)
                sample_values(2 * n + 1)
                w_o_tile(11 + n)
            for b in range(DB):
                pe.wait_ge(outs_act if b % 4 < 2 else outs_dve, b // 4 + 1)
                for g in range(KV):
                    at = (2 * b + g) * HEADS
                    last = nc.tensor.transpose(bank[4][:, at:at + HEADS], outs[:, b, g * HD:(g + 1) * HD],
                                               con[0:HEADS, IDN:IDN + HEADS])
            last.then_inc(outT_done, 1)
            w_o_tile(15)
            pe.wait_ge(so_lo, 2)
            for j in range(KM):
                if j < 2:
                    pe.wait_ge(tile_freed, 36 + j)
                else:
                    pe.wait_ge(o_ready, j - 1)
                stream_tile(0, [C_WOA + j], [HALF[0]], h_hi, h_lo, bank[(T_WOA + j) % 2][:, L:T], L)

            total(2, 2 * KM, L)
            keep_clock(KEEP)
            pe.wait_ge(o_ready, KM)
            out = bank[T_UP % 2][:, L:T]
            for k in range(KM):
                if k % 8 == 0:
                    lo_wait(pe, 0, C_UP + k // 8)
                pe.wait_ge(h_lo_ready, KM + k + 1)
                s, i = (C_UP + k // 8) % RING, k % 8
                w_hi, w_lo = (w[:, s, i * P:(i + 1) * P] for w in (hi, lo))
                mm(out, w_hi, h_hi[:, k, L:], start=(k == 0), stop=False)
                mm(out, w_hi, h_lo[:, k, L:], start=False, stop=False)
                last = mm(out, w_lo, h_hi[:, k, L:], start=False, stop=(k == KM - 1))
                if i == 7:
                    last.then_inc(chunk_used, 1)
                pe.wait_ge(sq_ready, 2 * KM + k + 1)
                ins = mm(misc[:, L:T], con[:, ONE:ONE + P], sq[:, k % 2, L:], start=(k == 0), stop=(k == KM - 1))
                if k < KM - 1:
                    ins.then_inc(sq_used, 1)
                else:
                    ins.then_inc(sum_ready, 1)

            def up_tile(r, v):
                if not (isinstance(r, int) and r == 0):
                    pe.wait_ge(up_ready, 2 * r + v - 1)
                stream_tile(r, [C_UP + 2 * v, C_UP + 2 * v + 1], HALF, h_hi, h_lo,
                            bank[(T_UP + v) % 2][:, L:T], L)

            up_tile(0, 1)
            with pe.Fori(1, FT) as i:
                up_tile(i, 0)
                up_tile(i, 1)
            KD = [list(range(DOWN_CUT[j], DOWN_CUT[j + 1])) for j in range(6)]

            def down_tile(r, i, t, ready=None):
                if isinstance(i, int) and i == 0:
                    pe.wait_ge(up_ready, 2 * FT - 1 + t)
                else:
                    pe.wait_ge(sq_ready, 3 * KM + 2 * i + t - 1)
                stream_tile(r, [C_DOWN + 6 * t + j for j in range(6)], KD, g_hi, g_lo,
                            bank[(T_DOWN + t) % 2][:, N_META:T], ready=ready)

            down_tile(0, 0, 0, g_lo_ready)
            down_tile(0, 0, 1)
            with pe.Fori(1, KM // 2) as i:
                down_tile(3 * i, i, 0)
                down_tile(3 * i, i, 1)
            total(4, 4 * KM - 1, N_META)
    ctx.close()


_OUTS = {
    "y": (P, KM, TG), "k": (P, KV, T), "v": (P, KV, T), "ik": (IDX_DIM, T), "u": (P, 8, T),
    "uplast": (P, 2 * FT, 2 + DB), "old_pool": (DB, POOL_BUF - 1, POOL_WIDTH), "old_conv": (DB, 1, 2 * D_FF),
}


def kernel(**inputs):
    import concourse.bacc as bacc
    from concourse.bass_utils import run_bass_kernel_spmd

    f = {n: np.asarray(v) for n, v in inputs.items()}

    def tiles(w, cols):
        k, n = w.shape
        return np.ascontiguousarray(
            w.reshape(k // P, P, n // cols, cols).transpose(2, 1, 0, 3)).reshape(n // cols, P, -1)

    def features(x):
        n = x.shape[-1]
        x = np.moveaxis(x, -1, 0)
        return np.ascontiguousarray(np.moveaxis(x.reshape((n // P, P) + x.shape[1:]), 1, 0))

    def pairs(x):
        s = x.shape[:-1]
        return np.moveaxis(x.reshape(s + (2, FT, P)), -3, -2).reshape(s + (2 * D_FF,))

    w_in = f["w_in"][0]
    q_end, k_end = HEADS * HD, HEADS * HD + KV * HD
    v_end = k_end + KV * HD
    iq_end = v_end + IDX_HEADS * IDX_DIM
    iw_end = iq_end + IKW
    w_main = np.concatenate([w_in[:, v_end:iq_end], w_in[:, iw_end:], w_in[:, q_end:v_end], w_in[:, :q_end]], 1)
    x = np.concatenate([f["meta_tokens"], f["x_prompt"][0], f["x_sample"][:, 0]], 0)
    par = [features(f[n][0]) for n in ("g_mix_pre", "g_mix_post", "g_ffn_pre", "g_ffn_post", "pool_scale")]
    par += [features(pairs(f["conv_w"][0])[i]) for i in range(3)] + [features(pairs(f["conv_b"][0]))]
    con, causal = shape_constants()
    n_pool = f["cache_k"].shape[1]
    table = np.ascontiguousarray(f["page_table"]).astype(np.int32, copy=False)
    state_conv = features(pairs(f["state_conv"][0]))
    arrays = {
        "x": features(x), "par": np.concatenate(par, 1), "con": con, "causal": causal,
        "w_ik": tiles(w_in[:, iq_end:iw_end], IKW)[0], "w_in": tiles(w_main, P), "w_o": tiles(f["w_o"][0], P),
        "w_up": tiles(pairs(f["w_up"][0]), P), "w_down": tiles(f["w_down"][0], P),
        "pool_w": np.ascontiguousarray(
            f["pool_w"][0].reshape(4, 2, P, 256).transpose(2, 0, 1, 3)).reshape(P, -1),
        "state_pool": features(f["state_pool"][0]).reshape(P, -1),
        "state_conv": np.ascontiguousarray(state_conv.transpose(0, 3, 1, 2)),
        "state_pool_rows": np.ascontiguousarray(f["state_pool"][0][:, 1:]),
        "state_conv_rows": np.ascontiguousarray(f["state_conv"][0][:, 1:]),
        "cache_k": np.ascontiguousarray(f["cache_k"][0].transpose(0, 3, 2, 1)).reshape(n_pool, P, KV * PAGE),
        "cache_v": f["cache_v"][0].reshape(n_pool, PAGE, KV * HD),
        "cache_kidx": np.ascontiguousarray(f["cache_kidx"][0].transpose(0, 2, 1)).reshape(n_pool * IDX_DIM, PAGE),
        "pages": table.reshape(1, -1),
        "pages_even": np.ascontiguousarray(table[0::2]).reshape(1, -1),
        "pages_odd": np.ascontiguousarray(table[1::2]).reshape(1, -1),
    }
    nc = bacc.Bacc("TRN2", target_bir_lowering=False, num_devices=1)
    ap, maps = {}, {}
    for n, v in arrays.items():
        maps["in_" + n] = np.ascontiguousarray(v)
        ap[n] = nc.dram_tensor("in_" + n, v.shape, mybir.dt.from_np(v.dtype), kind="ExternalInput").ap()
    for n, shape in _OUTS.items():
        ap[n] = nc.dram_tensor("out_" + n, shape, F32, kind="ExternalOutput").ap()
    build_program(nc, ap)
    got = run_bass_kernel_spmd(nc, [maps], core_ids=[0]).results[0]
    o = {n: np.asarray(got["out_" + n]) for n in _OUTS}

    def rows(x):
        return np.ascontiguousarray(x.transpose(2, 1, 0)).reshape(x.shape[2], -1)

    y, k, v, u, ik = rows(o["y"]), rows(o["k"]), rows(o["v"]), rows(o["u"]), np.ascontiguousarray(o["ik"].T)
    last = rows(o["uplast"]).reshape(2 + DB, FT, 2, P).transpose(0, 2, 1, 3).reshape(2 + DB, 2 * D_FF)
    kv = (KV, HD)
    return (
        y[:SEQ][None], y[SEQ:][:, None],
        k[:TP].reshape((1, 1, TP) + kv), v[:TP].reshape((1, 1, TP) + kv), ik[:TP][None, None],
        u[TP - POOL_BUF:TP][None, None], last[:2][None, None],
        k[TP:].reshape((1, DB, 1) + kv), v[TP:].reshape((1, DB, 1) + kv), ik[TP:].reshape(1, DB, 1, -1),
        np.concatenate([o["old_pool"], u[TP:][:, None]], 1)[None],
        np.concatenate([o["old_conv"], last[2:][:, None]], 1)[None],
    )
```
